# Optimizing a Trainium2 kernel written in Bass

```python
import math
import jax, jax.numpy as jnp
from jax import lax
import numpy as np

D_MODEL = 1024
BATCH = 1
SEQ = 128
DEPTH = 2
DEC_BATCH = 1
DEC_SEQ = 512
PAST_LEN = 128

GRID_W = 64
EPS = 1e-6
Q_BLOCK = 128
DA_H = 4
DA_HD = 64
DA_W = DA_H * 2 * DA_HD
ROPE_BASE = 10000.0
SSM_H = 8
SSM_P = 64
SSM_G = 2
SSM_HG = SSM_H // SSM_G
SSM_N = 128
SSM_DI = SSM_H * SSM_P
SSM_CHUNK = 128
CONV_W = 5
CONV_CH = SSM_DI + 2 * SSM_G * SSM_N
NA_H = 8
NA_HD = 64
NA_W = NA_H * NA_HD
WIN_R = 8
WIN_C = 16
QB_C = 16
IN_SIZES = (DA_W, DA_W, DA_W, SSM_DI, CONV_CH, 2 * SSM_H, NA_W, NA_W, NA_W)
IN_W = 3 * DA_W + SSM_DI + CONV_CH + 2 * SSM_H + 3 * NA_W
N_EXPERTS = 32
TOP_K = 4
EXPERT_FF = 128
SHARED_FF = 256
ROUTE_SCALE = 2.5

kernel_name = "hybrid_diffusion_trunk_step"

def rmsnorm(x, g):
    xf = x.astype(jnp.float32)
    y = xf * lax.rsqrt(jnp.mean(xf * xf, axis=-1, keepdims=True) + EPS)
    return (y * g.astype(jnp.float32)).astype(x.dtype)

def split_in(u):
    offs, acc = [], 0
    for s in IN_SIZES[:-1]:
        acc += s
        offs.append(acc)
    return jnp.split(u, offs, axis=-1)

def centred_dwconv(x, w, b):
    k = w.shape[0]
    y = lax.conv_general_dilated(x, w[:, None, :].astype(x.dtype), window_strides=(1,),
                                 padding=[(k // 2, k // 2)], dimension_numbers=("NWC", "WIO", "NWC"),
                                 feature_group_count=x.shape[-1])
    return y + b.astype(x.dtype)

def axial_rope_tables(n_tok):
    pos = jnp.arange(n_tok)
    rows = (pos // GRID_W).astype(jnp.float32)
    cols = (pos % GRID_W).astype(jnp.float32)
    n_freq = DA_HD // 4
    inv = ROPE_BASE ** (-jnp.arange(n_freq, dtype=jnp.float32) / n_freq)
    ar = rows[:, None] * inv
    ac = cols[:, None] * inv
    return (jnp.cos(ar), jnp.sin(ar), jnp.cos(ac), jnp.sin(ac))

def rot_half(x, cos, sin):
    x1, x2 = jnp.split(x, 2, axis=-1)
    return jnp.concatenate([x1 * cos - x2 * sin, x2 * cos + x1 * sin], axis=-1)

def apply_axial_rope(x, tabs):
    cr, sr, cc, sc = [t[:, None, :] for t in tabs]
    xr, xc = jnp.split(x.astype(jnp.float32), 2, axis=-1)
    return jnp.concatenate([rot_half(xr, cr, sr), rot_half(xc, cc, sc)], axis=-1).astype(x.dtype)

def diff_lambda(lam_p, layer):
    lam_init = 0.8 - 0.6 * math.exp(-0.3 * layer)
    lf = lam_p.astype(jnp.float32)
    lam = jnp.exp(jnp.sum(lf[0] * lf[1])) - jnp.exp(jnp.sum(lf[2] * lf[3])) + lam_init
    return lam, lam_init

def diff_attention(q, k, v, lam):
    bn, h, lq, _, d = q.shape
    nb = lq // Q_BLOCK
    qb = q.reshape(bn, h, nb, Q_BLOCK, 2, d).transpose(2, 0, 1, 3, 4, 5)
    scale = d ** -0.5

    def block(qi):
        s = jnp.einsum("bhqtd,bhktd->tbhqk", qi, k).astype(jnp.float32) * scale
        pr = jax.nn.softmax(s, axis=-1)
        a = pr[0] - lam * pr[1]
        return jnp.einsum("bhqk,bhkv->bhqv", a.astype(v.dtype), v)

    o = lax.map(block, qb)
    return o.transpose(1, 2, 0, 3, 4).reshape(bn, h, lq, 2 * d)

def block_attention(q, k, v):
    bn, h, lq, d = q.shape
    nb = lq // Q_BLOCK
    qb = q.reshape(bn, h, nb, Q_BLOCK, d).transpose(2, 0, 1, 3, 4)
    scale = d ** -0.5

    def block(qi):
        s = jnp.einsum("bhqd,bhkd->bhqk", qi, k).astype(jnp.float32) * scale
        return jnp.einsum("bhqk,bhkd->bhqd", jax.nn.softmax(s, axis=-1).astype(v.dtype), v)

    o = lax.map(block, qb)
    return o.transpose(1, 2, 0, 3, 4).reshape(bn, h, lq, d)

def neighbourhood_attention(q, k, v, kc, vc, rpb):
    bn, h, n, d = q.shape
    rows = n // GRID_W
    wr, wc = min(WIN_R, rows), WIN_C
    qr = math.gcd(rows, wr)
    kr = min(wr + qr - 1, rows)
    qc = QB_C
    kcw = min(wc + qc - 1, GRID_W)
    nrb, ncb = rows // qr, GRID_W // qc
    q_rows = np.arange(nrb)[:, None] * qr + np.arange(qr)
    key_rows = np.clip(np.arange(nrb) * qr - wr // 2, 0, rows - kr)[:, None] + np.arange(kr)
    q_cols = np.arange(ncb)[:, None] * qc + np.arange(qc)
    key_cols = np.clip(np.arange(ncb) * qc - wc // 2, 0, GRID_W - kcw)[:, None] + np.arange(kcw)
    s_r = np.clip(q_rows - wr // 2, 0, rows - wr)[:, :, None]
    s_c = np.clip(q_cols - wc // 2, 0, GRID_W - wc)[:, :, None]
    ok_r = (key_rows[:, None, :] >= s_r) & (key_rows[:, None, :] < s_r + wr)
    ok_c = (key_cols[:, None, :] >= s_c) & (key_cols[:, None, :] < s_c + wc)
    off_r = np.clip(key_rows[:, None, :] - q_rows[:, :, None] + WIN_R - 1, 0, 2 * WIN_R - 2)
    off_c = np.clip(key_cols[:, None, :] - q_cols[:, :, None] + WIN_C - 1, 0, 2 * WIN_C - 2)
    ri = lambda a: a[:, None, :, None, :, None]
    ci = lambda a: a[None, :, None, :, None, :]
    nq_blk, nk_blk = qr * qc, kr * kcw
    bias = rpb.astype(jnp.float32)[:, ri(off_r), ci(off_c)]
    bias = jnp.where(jnp.asarray(ri(ok_r) & ci(ok_c)), bias, -jnp.inf)
    bias = bias.reshape(h, nrb, ncb, nq_blk, nk_blk).transpose(1, 0, 2, 3, 4)
    qb = q.reshape(bn, h, nrb, qr, ncb, qc, d).transpose(2, 0, 1, 4, 3, 5, 6).reshape(nrb, bn, h, ncb, nq_blk, d)
    k5 = k.reshape(bn, h, rows, GRID_W, d)
    v5 = v.reshape(bn, h, rows, GRID_W, d)
    kcols = jnp.asarray(key_cols, jnp.int32)
    scale = d ** -0.5

    def gather(t5, kri):
        g = jnp.take(jnp.take(t5, kri, axis=2), kcols, axis=3)
        return g.transpose(0, 1, 3, 2, 4, 5).reshape(bn, h, ncb, nk_blk, d)

    def block(args):
        qi, kri, bi = args
        kg, vg = gather(k5, kri), gather(v5, kri)
        s_w = jnp.einsum("bhjqd,bhjkd->bhjqk", qi, kg).astype(jnp.float32) * scale + bi[None]
        s_x = jnp.einsum("bhjqd,bhcd->bhjqc", qi, kc).astype(jnp.float32) * scale
        pr = jax.nn.softmax(jnp.concatenate([s_w, s_x], axis=-1), axis=-1).astype(v.dtype)
        return (jnp.einsum("bhjqk,bhjkd->bhjqd", pr[..., :nk_blk], vg)
                + jnp.einsum("bhjqc,bhcd->bhjqd", pr[..., nk_blk:], vc))

    o = lax.map(block, (qb, jnp.asarray(key_rows, jnp.int32), bias))
    o = o.reshape(nrb, bn, h, ncb, qr, qc, d).transpose(1, 2, 0, 4, 3, 5, 6)
    return o.reshape(bn, h, n, d)

def segsum(x):
    t = x.shape[-1]
    xx = jnp.broadcast_to(x[..., :, None], x.shape + (t,))
    ss = jnp.cumsum(jnp.where(jnp.tril(jnp.ones((t, t), bool), -1), xx, 0.0), axis=-2)
    return jnp.where(jnp.tril(jnp.ones((t, t), bool)), ss, -jnp.inf)

def ssd_chunked(x, a, b, c, h0):
    bn, l = x.shape[0], x.shape[1]
    t = SSM_CHUNK
    nc = l // t
    x = x.reshape(bn, nc, t, SSM_G, SSM_HG, SSM_P)
    a = a.reshape(bn, nc, t, SSM_G, SSM_HG).transpose(0, 3, 4, 1, 2)
    b = b.astype(jnp.float32).reshape(bn, nc, t, SSM_G, SSM_N)
    c = c.astype(jnp.float32).reshape(bn, nc, t, SSM_G, SSM_N)
    a_cum = jnp.cumsum(a, axis=-1)
    lmat = jnp.exp(segsum(a))
    y_diag = jnp.einsum("bclgn,bcsgn,bghcls,bcsghp->bclghp", c, b, lmat, x)
    decay_states = jnp.exp(a_cum[..., -1:] - a_cum)
    states = jnp.einsum("bclgn,bghcl,bclghp->bcghpn", b, decay_states, x)
    states = jnp.concatenate([h0.astype(jnp.float32)[:, None], states], axis=1)
    chunk_tot = jnp.pad(a_cum[..., -1], ((0, 0), (0, 0), (0, 0), (1, 0)))
    decay_chunk = jnp.exp(segsum(chunk_tot))
    new_states = jnp.einsum("bghzc,bcghpn->bzghpn", decay_chunk, states)
    states, final = new_states[:, :-1], new_states[:, -1]
    y_off = jnp.einsum("bclgn,bcghpn,bghcl->bclghp", c, states, jnp.exp(a_cum))
    return (y_diag + y_off).reshape(bn, l, SSM_G, SSM_HG, SSM_P), final

def ssm_branch(z, xbc, dt, p, h0_f, h0_b):
    bn, l, _ = z.shape
    xbc = jax.nn.silu(centred_dwconv(xbc, p["ssm_conv_w"], p["ssm_conv_b"]))
    xs = xbc[..., :SSM_DI].reshape(bn, l, SSM_G, SSM_HG, SSM_P).astype(jnp.float32)
    bs = xbc[..., SSM_DI:SSM_DI + SSM_G * SSM_N].reshape(bn, l, SSM_G, SSM_N)
    cs = xbc[..., SSM_DI + SSM_G * SSM_N:].reshape(bn, l, SSM_G, SSM_N)
    dt = jax.nn.softplus(dt.astype(jnp.float32).reshape(bn, l, 2, SSM_H) + p["ssm_dt_bias"].astype(jnp.float32))
    a = -jnp.exp(p["ssm_a_log"].astype(jnp.float32))

    def direction(di, xs_, bs_, cs_, dt_, h0):
        dtd = dt_[:, :, di].reshape(bn, l, SSM_G, SSM_HG)
        y, hf = ssd_chunked(xs_ * dtd[..., None], dtd * a[di].reshape(SSM_G, SSM_HG), bs_, cs_,
                            h0.reshape(bn, SSM_G, SSM_HG, SSM_P, SSM_N))
        return y, hf.reshape(bn, SSM_H, SSM_P, SSM_N)

    y_f, h_f = direction(0, xs, bs, cs, dt, h0_f)
    y_b, h_b = direction(1, xs[:, ::-1], bs[:, ::-1], cs[:, ::-1], dt[:, ::-1], h0_b)
    y = y_f + y_b[:, ::-1] + xs * p["ssm_d"].astype(jnp.float32).reshape(SSM_G, SSM_HG, 1)
    y = y.reshape(bn, l, SSM_DI).astype(z.dtype) * jax.nn.silu(z)
    y = rmsnorm(y.reshape(bn, l, SSM_G, SSM_DI // SSM_G), p["ssm_norm"].reshape(SSM_G, -1)).reshape(bn, l, SSM_DI)
    return y, h_f.astype(z.dtype), h_b.astype(z.dtype)

def moe_ffn(h, p):
    bn, l, d = h.shape
    t = h.reshape(-1, d)
    s = jax.nn.sigmoid((t @ p["w_router"]).astype(jnp.float32))
    _, idx = lax.top_k(s + p["b_router"].astype(jnp.float32), TOP_K)
    sel = jnp.take_along_axis(s, idx, axis=-1)
    w = sel / jnp.sum(sel, axis=-1, keepdims=True) * ROUTE_SCALE
    gates = jnp.einsum("nk,nke->ne", w, jax.nn.one_hot(idx, N_EXPERTS, dtype=jnp.float32)).astype(h.dtype)
    hg = jnp.einsum("nd,edf->nef", t, p["w_e_gate"])
    hu = jnp.einsum("nd,edf->nef", t, p["w_e_up"])
    routed = jnp.einsum("nef,efd->nd", jax.nn.silu(hg) * hu * gates[:, :, None], p["w_e_down"])
    shared = (jax.nn.silu(t @ p["w_s_gate"]) * (t @ p["w_s_up"])) @ p["w_s_down"]
    return (routed + shared).reshape(bn, l, d)

def trunk_layer(x, cvec, p, layer, ctx=None):
    bn, n, _ = x.shape
    mods = jax.nn.silu(cvec) @ p["w_ada"] + p["b_ada"]
    sh1, sc1, g1, sh2, sc2, g2 = jnp.split(mods[:, None, :], 6, axis=-1)
    h = rmsnorm(x, p["g_pre1"]) * (1.0 + sc1) + sh1
    dq, dk, dv, sz, sxbc, sdt, nq, nk, nv = split_in(h @ p["w_in"])
    dq = dq.reshape(bn, n, DA_H, 2, DA_HD).transpose(0, 2, 1, 3, 4)
    dk = dk.reshape(bn, n, DA_H, 2, DA_HD).transpose(0, 2, 1, 3, 4)
    dv = dv.reshape(bn, n, DA_H, 2 * DA_HD).transpose(0, 2, 1, 3)
    nq, nk, nv = [t.reshape(bn, n, NA_H, NA_HD).transpose(0, 2, 1, 3) for t in (nq, nk, nv)]
    lam, lam_init = diff_lambda(p["da_lambda"], layer)
    if ctx is None:
        h0_f = jnp.zeros((bn, SSM_H, SSM_P, SSM_N), x.dtype)
        h0_b = h0_f
        o_da = diff_attention(dq, dk, dv, lam)
        o_na = block_attention(nq, nk, nv)
    else:
        ck, cv, cnk, cnv, h0_f, h0_b = ctx
        tabs = axial_rope_tables(n)
        o_da = diff_attention(apply_axial_rope(dq, tabs),
                              jnp.concatenate([ck, apply_axial_rope(dk, tabs)], axis=2),
                              jnp.concatenate([cv, dv], axis=2), lam)
        o_na = neighbourhood_attention(nq, nk, nv, cnk, cnv, p["na_rpb"])
    o_da = (rmsnorm(o_da, p["da_subln"]) * (1.0 - lam_init)).transpose(0, 2, 1, 3).reshape(bn, n, DA_W)
    o_na = o_na.transpose(0, 2, 1, 3).reshape(bn, n, NA_W)
    o_ssm, hf, hb = ssm_branch(sz, sxbc, sdt, p, h0_f, h0_b)
    ga, gs, gn = jnp.split(jax.nn.sigmoid(h @ p["w_gate"]), 3, axis=-1)
    mix = (ga * (o_da @ p["w_br_da"]) + gs * (o_ssm @ p["w_br_ssm"]) + gn * (o_na @ p["w_br_na"])) @ p["w_out"]
    x = x + g1 * rmsnorm(mix, p["g_post1"])
    h2 = rmsnorm(x, p["g_pre2"]) * (1.0 + sc2) + sh2
    x = x + g2 * rmsnorm(moe_ffn(h2, p), p["g_post2"])
    state = (dk, dv, nk, nv, hf, hb) if ctx is None else None
    return x, state

def setup_inputs(seed: int = 0) -> dict:
    key = jax.random.key(seed)
    ks = iter(jax.random.split(key, 48))
    nrm = lambda shape, s: jax.random.normal(next(ks), shape, jnp.float32) * s
    L, D = DEPTH, D_MODEL
    out = {}
    out["x_prompt"] = nrm((BATCH, SEQ, D), 1.0)
    out["x_sample"] = nrm((DEC_BATCH, DEC_SEQ, D), 1.0)
    out["c"] = nrm((DEC_BATCH, D), 1.0)
    out["cache_da_k"] = nrm((DEC_BATCH, L, DA_H, PAST_LEN, 2, DA_HD), 1.0)
    out["cache_da_v"] = nrm((DEC_BATCH, L, DA_H, PAST_LEN, 2 * DA_HD), 1.0)
    out["cache_na_k"] = nrm((DEC_BATCH, L, NA_H, PAST_LEN, NA_HD), 1.0)
    out["cache_na_v"] = nrm((DEC_BATCH, L, NA_H, PAST_LEN, NA_HD), 1.0)
    out["state_ssm_f"] = nrm((DEC_BATCH, L, SSM_H, SSM_P, SSM_N), 0.5)
    out["state_ssm_b"] = nrm((DEC_BATCH, L, SSM_H, SSM_P, SSM_N), 0.5)
    out["c_ctx"] = nrm((D,), 1.0)
    out["w_ada"] = nrm((L, D, 6 * D), 0.5 * D ** -0.5)
    out["b_ada"] = nrm((L, 6 * D), 0.02)
    out["g_pre1"] = 1.0 + nrm((L, D), 0.05)
    out["g_post1"] = 1.0 + nrm((L, D), 0.05)
    out["g_pre2"] = 1.0 + nrm((L, D), 0.05)
    out["g_post2"] = 1.0 + nrm((L, D), 0.05)
    out["w_in"] = nrm((L, D, IN_W), D ** -0.5)
    out["w_gate"] = nrm((L, D, 3 * D), D ** -0.5)
    out["da_lambda"] = nrm((L, 4, DA_HD), 0.1)
    out["da_subln"] = 1.0 + nrm((L, 2 * DA_HD), 0.05)
    out["ssm_conv_w"] = nrm((L, CONV_W, CONV_CH), CONV_W ** -0.5)
    out["ssm_conv_b"] = nrm((L, CONV_CH), 0.02)
    dt = jnp.exp(jax.random.uniform(next(ks), (L, 2, SSM_H), jnp.float32, math.log(1e-3), math.log(1e-1)))
    out["ssm_dt_bias"] = dt + jnp.log(-jnp.expm1(-dt))
    out["ssm_a_log"] = jnp.log(jax.random.uniform(next(ks), (L, 2, SSM_H), jnp.float32, 1.0, 16.0))
    out["ssm_d"] = 1.0 + nrm((L, SSM_H), 0.1)
    out["ssm_norm"] = 1.0 + nrm((L, SSM_DI), 0.05)
    out["na_rpb"] = nrm((L, NA_H, 2 * WIN_R - 1, 2 * WIN_C - 1), 0.05)
    out["w_br_da"] = nrm((L, DA_W, D), DA_W ** -0.5)
    out["w_br_ssm"] = nrm((L, SSM_DI, D), SSM_DI ** -0.5)
    out["w_br_na"] = nrm((L, NA_W, D), NA_W ** -0.5)
    out["w_out"] = nrm((L, D, D), D ** -0.5)
    out["w_router"] = nrm((L, D, N_EXPERTS), D ** -0.5)
    out["b_router"] = nrm((L, N_EXPERTS), 0.01)
    out["w_e_gate"] = nrm((L, N_EXPERTS, D, EXPERT_FF), D ** -0.5)
    out["w_e_up"] = nrm((L, N_EXPERTS, D, EXPERT_FF), D ** -0.5)
    out["w_e_down"] = nrm((L, N_EXPERTS, EXPERT_FF, D), EXPERT_FF ** -0.5)
    out["w_s_gate"] = nrm((L, D, SHARED_FF), D ** -0.5)
    out["w_s_up"] = nrm((L, D, SHARED_FF), D ** -0.5)
    out["w_s_down"] = nrm((L, SHARED_FF, D), SHARED_FF ** -0.5)
    return out

def reference(x_prompt, x_sample, c, cache_da_k, cache_da_v, cache_na_k, cache_na_v, state_ssm_f, state_ssm_b,
              c_ctx, w_ada, b_ada, g_pre1, g_post1, g_pre2, g_post2, w_in, w_gate, da_lambda, da_subln,
              ssm_conv_w, ssm_conv_b, ssm_dt_bias, ssm_a_log, ssm_d, ssm_norm, na_rpb, w_br_da, w_br_ssm,
              w_br_na, w_out, w_router, b_router, w_e_gate, w_e_up, w_e_down, w_s_gate, w_s_up, w_s_down):
    stacked = {
        "w_ada": w_ada, "b_ada": b_ada, "g_pre1": g_pre1, "g_post1": g_post1, "g_pre2": g_pre2,
        "g_post2": g_post2, "w_in": w_in, "w_gate": w_gate, "da_lambda": da_lambda, "da_subln": da_subln,
        "ssm_conv_w": ssm_conv_w, "ssm_conv_b": ssm_conv_b, "ssm_dt_bias": ssm_dt_bias, "ssm_a_log": ssm_a_log,
        "ssm_d": ssm_d, "ssm_norm": ssm_norm, "na_rpb": na_rpb, "w_br_da": w_br_da, "w_br_ssm": w_br_ssm,
        "w_br_na": w_br_na, "w_out": w_out, "w_router": w_router, "b_router": b_router, "w_e_gate": w_e_gate,
        "w_e_up": w_e_up, "w_e_down": w_e_down, "w_s_gate": w_s_gate, "w_s_up": w_s_up, "w_s_down": w_s_down,
    }
    xp, xs = x_prompt, x_sample
    cvec_ctx = c_ctx[None]
    new = ([], [], [], [], [], [])
    for layer in range(DEPTH):
        p = {name: arr[layer] for name, arr in stacked.items()}
        xp, st = trunk_layer(xp, cvec_ctx, p, layer)
        for lst, arr in zip(new, st):
            lst.append(arr)
        ctx = (cache_da_k[:, layer], cache_da_v[:, layer], cache_na_k[:, layer], cache_na_v[:, layer],
               state_ssm_f[:, layer], state_ssm_b[:, layer])
        xs, _ = trunk_layer(xs, c, p, layer, ctx)
    new_da_k = jnp.stack(new[0], axis=1)
    new_da_v = jnp.stack(new[1], axis=1)
    new_na_k = jnp.stack(new[2], axis=1)
    new_na_v = jnp.stack(new[3], axis=1)
    new_ssm_f = jnp.stack(new[4], axis=1)
    new_ssm_b = jnp.stack(new[5], axis=1)
    return (xp, xs, new_da_k, new_da_v, new_na_k, new_na_v, new_ssm_f, new_ssm_b)


_drawn_inputs = setup_inputs


def setup_inputs(seed=0):
    import zlib

    import numpy as np

    out = dict(_drawn_inputs(seed))
    spreads = {}
    factors = {'na_rpb': 3.522}
    for name, (base, spread) in spreads.items():
        noise = np.random.default_rng([zlib.crc32(name.encode()), seed]).standard_normal(out[name].shape)
        drawn = base * np.exp(spread * noise) if base else spread * noise
        out[name] = __import__('jax').numpy.asarray(drawn.astype(out[name].dtype))
    for name, factor in factors.items():
        out[name] = (out[name] * factor).astype(out[name].dtype)
    return out
```

```python
import math
from contextlib import ExitStack

import concourse.bass as bass
import numpy as np
from concourse import mybir

F32 = mybir.dt.float32
ALU = mybir.AluOpType
ACT = mybir.ActivationFunctionType
AX = mybir.AxisListType

P = 128
D = 1024
KT = D // P
DEPTH = 2
CTX = 128
LAT = 512
TOK = CTX + LAT
TILES = TOK // P
PAST = 128
GRID_W = 64
ROWS = LAT // GRID_W
EPS = 1e-6
DA_H, DA_HD = 4, 64
NA_H, NA_HD = 8, 64
SSM_H, SSM_P, SSM_N, SSM_G = 8, 64, 128, 2
CONV_W = 5
CONV_CH = 1024
WIN_R, WIN_C, QB_C = 8, 16, 16
NBLK = GRID_W // QB_C
WCOLS = 32
NKEY = ROWS * WCOLS
RPB_R, RPB_C = 2 * WIN_R - 1, 2 * WIN_C - 1
RPB_FRONT = 32
RPB_ROW = RPB_FRONT + RPB_R * WCOLS + 32
NE, TOP_K, FF, SFF = 32, 4, 128, 256
ROUTE_SCALE = 2.5
SEC = 512
SLOTS = 4
XPW = TOK + 6
MASKED = -1.0e30

OFF = {}
_at = 0
for _n, _w in (("dq", 512), ("dk", 512), ("dv", 512), ("z", 512), ("xb0", 512), ("xb1", 512), ("dt", 16),
               ("nq", 512), ("nk", 512), ("nv", 512)):
    OFF[_n] = _at
    _at += _w

SECTIONS = [("ada", i) for i in range(12)]
SECTIONS += [("in", n) for n in ("xb0", "xb1", "z")] + [("gate", 2), ("br", "s"), ("gate", 3)]
SECTIONS += [("in", n) for n in ("dq", "dk", "dv")] + [("gate", 0), ("br", "a"), ("gate", 1)]
SECTIONS += [("in", n) for n in ("nq", "nk", "nv")] + [("gate", 4), ("br", "n"), ("gate", 5)]
SECTIONS += [("out", 0), ("out", 1), ("shared_up", 0), ("shared_down", 0)]
FIRST_EXPERT = len(SECTIONS)
SECTIONS += [("expert", e) for e in range(NE)]
AT = {s: i for i, s in enumerate(SECTIONS)}


def parts_of(i):
    return {"expert": 3, "shared_up": 2}.get(SECTIONS[i][0], 1)


def full_count(i):
    return 16 * sum(parts_of(j) for j in range(i % SLOTS, i + 1, SLOTS))


def tok(t):
    return slice(t * P, (t + 1) * P)


def col0(j):
    return min(max(QB_C * j - WIN_C // 2, 0), GRID_W - WCOLS)


def shape_constants():
    t = np.arange(P)
    a, b = t[:, None], t[None, :]
    rot = np.zeros((P, P), np.float32)
    for o in range(P):
        if o % 32 < 16:
            rot[o + 16, o] = -1.0
        else:
            rot[o - 16, o] = 1.0
    base = np.concatenate([m.astype(np.float32) for m in
                           (a == b, rot, a <= b, a > b, a >= b, a < b, np.ones((P, P)))], axis=1)
    n_freq = DA_HD // 4
    inv = (np.float32(10000.0) ** (-np.arange(n_freq, dtype=np.float32) / np.float32(n_freq))).astype(np.float32)
    pos = np.arange(LAT)
    ang = np.zeros((P, LAT), np.float32)
    for p in range(P):
        d = p % DA_HD
        at = (pos // GRID_W if d < 32 else pos % GRID_W).astype(np.float32)
        ang[p] = at * inv[d % 16]
    rope = np.concatenate([np.cos(ang), np.sin(ang)], axis=1).astype(np.float32)
    mask = np.zeros((P, NBLK, NKEY), np.float32)
    for q in range(P):
        for j in range(NBLK):
            qc = QB_C * j + QB_C - 1 - q % QB_C
            s = min(max(qc - WIN_C // 2, 0), GRID_W - WIN_C)
            kc = col0(j) + np.arange(NKEY) % WCOLS
            mask[q, j] = np.where((kc >= s) & (kc < s + WIN_C), 0.0, MASKED)
    lam = np.zeros((DEPTH, P, 2), np.float32)
    for layer in range(DEPTH):
        li = 0.8 - 0.6 * math.exp(-0.3 * layer)
        lam[layer, :, 0], lam[layer, :, 1] = li, 1.0 - li
    sel = np.zeros((2, 2, P), np.float32)
    sel[0, 0], sel[1, 1] = 1.0, 1.0
    return {"k_base": base, "k_rope": rope, "k_mask": mask.reshape(P, -1), "k_lam": lam, "k_sel": sel}


class Link:

    def __init__(self, sem):
        self.sem, self.n = sem, 0

    def __call__(self, eng, ins):
        ins.then_inc(self.sem, 1)
        self.n += 1
        eng.wait_ge(self.sem, self.n)


class Cx:
    pass


def spread(ap, axis, n):
    ap = ap.unsqueeze(axis)
    shape = list(ap.shape)
    shape[axis] = n
    return ap.broadcast_to(shape)


def reverse(ap, *axes):
    dims = [list(d) for d in ap.ap]
    offset = ap.offset
    for x in axes:
        offset = offset + dims[x][0] * (dims[x][1] - 1)
        dims[x][0] = -dims[x][0]
    return bass.AP(tensor=ap.tensor, offset=offset, ap=dims)



def load_section(cx, sp, L, i, first=False):
    kind, which = SECTIONS[i]
    s = i % SLOTS
    if i >= SLOTS and not first:
        sp.wait_ge(cx.ring_free, i - SLOTS + 1)
    w = cx.w
    slot = cx.ring[:, s, :]

    def fm(src, a, b, dst):
        sp.dma_start(dst, src[bass.ds(L, 1), :, a:b].rearrange("l (p k) n -> p (l k) n", k=KT)).then_inc(
            cx.ring_full[s], 16)

    wide = slot.rearrange("p (k n) -> p k n", k=KT)
    if kind == "ada":
        fm(w["w_ada"], which * SEC, (which + 1) * SEC, wide)
    elif kind == "in":
        fm(w["w_in"], OFF[which], OFF[which] + SEC, wide)
    elif kind == "gate":
        fm(w["w_gate"], which * SEC, (which + 1) * SEC, wide)
    elif kind == "br":
        src = w[{"a": "w_br_da", "s": "w_br_ssm", "n": "w_br_na"}[which]]
        sp.dma_start(slot.rearrange("p (k n) -> p k n", k=4),
                     src[bass.ds(L, 1)].rearrange("l (k p) n -> p (l k) n", p=P)).then_inc(cx.ring_full[s], 16)
    elif kind == "out":
        sp.dma_start(wide, w["w_out"][bass.ds(L, 1), :, which * SEC:(which + 1) * SEC].rearrange(
            "l (k p) n -> p (l k) n", p=P)).then_inc(cx.ring_full[s], 16)
    elif kind == "shared_up":
        fm(w["w_s_gate"], 0, SFF, wide[:, :, 0:SFF])
        fm(w["w_s_up"], 0, SFF, wide[:, :, SFF:2 * SFF])
    elif kind == "shared_down":
        sp.dma_start(slot[:, 0:2 * D].rearrange("p (k n) -> p k n", k=2),
                     w["w_s_down"][bass.ds(L, 1)].rearrange("l (k p) n -> p (l k) n", p=P)).then_inc(
            cx.ring_full[s], 16)
    else:
        load_expert(cx, sp, L * NE + which, s)


def load_expert(cx, sp, le, s):
    w = cx.w
    for n, name in enumerate(("w_e_gate", "w_e_up")):
        sp.dma_start(cx.ring[:, s, n * D:(n + 1) * D],
                     w[name].rearrange("l e (p k) f -> (l e) p (k f)", k=KT)[bass.ds(le, 1)].rearrange(
                         "o p n -> (o p) n")).then_inc(cx.ring_full[s], 16)
    sp.dma_start(cx.ring[:, s, 2 * D:3 * D],
                 w["w_e_down"].rearrange("l e f d -> (l e) f d")[bass.ds(le, 1)].rearrange(
                     "o p n -> (o p) n")).then_inc(cx.ring_full[s], 16)


def load_behind(cx, sp, L, a, b):
    for i in range(AT[a] + SLOTS, AT[b] + SLOTS + 1):
        load_section(cx, sp, L, i)


def section_ready(cx, pe, key):
    i = AT[key]
    pe.wait_ge(cx.ring_full[i % SLOTS], full_count(i))
    return cx.ring[:, i % SLOTS, :]


def project_fm(cx, pe, wide, c, lat, ctx, hT=None, kt_n=KT):
    hT = cx.hT if hT is None else hT
    for k in range(kt_n):
        pe.matmul(lat, wide[:, k, c], hT[:, k, CTX:TOK], start=(k == 0), stop=(k == kt_n - 1))
    for k in range(kt_n):
        last = pe.matmul(ctx, wide[:, k, c], hT[:, k, 0:CTX], start=(k == 0), stop=(k == kt_n - 1))
    return last


def project_tm(cx, pe, wide, t, out):
    for k in range(KT):
        last = pe.matmul(out, cx.hT[:, k, tok(t)], wide[:, k, :], start=(k == 0), stop=(k == KT - 1))
    return last



def norm_scalar(cx, act, sub, x, xn):
    for t in range(TILES):
        act.activation(xn[:, t, :], x[:, t, :], ACT.Square, accum_out=cx.ssq[:, sub, t:t + 1]).then_inc(
            cx.squares_ready, 1)
    act.wait_ge(cx.squares_ready, (sub + 1) * TILES)
    act.activation(cx.rms[:, sub, :], cx.ssq[:, sub, :], ACT.Sqrt, scale=1.0 / D, bias=cx.eps[:, :]).then_inc(
        cx.rms_ready, 1)


def norm_vector(cx, dve, sub, x, xn):
    dve.wait_ge(cx.rms_ready, sub + 1)
    cx.vlink(dve, dve.reciprocal(cx.rstd[:, sub, :], cx.rms[:, sub, :]))
    for t in range(TILES):
        dve.tensor_scalar(xn[:, t, :], x[:, t, :], cx.rstd[:, sub, t:t + 1], None, ALU.mult).then_inc(
            cx.xn_ready, 1)


def norm_tensor(cx, pe, sub, xn):
    pe.wait_ge(cx.xn_ready, (sub + 1) * TILES)
    for k in range(KT):
        n = sub * KT + k
        if k >= 4:
            pe.wait_ge(cx.h_lat_ready, n - 3)
            pe.wait_ge(cx.h_ctx_ready, n - 3)
        for t in range(TILES):
            out = cx.ps[:, 4 + k % 4, 0:P] if t == 0 else cx.ps[:, k % 4, tok(t - 1)]
            ins = pe.transpose(out, xn[:, t, k:D:KT], cx.ident)
        ins.then_inc(cx.xnT_ready, 1)


def modulate_scalar(cx, act, sub):
    act.wait_ge(cx.mods_ready, 1)
    for k in range(KT):
        act.wait_ge(cx.xnT_ready, sub * KT + k + 1)
        act.activation(cx.hT[:, k, CTX:TOK], cx.ps[:, k % 4, :], ACT.Identity, scale=cx.mod_scale[:, sub, k, 1:2],
                       bias=cx.mod_shift[:, sub, k, 1:2]).then_inc(cx.h_lat_ready, 1)


def modulate_vector(cx, dve, sub):
    for k in range(KT):
        dve.wait_ge(cx.xnT_ready, sub * KT + k + 1)
        dve.tensor_scalar(cx.hT[:, k, 0:CTX], cx.ps[:, 4 + k % 4, 0:P], cx.mod_scale[:, sub, k, 0:1],
                          cx.mod_shift[:, sub, k, 0:1], ALU.mult, ALU.add).then_inc(cx.h_ctx_ready, 1)



def stage_ada(nc, cx, L):
    w = cx.w
    with ExitStack() as st:
        def sb(name, shape):
            return st.enter_context(nc.sbuf_tensor(name, shape, F32))
        x = sb("ada_x", [P, TILES, D])
        xn = sb("ada_xn", [P, TILES, D])
        csT = sb("ada_csT", [P, 2, KT])
        mods = sb("ada_mods", [2, 6 * D])
        gpre = sb("ada_gpre", [P, 2, KT])
        gpost = sb("ada_gpost", [P, 2, D])
        sem = cx.sem
        block = st.enter_context(nc.Block())

        @block.sync
        def _(sp):
            sp.dma_start(csT[:, 0, :], w["c_ctx"].rearrange("(p k) -> p k", k=KT)).then_inc(sem("ada_small"), 16)
            sp.dma_start(csT[:, 1, :], w["c"].rearrange("o (p k) -> (o p) k", k=KT)).then_inc(sem("ada_small"), 16)
            for i in range(SLOTS):
                load_section(cx, sp, L, i, first=True)
            b = w["b_ada"][bass.ds(L, 1), :]
            for g in range(2):
                sp.dma_start(mods[g:g + 1, :], b).then_inc(sem("ada_bias"), 16)
            sp.dma_start(x[:, 0, :], cx.y_prompt.rearrange("o n d -> (o n) d")).then_inc(sem("x_loaded"), 16)
            sp.dma_start(x[:, 1:TILES, :], cx.y_sample.rearrange("o (t p) d -> p (o t) d", p=P)).then_inc(
                sem("x_loaded"), 16)
            for n, (pre, post) in enumerate((("g_pre1", "g_post1"), ("g_pre2", "g_post2"))):
                sp.dma_start(gpre[:, n, :], w[pre][bass.ds(L, 1)].rearrange("o (p k) -> (o p) k", k=KT)).then_inc(
                    sem("ada_gains"), 16)
                sp.dma_start(gpost[:, n, :], w[post][bass.ds(L, 1)].broadcast_to([P, D])).then_inc(
                    sem("ada_gains"), 16)
            with sp.Fori(1, 3) as i:
                for s in range(SLOTS):
                    sp.wait_ge(cx.ring_free, i * SLOTS + (s + 1 - SLOTS))
                    sp.dma_start(cx.ring[:, s, :].rearrange("p (k n) -> p k n", k=KT),
                                 w["w_ada"].rearrange("l (p k) (c n) -> l p k c n", k=KT, n=SEC)[
                                     bass.ds(L, 1), :, :, bass.ds(i * SLOTS + s, 1), :].rearrange(
                                     "l p k c n -> p (l k) (c n)")).then_inc(cx.ring_full[s], 16)
            for i in range(12, 16):
                load_section(cx, sp, L, i)

        @block.scalar
        def _(act):
            act.wait_ge(sem("ada_small"), 32)
            act.activation(csT[:, :, :], csT[:, :, :], ACT.Silu).then_inc(sem("c_silu"), 1)
            act.wait_ge(sem("x_loaded"), 32)
            norm_scalar(cx, act, 0, x, xn)
            modulate_scalar(cx, act, 0)

        @block.vector
        def _(dve):
            dve.wait_ge(sem("ada_bias"), 32)
            with dve.Fori(0, 3) as i:
                for s in range(SLOTS):
                    dve.wait_ge(sem("ada_mm"), i * SLOTS + (s + 1))
                    m = mods[:, bass.ds((i * SLOTS + s) * SEC, SEC)]
                    dve.tensor_tensor(m, cx.ps[0:2, s, :], m, ALU.add).then_inc(sem("ada_out"), 1)
            norm_vector(cx, dve, 0, x, xn)
            dve.wait_ge(sem("ada_turned"), 1)
            dve.wait_ge(sem("ada_gains"), 64)
            tp = cx.ps[:, 4, 0:64].rearrange("p (s k g) -> p s k g", s=4, k=KT)
            for sub in range(2):
                dve.tensor_copy(cx.mod_shift[:, sub, :, :], tp[:, 2 * sub, :, :])
                ins = dve.scalar_tensor_tensor(out=cx.mod_scale[:, sub, :, :], in0=tp[:, 2 * sub + 1, :, :], scalar=1.0,
                                               in1=spread(gpre[:, sub, :], 2, 2), op0=ALU.add, op1=ALU.mult)
            ins.then_inc(cx.mods_ready, 1)
            for sub in range(2):
                for g in range(2):
                    for h in range(2):
                        dve.wait_ge(sem("gate_rows"), sub * 4 + g * 2 + h + 1)
                        dve.tensor_tensor(cx.gate_post[:, sub, g, h * SEC:(h + 1) * SEC], cx.ps[:, g * 2 + h, :],
                                          gpost[:, sub, h * SEC:(h + 1) * SEC], ALU.mult).then_inc(sem("gate_out"), 1)
            dve.wait_ge(cx.mods_ready, 1)
            modulate_vector(cx, dve, 0)

        @block.tensor
        def _(pe):
            pe.wait_ge(sem("c_silu"), 1)

            def four_sections(i):
                for s in range(SLOTS):
                    pe.wait_ge(cx.ring_full[s], i * 16 + 16)
                    for k in range(KT):
                        ins = pe.matmul(cx.ps[0:2, s, :], csT[:, :, k], cx.ring[:, s, k * SEC:(k + 1) * SEC],
                                        start=(k == 0), stop=(k == KT - 1))
                    ins.then_inc(sem("ada_mm"), 1)
                    pe.wait_ge(sem("ada_mm"), i * SLOTS + (s + 1))
                    pe.sem_inc(cx.ring_free, 1)

            four_sections(0)
            with pe.Fori(1, 3) as i:
                pe.wait_ge(sem("ada_out"), i * SLOTS)
                four_sections(i)
            pe.wait_ge(sem("ada_out"), 12)
            for s, section in enumerate((0, 1, 3, 4)):
                for k in range(KT):
                    c = (s * KT + k) * 2
                    ins = pe.transpose(cx.ps[:, 4, c:c + 2], mods[:, section * D + k:(section + 1) * D:KT],
                                       cx.ident[0:2, 0:2])
            ins.then_inc(sem("ada_turned"), 1)
            for sub, section in enumerate((2, 5)):
                for g in range(2):
                    for h in range(2):
                        if sub:
                            pe.wait_ge(sem("gate_out"), g * 2 + h + 1)
                        a = section * D + h * SEC
                        pe.matmul(cx.ps[:, g * 2 + h, :], cx.sel[:, g, :], mods[:, a:a + SEC], start=True,
                                  stop=True).then_inc(sem("gate_rows"), 1)
            pe.wait_ge(sem("gate_out"), 8)
            pe.wait_ge(cx.mods_ready, 1)
            norm_tensor(cx, pe, 0, xn)



def conv_tile(t):
    a = 2 if t == 0 else 4 + t * P
    return slice(a, a + P)


def stage_ssm(nc, cx, L):
    w = cx.w
    sem = cx.sem
    LE, GT, GE, LT, ONES = cx.le, cx.gt, cx.ge, cx.lt, cx.ones
    with ExitStack() as st:
        def sb(name, shape):
            return st.enter_context(nc.sbuf_tensor(name, shape, F32))
        xp = sb("ssm_xp", [P, 4, XPW])
        cv = sb("ssm_cv", [P, 8, XPW])
        sz = sb("ssm_sz", [P, TILES, 512])
        xs = sb("ssm_xs", [P, TILES, 512])
        bt = sb("ssm_bt", [P, TILES, 256])
        xdt = sb("ssm_xdt", [P, 2, 512])
        xdd = sb("ssm_xdd", [P, 512])
        am = sb("ssm_am", [P, 8, P])
        mt = sb("ssm_mt", [P, 2, 8, P])
        cbm = sb("ssm_cbm", [P, 2, 2, P])
        tmp = sb("ssm_tmp", [P, 512])
        rows = sb("ssm_rows", [52, P])
        cols = sb("ssm_cols", [P, 52])
        nrm = cols[:, 48:52]
        wdt = sb("ssm_wdt", [P, KT, 16])
        dv = sb("ssm_dv", [P, 8, TILES, 16])
        hb = sb("ssm_hb", [P, 3, 16])
        dec = sb("ssm_dec", [P, 6, TILES, 8])
        st2 = sb("ssm_ss", [P, 3, 2 * TILES])
        dt, a = dv[:, 7], dv[:, 6]
        state = [cv[:, 0:4, :].rearrange("p a b -> p (a b)")[:, 0:2048].rearrange("p (k f) -> p k f", k=4),
                 xp[:, :, :].rearrange("p a b -> p (a b)")[:, 0:2048].rearrange("p (k f) -> p k f", k=4)]
        hin = am[:, 0:4, :]
        ps = cx.ps
        block = st.enter_context(nc.Block())
        steps = [(0, 1, 1), (1, 4, 2), (0, 2, 2), (1, 3, 1), (0, 3, 3), (1, 2, 0)]

        @block.sync
        def _(sp):
            sp.dma_start(rows[0:40, :], w["ssm_conv_w"].rearrange("l j (m p) -> l (j m) p", p=P)[
                bass.ds(L, 1)].rearrange("o r p -> (o r) p")).then_inc(sem("ssm_conv_in"), 16)
            sp.dma_start(rows[40:48, :], w["ssm_conv_b"].rearrange("l (m p) -> l m p", p=P)[
                bass.ds(L, 1)].rearrange("o r p -> (o r) p")).then_inc(sem("ssm_conv_in"), 16)
            sp.dma_start(rows[48:52, :], w["ssm_norm"].rearrange("l (m p) -> l m p", p=P)[
                bass.ds(L, 1)].rearrange("o r p -> (o r) p")).then_inc(sem("ssm_conv_in"), 16)
            sp.dma_start(wdt[:, :, :], w["w_in"][bass.ds(L, 1), :, OFF["dt"]:OFF["dt"] + 16].rearrange(
                "l (p k) n -> p (l k) n", k=KT)).then_inc(sem("ssm_small"), 16)
            sp.dma_start(hb[:, 0, :], w["ssm_dt_bias"].rearrange("l a b -> l (a b)")[bass.ds(L, 1)].broadcast_to(
                [P, 16])).then_inc(sem("ssm_small"), 16)
            sp.dma_start(hb[:, 1, :], w["ssm_a_log"].rearrange("l a b -> l (a b)")[bass.ds(L, 1)].broadcast_to(
                [P, 16])).then_inc(sem("ssm_small"), 16)
            sp.dma_start(hb[:, 2, 0:8], w["ssm_d"][bass.ds(L, 1)].broadcast_to([P, 8])).then_inc(
                sem("ssm_small"), 16)
            load_behind(cx, sp, L, ("in", "xb0"), ("in", "z"))
            for d, name in enumerate(("state_ssm_f", "state_ssm_b")):
                if d:
                    sp.wait_ge(sem("h0_turned"), 1)
                sp.dma_start(hin, w[name].rearrange("o l h p n -> (o l) (h p) n")[bass.ds(L, 1)].rearrange(
                    "o (m q) n -> q (o m) n", q=P)).then_inc(sem("h0_loaded"), 16)
                if d == 0:
                    sp.wait_ge(sem("h0_loaded"), 16)
            for d, out in enumerate((cx.new_ssm_f, cx.new_ssm_b)):
                sp.wait_ge(sem("hf_copied"), d + 1)
                sp.dma_start(out.rearrange("o l h p n -> (o l) (h p) n")[bass.ds(L, 1)].rearrange(
                    "o (m q) n -> q (o m) n", q=P), mt[:, d, 0:4, :]).then_inc(sem("hf_stored"), 16)
            sp.wait_ge(sem("hf_stored"), 32)

        @block.tensor
        def _(pe):
            pe.wait_ge(sem("ssm_conv_in"), 48)
            pe.transpose(ps[:, 7, 0:52], rows[:, :], cx.ident[0:52, 0:52]).then_inc(sem("cols_turned"), 1)
            for m in range(8):
                wide = section_ready(cx, pe, ("in", f"xb{m // 4}")).rearrange("p (k n) -> p k n", k=KT)
                if m >= 2:
                    pe.wait_ge(sem("xb_lat_out"), m - 1)
                    pe.wait_ge(sem("xb_ctx_out"), m - 1)
                c = slice((m % 4) * P, (m % 4 + 1) * P)
                project_fm(cx, pe, wide, c, ps[:, m % 2, :], ps[:, 2 + m % 2, 0:P]).then_inc(sem("xb_mm"), 1)
                if m % 4 == 3:
                    pe.wait_ge(sem("xb_mm"), m + 1)
                    pe.sem_inc(cx.ring_free, 1)
            pe.wait_ge(sem("ssm_small"), 64)
            for t in range(TILES):
                for k in range(KT):
                    ins = pe.matmul(ps[:, 6, t * 16:(t + 1) * 16], cx.hT[:, k, tok(t)], wdt[:, k, :],
                                    start=(k == 0), stop=(k == KT - 1))
            ins.then_inc(sem("dt_mm"), 1)
            wide = section_ready(cx, pe, ("in", "z")).rearrange("p (k n) -> p k n", k=KT)
            for t in range(TILES):
                if t >= 2:
                    pe.wait_ge(sem("z_out"), t - 1)
                project_tm(cx, pe, wide, t, ps[:, 4 + t % 2, :]).then_inc(sem("z_mm"), 1)
            pe.wait_ge(sem("z_mm"), TILES)
            pe.sem_inc(cx.ring_free, 1)
            pe.wait_ge(sem("a_ready"), 1)
            pe.wait_ge(sem("dt_read"), 1)
            for n, (m, d) in enumerate(((LE, 0), (GE, 1), (GT, 0), (LT, 1), (ONES, 0), (ONES, 1))):
                ins = pe.matmul(ps[:, 6, n * 40:(n + 1) * 40].rearrange("p (t h) -> p t h", h=8), m, a[:, :, d * 8:(d + 1) * 8], start=True, stop=True)
            ins.then_inc(sem("dec_mm"), 1)
            pe.wait_ge(sem("xb_silu"), 6)
            pe.wait_ge(sem("xb_lat_out"), 8)
            pe.wait_ge(sem("xb_ctx_out"), 8)
            for t in range(TILES):
                if t >= 2:
                    pe.wait_ge(sem("xs_out"), t - 1)
                    pe.wait_ge(sem("b_out"), t - 1)
                for m in range(4):
                    pe.transpose(ps[:, t % 2, m * P:(m + 1) * P], cv[:, m, conv_tile(t)], cx.ident)
                for m in range(2):
                    ins = pe.transpose(ps[:, 2 + t % 2, m * P:(m + 1) * P], cv[:, 4 + m, conv_tile(t)], cx.ident)
                ins.then_inc(sem("xs_turned"), 1)
            pe.wait_ge(sem("xs_out"), TILES)
            pe.wait_ge(sem("b_out"), TILES)
            for d in range(2):
                pe.wait_ge(sem("h0_loaded"), 16 * (d + 1))
                for m in range(4):
                    ins = pe.transpose(ps[:, d, m * P:(m + 1) * P], hin[:, m, :], cx.ident)
                ins.then_inc(sem("h0_turned"), 1)
            pe.wait_ge(sem("z_out"), TILES)
            for n, (d, t, _) in enumerate([(0, 0, 0), (1, 0, 0)] + steps):
                pe.wait_ge(sem("xdd_ready"), n + 1)
                if n >= 2:
                    pe.wait_ge(sem("ds_used"), n - 1)
                for g in range(SSM_G):
                    ins = pe.matmul(ps[:, 4 + n % 2, g * 256:(g + 1) * 256], bt[:, t, g * P:(g + 1) * P],
                                    xdd[:, g * 256:(g + 1) * 256], start=True, stop=True)
                ins.then_inc(sem("ds_mm"), 1)
                if n < 2:
                    pe.wait_ge(sem("ds_used"), n + 1)
                    for m in range(4):
                        ins = pe.transpose(ps[:, 2 + n, m * P:(m + 1) * P], tmp[:, m * P:(m + 1) * P], cx.ident)
                    ins.then_inc(sem("hf_turned"), 1)
            pe.wait_ge(sem("h0_ready"), 2)
            pe.wait_ge(sem("hf_copied"), 2)
            pe.wait_ge(sem("ds_used"), 8)
            pe.wait_ge(sem("xb_silu"), 8)
            for t in range(TILES):
                if t:
                    pe.wait_ge(sem("cb_out"), t)
                for g in range(SSM_G):
                    ins = pe.matmul(ps[:, 0, g * P:(g + 1) * P], cv[:, 4 + g, conv_tile(t)], cv[:, 6 + g, conv_tile(t)],
                                    start=True, stop=True)
                ins.then_inc(sem("cb_mm"), 1)
                for d in range(2):
                    n = 2 * t + d
                    pe.wait_ge(sem("am_ready"), n + 1)
                    if n:
                        pe.wait_ge(sem("seg_exp"), n)
                    for h in range(2):
                        ins = pe.matmul(ps[:, 1 + h, :], (GT, LT)[d], am[:, 4 * h:4 * h + 4, :].rearrange("p h s -> p (h s)"), start=True, stop=True)
                    ins.then_inc(sem("seg_mm"), 1)
                if t:
                    pe.wait_ge(sem("y_done"), t)
                    for d in range(2):
                        for g in range(SSM_G):
                            ins = pe.matmul(ps[:, 4 + d, g * 256:(g + 1) * 256], cv[:, 6 + g, conv_tile(t)],
                                            state[d][:, t - 1, g * 256:(g + 1) * 256], start=True, stop=True)
                    ins.then_inc(sem("yoff_mm"), 1)
                pe.wait_ge(sem("mt_ready"), 2 * t + 2)
                for h in range(SSM_H):
                    for d in range(2):
                        ins = pe.matmul(ps[:, 3, h * 64:(h + 1) * 64], mt[:, d, h, :], xdt[:, d, h * 64:(h + 1) * 64],
                                        start=(d == 0), stop=(d == 1))
                ins.then_inc(sem("y_mm"), 1)
            pe.wait_ge(sem("y_normed"), 1)
            for m in range(4):
                if m >= 2:
                    pe.wait_ge(sem("ossm_lat"), m - 1)
                    pe.wait_ge(sem("ossm_ctx"), m - 1)
                for t in range(TILES):
                    out = ps[:, 6 + m % 2, 0:P] if t == 0 else ps[:, m % 2, tok(t - 1)]
                    ins = pe.transpose(out, xs[:, t, m * P:(m + 1) * P], cx.ident)
                ins.then_inc(sem("ossm_turned"), 1)

        @block.scalar
        def _(act):
            for m in range(8):
                act.wait_ge(sem("xb_mm"), m + 1)
                if m >= 4:
                    act.wait_ge(sem("conv_done"), m - 3)
                act.activation(xp[:, m % 4, 4 + CTX:4 + TOK], ps[:, m % 2, :], ACT.Copy).then_inc(
                    sem("xb_lat_out"), 1)
                if m >= 2:
                    act.wait_ge(sem("conv_done"), m - 1)
                    act.activation(cv[:, m - 2, 2:XPW - 2], cv[:, m - 2, 2:XPW - 2], ACT.Silu).then_inc(
                        sem("xb_silu"), 1)
            for m in range(6, 8):
                act.wait_ge(sem("conv_done"), m + 1)
                act.activation(cv[:, m, 2:XPW - 2], cv[:, m, 2:XPW - 2], ACT.Silu).then_inc(sem("xb_silu"), 1)
            for t in range(TILES):
                act.wait_ge(sem("z_mm"), t + 1)
                act.activation(sz[:, t, :], ps[:, 4 + t % 2, :], ACT.Silu).then_inc(sem("z_out"), 1)
            act.wait_ge(sem("dt_abs"), 1)
            act.wait_ge(sem("ssm_small"), 64)
            act.activation(dv[:, 2], dv[:, 1], ACT.Exp, scale=-1.0)
            act.activation(hb[:, 1, :], hb[:, 1, :], ACT.Exp).then_inc(sem("dt_exp"), 1)
            act.wait_ge(sem("dt_one"), 1)
            act.activation(dv[:, 4], dv[:, 3], ACT.Ln).then_inc(sem("dt_ln"), 1)
            act.wait_ge(sem("dec_mm"), 1)
            act.activation(dec[:, :, :, :].rearrange("p n t h -> p (n t h)"), ps[:, 6, 0:240], ACT.Exp).then_inc(
                sem("dec_ready"), 1)
            for t in range(TILES):
                act.wait_ge(sem("xs_turned"), t + 1)
                act.activation(xs[:, t, :], ps[:, t % 2, :], ACT.Copy).then_inc(sem("xs_out"), 1)
            for d in range(2):
                act.wait_ge(sem("h0_turned"), d + 1)
                act.activation(state[d][:, 0 if d == 0 else 3, :], ps[:, d, :], ACT.Copy).then_inc(sem("h0_ready"), 1)
            for d in range(2):
                act.wait_ge(sem("hf_turned"), d + 1)
                act.activation(mt[:, d, 0:4, :].rearrange("p m n -> p (m n)"), ps[:, 2 + d, :], ACT.Copy).then_inc(
                    sem("hf_copied"), 1)
            act.wait_ge(sem("hf_stored"), 32)
            for t in range(TILES):
                for d in range(2):
                    n = 2 * t + d
                    act.wait_ge(sem("seg_mm"), n + 1)
                    if t:
                        act.wait_ge(sem("y_mm"), t)
                    act.activation(mt[:, d, :, :].rearrange("p h s -> p (h s)"),
                                   ps[:, 1:3, :].rearrange("p b s -> p (b s)"), ACT.Exp).then_inc(sem("seg_exp"), 1)
            act.wait_ge(sem("y_done"), TILES)
            for t in range(TILES):
                for g in range(SSM_G):
                    act.activation(ps[:, t, g * 256:(g + 1) * 256], xs[:, t, g * 256:(g + 1) * 256],
                                   ACT.Square, accum_out=st2[:, 0, 2 * t + g:2 * t + g + 1]).then_inc(
                        sem("y_squares"), 1)
            act.wait_ge(sem("y_squares"), 2 * TILES)
            act.activation(st2[:, 1, :], st2[:, 0, :], ACT.Sqrt, scale=1.0 / 256, bias=cx.eps[:, :]).then_inc(
                sem("y_rms"), 1)
            for m in range(4):
                act.wait_ge(sem("ossm_turned"), m + 1)
                act.activation(cx.oT[:, m, CTX:TOK], ps[:, m % 2, :], ACT.Copy, scale=nrm[:, m:m + 1]).then_inc(
                    sem("ossm_lat"), 1)

        @block.vector
        def _(dve):
            step = cx.vlink
            dve.memset(xp[:, :, 0:2], 0.0)
            dve.memset(xp[:, :, 2 + CTX:4 + CTX], 0.0)
            step(dve, dve.memset(xp[:, :, XPW - 2:XPW], 0.0))
            dve.wait_ge(sem("cols_turned"), 1)
            dve.tensor_copy(cols[:, :], ps[:, 7, 0:52]).then_inc(sem("cols_ready"), 1)
            dve.wait_ge(sem("cols_ready"), 1)

            def ctx_out(m):
                dve.wait_ge(sem("xb_mm"), m + 1)
                dve.tensor_copy(xp[:, m % 4, 2:2 + CTX], ps[:, 2 + m % 2, 0:P]).then_inc(sem("xb_ctx_out"), 1)

            for m in range(8):
                ctx_out(m)
                dve.wait_ge(sem("xb_ctx_out"), m + 1)
                dve.wait_ge(sem("xb_lat_out"), m + 1)
                o = cv[:, m, 2:XPW - 2]
                n = XPW - 4
                step(dve, dve.tensor_scalar(o, xp[:, m % 4, 0:n], cols[:, m:m + 1], cols[:, 40 + m:41 + m],
                                            ALU.mult, ALU.add))
                for j in range(1, CONV_W):
                    ins = dve.scalar_tensor_tensor(out=o, in0=xp[:, m % 4, j:j + n], scalar=cols[:, 8 * j + m:8 * j + m + 1], in1=o,
                                                   op0=ALU.mult, op1=ALU.add)
                    if j < CONV_W - 1:
                        step(dve, ins)
                ins.then_inc(sem("conv_done"), 1)
            dve.wait_ge(sem("ssm_small"), 64)
            dve.wait_ge(sem("dt_mm"), 1)
            dve.tensor_tensor(dv[:, 0], ps[:, 6, 0:80].rearrange("p (t h) -> p t h", h=16),
                              spread(hb[:, 0, :], 1, TILES), ALU.add).then_inc(sem("dt_read"), 1)
            dve.wait_ge(sem("dt_read"), 1)
            step(dve, dve.tensor_scalar(dv[:, 1], dv[:, 0], -1.0, None, ALU.mult))
            dve.tensor_tensor(dv[:, 1], dv[:, 1], dv[:, 0], ALU.max).then_inc(sem("dt_abs"), 1)
            dve.wait_ge(sem("dt_exp"), 1)
            dve.tensor_scalar(dv[:, 3], dv[:, 2], 1.0, None, ALU.add).then_inc(sem("dt_one"), 1)
            dve.wait_ge(sem("dt_one"), 1)
            step(dve, dve.tensor_scalar(dv[:, 5], dv[:, 3], -1.0, 1.0e-30, ALU.add, ALU.max))
            step(dve, dve.reciprocal(dv[:, 6], dv[:, 5]))
            step(dve, dve.tensor_tensor(dv[:, 5], dv[:, 6], dv[:, 2], ALU.mult))
            dve.wait_ge(sem("dt_ln"), 1)
            step(dve, dve.tensor_tensor(dv[:, 5], dv[:, 5], dv[:, 4], ALU.mult))
            step(dve, dve.tensor_scalar(dv[:, 6], dv[:, 2], -0.5, 1.0, ALU.mult, ALU.add))
            step(dve, dve.tensor_tensor(dv[:, 6], dv[:, 6], dv[:, 2], ALU.mult))
            step(dve, dve.tensor_tensor(dv[:, 5], dv[:, 5], dv[:, 6], ALU.max))
            step(dve, dve.tensor_scalar(dv[:, 1], dv[:, 0], 0.0, None, ALU.max))
            step(dve, dve.tensor_tensor(dt, dv[:, 5], dv[:, 1], ALU.add))
            step(dve, dve.tensor_scalar(dv[:, 3], dt, -1.0, None, ALU.mult))
            dve.tensor_tensor(a, dv[:, 3], spread(hb[:, 1, :], 1, TILES), ALU.mult).then_inc(sem("a_ready"), 1)
            for t in range(TILES):
                dve.wait_ge(sem("xs_turned"), t + 1)
                dve.tensor_copy(bt[:, t, :], ps[:, 2 + t % 2, 0:256]).then_inc(sem("b_out"), 1)

            def by_head(ap):
                return ap.rearrange("p (h q) -> p h q", h=SSM_H)

            def x_dt(t, d):
                return dve.tensor_tensor(by_head(xdt[:, d, :]), by_head(xs[:, t, :]),
                                         spread(dt[:, t, d * 8:(d + 1) * 8], 2, SSM_P), ALU.mult)

            dve.wait_ge(sem("dec_ready"), 1)
            dve.wait_ge(sem("xs_out"), TILES)
            dve.wait_ge(sem("h0_ready"), 2)
            for n, (d, t, slot) in enumerate([(0, 0, 0), (1, 0, 0)] + steps):
                step(dve, x_dt(t, d))
                if n:
                    dve.wait_ge(sem("ds_mm"), n)
                dve.tensor_tensor(by_head(xdd[:, :]), by_head(xdt[:, d, :]), spread(dec[:, 2 + d, t, :], 2, SSM_P),
                                  ALU.mult).then_inc(sem("xdd_ready"), 1)
                dve.wait_ge(sem("ds_mm"), n + 1)
                if n < 2:
                    if n:
                        dve.wait_ge(sem("hf_turned"), 1)
                    dve.tensor_copy(tmp[:, :], ps[:, 4 + n % 2, :]).then_inc(sem("ds_used"), 1)
                else:
                    old = state[d][:, t - 1, :]
                    new = state[d][:, slot, :]
                    if n == 2:
                        dve.wait_ge(sem("hf_turned"), 2)
                    elif n > 3:
                        dve.wait_ge(sem("ds_used"), n - 1)
                    step(dve, dve.tensor_tensor(by_head(tmp[:, :]), by_head(old), spread(dec[:, 4 + d, t, :], 2, SSM_P),
                                                ALU.mult))
                    dve.tensor_tensor(new, ps[:, 4 + n % 2, :], tmp[:, :], ALU.add).then_inc(sem("ds_used"), 1)
            dve.wait_ge(sem("h0_turned"), 2)
            for t in range(TILES):
                for d in range(2):
                    n = 2 * t + d
                    if n:
                        dve.wait_ge(sem("seg_mm"), n)
                    dve.tensor_tensor(am[:, :, :], spread(a[:, t, d * 8:(d + 1) * 8], 2, P), spread((LE, GE)[d], 1, 8),
                                      ALU.mult).then_inc(sem("am_ready"), 1)
                if t:
                    dve.wait_ge(sem("y_mm"), t)
                for d in range(2):
                    step(dve, x_dt(t, d))
                dve.wait_ge(sem("cb_mm"), t + 1)
                for d in range(2):
                    ins = dve.tensor_tensor(cbm[:, d, :, :], ps[:, 0, 0:256].rearrange("p (g l) -> p g l", g=2),
                                            spread((LE, GE)[d], 1, 2), ALU.mult)
                    if d == 0:
                        step(dve, ins)
                ins.then_inc(sem("cb_out"), 1)
                dve.wait_ge(sem("cb_out"), t + 1)
                for d in range(2):
                    dve.wait_ge(sem("seg_exp"), 2 * t + d + 1)
                    m4 = mt[:, d, :, :].rearrange("p (g h) s -> p g h s", g=2)
                    dve.tensor_tensor(m4, m4, spread(cbm[:, d, :, :], 2, 4), ALU.mult).then_inc(sem("mt_ready"), 1)
                y = xs[:, t, :]
                step(dve, dve.tensor_tensor(by_head(y), by_head(y), spread(hb[:, 2, 0:8], 2, SSM_P), ALU.mult))
                dve.wait_ge(sem("y_mm"), t + 1)
                step(dve, dve.tensor_tensor(y, ps[:, 3, :], y, ALU.add))
                if t:
                    dve.wait_ge(sem("yoff_mm"), t)
                    for d in range(2):
                        step(dve, dve.tensor_tensor(by_head(tmp[:, :]), by_head(ps[:, 4 + d, :]),
                                                    spread(dec[:, d, t, :], 2, SSM_P), ALU.mult))
                        step(dve, dve.tensor_tensor(y, y, tmp[:, :], ALU.add))
                dve.tensor_tensor(y, y, sz[:, t, :], ALU.mult).then_inc(sem("y_done"), 1)
            dve.wait_ge(sem("y_rms"), 1)
            step(dve, dve.reciprocal(st2[:, 2, :], st2[:, 1, :]))
            for t in range(TILES):
                for g in range(SSM_G):
                    y = xs[:, t, g * 256:(g + 1) * 256]
                    ins = dve.tensor_scalar(y, y, st2[:, 2, 2 * t + g:2 * t + g + 1], None, ALU.mult)
            ins.then_inc(sem("y_normed"), 1)
            for m in range(4):
                dve.wait_ge(sem("ossm_turned"), m + 1)
                dve.tensor_scalar(cx.oT[:, m, 0:CTX], ps[:, 6 + m % 2, 0:P], nrm[:, m:m + 1], None, ALU.mult).then_inc(
                    sem("ossm_ctx"), 1)



def stage_mix(nc, cx, L, n, branch, g0):
    sem = cx.sem
    ps = cx.ps
    with ExitStack() as st:
        gate = st.enter_context(nc.sbuf_tensor(f"mix_gate{n}", [P, 2, TOK], F32))
        prod = st.enter_context(nc.sbuf_tensor(f"mix_prod{n}", [P, 2, TOK], F32))
        block = st.enter_context(nc.Block())

        @block.sync
        def _(sp):
            load_behind(cx, sp, L, ("gate", g0), ("gate", g0 + 1))

        @block.tensor
        def _(pe):
            for m in range(KT):
                u = n * KT + m
                b = 4 * (m % 2)
                if m >= 2:
                    pe.wait_ge(sem("mix_gated"), u - 1)
                wg = section_ready(cx, pe, ("gate", g0 + m // 4)).rearrange("p (k n) -> p k n", k=KT)
                wb = section_ready(cx, pe, ("br", branch)).rearrange("p (k n) -> p k n", k=4)
                project_fm(cx, pe, wb, slice(m * P, (m + 1) * P), ps[:, b, :], ps[:, b + 1, 0:P], cx.oT, 4)
                c = slice((m % 4) * P, (m % 4 + 1) * P)
                project_fm(cx, pe, wg, c, ps[:, b + 2, :], ps[:, b + 3, 0:P]).then_inc(sem("mix_mm"), 1)
                if m % 4 == 3:
                    pe.wait_ge(sem("mix_mm"), u + 1)
                    for _i in range(1 + m // 4):
                        pe.sem_inc(cx.ring_free, 1)

        @block.scalar
        def _(act):
            for m in range(KT):
                u = n * KT + m
                b = 4 * (m % 2)
                act.wait_ge(sem("mix_mm"), u + 1)
                if m >= 2:
                    act.wait_ge(sem("mix_gated"), u - 1)
                act.activation(gate[:, m % 2, CTX:TOK], ps[:, b + 2, :], ACT.Sigmoid)
                act.activation(gate[:, m % 2, 0:CTX], ps[:, b + 3, 0:P], ACT.Sigmoid).then_inc(sem("mix_sig"), 1)

        @block.vector
        def _(dve):
            for m in range(KT):
                u = n * KT + m
                b = 4 * (m % 2)
                dve.wait_ge(sem("mix_sig"), u + 1)
                to = cx.mixT[:, m, :] if n == 0 else prod[:, m % 2, :]
                dve.tensor_tensor(to[:, CTX:TOK], ps[:, b, :], gate[:, m % 2, CTX:TOK], ALU.mult)
                dve.tensor_tensor(to[:, 0:CTX], ps[:, b + 1, 0:P], gate[:, m % 2, 0:CTX], ALU.mult).then_inc(
                    sem("mix_gated"), 1)
                if n:
                    dve.wait_ge(sem("mix_gated"), u + 1)
                    dve.tensor_tensor(cx.mixT[:, m, :], cx.mixT[:, m, :], to, ALU.add)



def stage_da(nc, cx, L):
    w = cx.w
    sem = cx.sem
    ps = cx.ps
    KW = TOK + PAST
    units = [(t, h) for t in range(TILES) for h in range(DA_H)]
    with ExitStack() as st:
        def sb(name, shape):
            return st.enter_context(nc.sbuf_tensor(name, shape, F32))
        qT = sb("da_qT", [P, DA_H, TOK])
        kT = sb("da_kT", [P, DA_H, KW])
        v = sb("da_v", [P, TILES + 1, 512])
        stage = sb("da_stage", [P, DA_H, P])
        rope = sb("da_rope", [P, 2, LAT])
        rt = sb("da_rt", [P, 2, LAT])
        e = sb("da_e", [P, 2, 2, PAST + LAT])
        aT = sb("da_aT", [P, 5, P])
        o = sb("da_o", [P, TILES, 512])
        sub = sb("da_sub", [P, P])
        lam = sb("da_lam", [P, 4, DA_HD])
        lk = sb("da_lk", [P, 2])
        ls = sb("da_ls", [P, 8])
        nmx = sb("da_nmx", [P, 2, 2])
        sm = sb("da_sm", [P, 2, 2])
        rc = sb("da_rc", [P, 2, 2])
        ss = sb("da_ss", [P, 3, 20])
        block = st.enter_context(nc.Block())

        @block.sync
        def _(sp):
            sp.dma_start(stage[:, :, :], w["cache_da_k"].rearrange("o l h n t d -> (o l) h n (t d)")[
                bass.ds(L, 1)].rearrange("o h n d -> n (o h) d")).then_inc(sem("da_cache_k"), 16)
            sp.dma_start(v[:, 1, :].rearrange("p (h d) -> p h d", h=DA_H),
                         w["cache_da_v"].rearrange("o l h n d -> (o l) h n d")[bass.ds(L, 1)].rearrange(
                             "o h n d -> n (o h) d")).then_inc(sem("da_cache_v"), 16)
            sp.dma_start(rope[:, :, :].rearrange("p a b -> p (a b)"), w["k_rope"]).then_inc(sem("da_small"), 16)
            sp.dma_start(sub[:, :], w["da_subln"][bass.ds(L, 1)].broadcast_to([P, P])).then_inc(sem("da_small"), 16)
            sp.dma_start(lam[:, :, :].rearrange("p a b -> p (a b)"),
                         w["da_lambda"].rearrange("l a b -> l (a b)")[bass.ds(L, 1)].broadcast_to(
                             [P, 4 * DA_HD])).then_inc(sem("da_small"), 16)
            sp.dma_start(lk[:, :], w["k_lam"][bass.ds(L, 1)].rearrange("o p n -> (o p) n")).then_inc(
                sem("da_small"), 16)
            load_behind(cx, sp, L, ("in", "dq"), ("in", "dv"))
            sp.wait_ge(sem("da_k_staged"), 1)
            sp.dma_start(cx.new_da_k.rearrange("o l h n t d -> (o l) h n (t d)")[bass.ds(L, 1)].rearrange(
                "o h n d -> n (o h) d"), stage[:, :, :]).then_inc(sem("da_stored"), 16)
            sp.wait_ge(sem("da_v_out"), 1)
            sp.dma_start(cx.new_da_v.rearrange("o l h n d -> (o l) h n d")[bass.ds(L, 1)].rearrange(
                "o h n d -> n (o h) d"), v[:, 0, :].rearrange("p (h d) -> p h d", h=DA_H)).then_inc(
                sem("da_stored"), 16)
            sp.wait_ge(sem("da_stored"), 32)

        def s_banks(n):
            return 2 * (n % 3)

        @block.tensor
        def _(pe):
            for n in range(8):
                q, m = n < 4, n % 4
                wide = section_ready(cx, pe, ("in", "dq" if q else "dk")).rearrange("p (k n) -> p k n", k=KT)
                if n >= 2:
                    pe.wait_ge(sem("da_lat_out"), n - 1)
                    pe.wait_ge(sem("da_ctx_out"), n - 1)
                c = slice(m * P, (m + 1) * P)
                project_fm(cx, pe, wide, c, ps[:, n % 2, :], ps[:, 2 + n % 2, 0:P]).then_inc(sem("da_mm"), 1)
                if m == 3:
                    pe.wait_ge(sem("da_mm"), n + 1)
                    pe.sem_inc(cx.ring_free, 1)
                if n >= 2:
                    src = (qT if n - 2 < 4 else kT)[:, (n - 2) % 4, -LAT:]
                    if n >= 4:
                        pe.wait_ge(sem("da_sin"), n - 3)
                    pe.matmul(ps[:, 4 + n % 2, :], cx.rot, src, start=True, stop=True).then_inc(sem("da_rot"), 1)
            wide = section_ready(cx, pe, ("in", "dv")).rearrange("p (k n) -> p k n", k=KT)
            for t in range(TILES):
                if t >= 2:
                    pe.wait_ge(sem("da_v_out"), t - 1)
                project_tm(cx, pe, wide, t, ps[:, 6 + t % 2, :]).then_inc(sem("da_v_mm"), 1)
                if t < 2:
                    n = 8 + t
                    pe.wait_ge(sem("da_lat_out"), n - 1)
                    pe.wait_ge(sem("da_sin"), n - 3)
                    pe.matmul(ps[:, 4 + n % 2, :], cx.rot, kT[:, n - 6, -LAT:], start=True, stop=True).then_inc(
                        sem("da_rot"), 1)
            pe.wait_ge(sem("da_v_mm"), TILES)
            pe.sem_inc(cx.ring_free, 1)
            pe.wait_ge(sem("da_cache_k"), 16)
            pe.wait_ge(sem("da_ctx_out"), 8)
            pe.wait_ge(sem("da_lat_out"), 8)
            for h in range(DA_H):
                ins = pe.transpose(ps[:, 0, h * P:(h + 1) * P], stage[:, h, :], cx.ident)
            ins.then_inc(sem("da_kc_turned"), 1)
            for h in range(DA_H):
                ins = pe.transpose(ps[:, 1, h * P:(h + 1) * P], kT[:, h, 0:CTX], cx.ident)
            ins.then_inc(sem("da_kc_turned"), 1)
            pe.wait_ge(sem("da_kc_out"), 1)
            pe.wait_ge(sem("da_k_staged"), 1)
            pe.wait_ge(sem("da_roped"), 8)
            pe.wait_ge(sem("da_v_out"), TILES)

            def scores(u, m):
                t, h = units[u]
                n = 2 * u + m
                if n >= 3:
                    pe.wait_ge(sem("da_exp"), n - 2)
                b = s_banks(n)
                rows = slice(64 * m, 64 * m + 64)
                lhs = qT[rows, h, tok(t)]
                if t == 0:
                    ins = pe.matmul(ps[:, b, 0:CTX], lhs, kT[rows, h, 0:CTX], start=True, stop=True)
                else:
                    for x in range(2):
                        ins = pe.matmul(ps[:, b + x, 0:320], lhs, kT[rows, h, CTX + 320 * x:CTX + 320 * (x + 1)],
                                        start=True, stop=True)
                ins.then_inc(sem("da_scores"), 1)

            def turn(u):
                pe.wait_ge(sem("da_a_ready"), u + 1)
                if u:
                    pe.wait_ge(sem("da_o_out"), u)
                keys = 1 if units[u][0] == 0 else 5
                for c in range(keys):
                    out = ps[:, 7, 0:P] if c == 0 else ps[:, 6, (c - 1) * P:c * P]
                    ins = pe.transpose(out, e[:, u % 2, 0, c * P:(c + 1) * P], cx.ident)
                ins.then_inc(sem("da_turned"), 1)

            def values(u):
                t, h = units[u]
                pe.wait_ge(sem("da_aT_out"), u + 1)
                keys = 1 if t == 0 else 5
                for c in range(keys):
                    ins = pe.matmul(ps[:, 7, 256:384], aT[:, c, :], v[:, c + (t > 0), h * P:(h + 1) * P],
                                    start=(c == 0), stop=(c == keys - 1))
                ins.then_inc(sem("da_o_mm"), 1)

            pe.wait_ge(sem("da_cache_v"), 16)
            scores(0, 0)
            scores(0, 1)
            scores(1, 0)
            for u in range(len(units)):
                if u + 1 < len(units):
                    scores(u + 1, 1)
                turn(u)
                if u + 2 < len(units):
                    scores(u + 2, 0)
                values(u)
            pe.wait_ge(sem("da_normed"), 1)
            for h in range(DA_H):
                if h >= 2:
                    pe.wait_ge(sem("oda_lat"), h - 1)
                    pe.wait_ge(sem("oda_ctx"), h - 1)
                for t in range(TILES):
                    out = ps[:, 2 + h % 2, 0:P] if t == 0 else ps[:, h % 2, tok(t - 1)]
                    ins = pe.transpose(out, o[:, t, h * P:(h + 1) * P], cx.ident)
                ins.then_inc(sem("oda_turned"), 1)

        @block.scalar
        def _(act):
            for n in range(8):
                act.wait_ge(sem("da_mm"), n + 1)
                dst = qT if n < 4 else kT
                act.activation(dst[:, n % 4, -LAT:], ps[:, n % 2, :], ACT.Copy,
                               scale=DA_HD ** -0.5 if n < 4 else 1.0).then_inc(sem("da_lat_out"), 1)
            act.wait_ge(sem("da_small"), 64)
            act.wait_ge(sem("da_lam_sums"), 1)
            act.activation(ls[:, 2:4], ls[:, 0:2], ACT.Exp).then_inc(sem("da_lam_exp"), 1)
            for t in range(TILES):
                act.wait_ge(sem("da_v_mm"), t + 1)
                act.activation(v[:, t if t == 0 else t + 1, :], ps[:, 6 + t % 2, :], ACT.Copy).then_inc(
                    sem("da_v_out"), 1)
            act.wait_ge(sem("da_kc_turned"), 2)
            act.activation(kT[:, :, CTX:CTX + PAST], ps[:, 0, :].rearrange("p (h n) -> p h n", h=DA_H),
                           ACT.Copy).then_inc(sem("da_kc_out"), 1)

            def evacuate(u):
                act.wait_ge(sem("da_turned"), u + 1)
                if u:
                    act.wait_ge(sem("da_o_mm"), u)
                if units[u][0]:
                    act.activation(aT[:, 1:5, :].rearrange("p c q -> p (c q)"), ps[:, 6, :], ACT.Copy)
                act.activation(aT[:, 0, :], ps[:, 7, 0:P], ACT.Copy).then_inc(sem("da_aT_out"), 1)

            def exps(u, m):
                t = units[u][0]
                n = 2 * u + m
                if u >= 2:
                    act.wait_ge(sem("da_turned"), u - 1)
                act.wait_ge(sem("da_max"), n + 1)
                b = s_banks(n)
                if t == 0:
                    src, dst = ps[:, b, 0:CTX], e[:, u % 2, m, 0:CTX]
                else:
                    src = ps[:, b:b + 2, 0:320]
                    dst = e[:, u % 2, m, :].rearrange("p (x k) -> p x k", x=2)
                act.activation(dst, src, ACT.Exp, bias=nmx[:, u % 2, m:m + 1],
                               accum_out=sm[:, u % 2, m:m + 1]).then_inc(sem("da_exp"), 1)

            exps(0, 0)
            exps(0, 1)
            for u in range(len(units)):
                if u + 1 < len(units):
                    exps(u + 1, 0)
                evacuate(u)
                if u + 1 < len(units):
                    exps(u + 1, 1)
            act.wait_ge(sem("da_o_out"), len(units))
            for t in range(TILES):
                for h in range(DA_H):
                    act.activation(ps[:, t, h * P:(h + 1) * P], o[:, t, h * P:(h + 1) * P], ACT.Square,
                                   accum_out=ss[:, 0, t * 4 + h:t * 4 + h + 1]).then_inc(sem("da_squares"), 1)
            act.wait_ge(sem("da_squares"), 20)
            act.activation(ss[:, 1, :], ss[:, 0, :], ACT.Sqrt, scale=1.0 / (2 * DA_HD), bias=cx.eps[:, :]).then_inc(
                sem("da_rms"), 1)
            for h in range(DA_H):
                act.wait_ge(sem("oda_turned"), h + 1)
                act.activation(cx.oT[:, h, CTX:TOK], ps[:, h % 2, :], ACT.Copy).then_inc(sem("oda_lat"), 1)

        @block.vector
        def _(dve):
            step = cx.vlink

            def rope_chunk(n):
                x = (qT if n < 4 else kT)[:, n % 4, -LAT:]
                dve.wait_ge(sem("da_rot"), n + 1)
                r = rt[:, n % 2, :]
                dve.tensor_tensor(r, ps[:, 4 + n % 2, :], rope[:, 1, :], ALU.mult).then_inc(sem("da_sin"), 1)
                step(dve, dve.tensor_tensor(x, x, rope[:, 0, :], ALU.mult))
                dve.tensor_tensor(x, x, r, ALU.add).then_inc(sem("da_roped"), 1)

            dve.wait_ge(sem("da_small"), 64)
            step(dve, dve.tensor_tensor(lam[:, 0:4:2, :], lam[:, 0:4:2, :], lam[:, 1:4:2, :], ALU.mult))
            dve.tensor_reduce(ls[:, 0:2], lam[:, 0:4:2, :], AX.X, ALU.add).then_inc(sem("da_lam_sums"), 1)
            for n in range(8):
                dve.wait_ge(sem("da_mm"), n + 1)
                dve.tensor_scalar((qT if n < 4 else kT)[:, n % 4, 0:CTX], ps[:, 2 + n % 2, 0:P],
                                  DA_HD ** -0.5 if n < 4 else 1.0, None, ALU.mult).then_inc(sem("da_ctx_out"), 1)
                if n >= 2:
                    rope_chunk(n - 2)
            rope_chunk(6)
            rope_chunk(7)
            dve.wait_ge(sem("da_lam_exp"), 1)
            step(dve, dve.tensor_tensor(ls[:, 4:5], ls[:, 3:4], ls[:, 2:3], ALU.subtract))
            step(dve, dve.tensor_tensor(ls[:, 5:6], ls[:, 4:5], lk[:, 0:1], ALU.subtract))
            step(dve, dve.tensor_scalar(sub[:, :], sub[:, :], lk[:, 1:2], None, ALU.mult))
            dve.wait_ge(sem("da_kc_turned"), 2)
            dve.tensor_copy(stage[:, :, :].rearrange("p h d -> p (h d)"), ps[:, 1, :]).then_inc(
                sem("da_k_staged"), 1)

            def maxima(u, m):
                n = 2 * u + m
                dve.wait_ge(sem("da_scores"), n + 1)
                b = s_banks(n)
                if n >= 4:
                    dve.wait_ge(sem("da_exp"), n - 3)
                src = ps[:, b, 0:CTX] if units[u][0] == 0 else ps[:, b:b + 2, 0:320]
                dve.tensor_reduce(nmx[:, u % 2, m:m + 1], src, AX.X if units[u][0] == 0 else AX.XY, ALU.max,
                                  negate=True).then_inc(sem("da_max"), 1)

            def combine(u):
                keys = CTX if units[u][0] == 0 else PAST + LAT
                dve.wait_ge(sem("da_exp"), 2 * u + 2)
                step(dve, dve.reciprocal(rc[:, u % 2, :], sm[:, u % 2, :]))
                e0, e1 = e[:, u % 2, 0, 0:keys], e[:, u % 2, 1, 0:keys]
                step(dve, dve.tensor_scalar(e1, e1, rc[:, u % 2, 1:2], ls[:, 5:6], ALU.mult, ALU.mult))
                dve.scalar_tensor_tensor(out=e0, in0=e0, scalar=rc[:, u % 2, 0:1], in1=e1, op0=ALU.mult,
                                         op1=ALU.add).then_inc(sem("da_a_ready"), 1)

            def take(u):
                t, h = units[u]
                dve.wait_ge(sem("da_o_mm"), u + 1)
                dve.tensor_copy(o[:, t, h * P:(h + 1) * P], ps[:, 7, 256:384]).then_inc(sem("da_o_out"), 1)

            maxima(0, 0)
            maxima(0, 1)
            maxima(1, 0)
            for u in range(len(units)):
                if u + 1 < len(units):
                    maxima(u + 1, 1)
                combine(u)
                if u + 2 < len(units):
                    maxima(u + 2, 0)
                take(u)
            dve.wait_ge(sem("da_rms"), 1)
            step(dve, dve.reciprocal(ss[:, 2, :], ss[:, 1, :]))
            for t in range(TILES):
                for h in range(DA_H):
                    x = o[:, t, h * P:(h + 1) * P]
                    ins = dve.scalar_tensor_tensor(out=x, in0=x, scalar=ss[:, 2, t * 4 + h:t * 4 + h + 1],
                                                   in1=sub[:, :], op0=ALU.mult, op1=ALU.mult)
            ins.then_inc(sem("da_normed"), 1)
            for h in range(DA_H):
                dve.wait_ge(sem("oda_turned"), h + 1)
                dve.tensor_copy(cx.oT[:, h, 0:CTX], ps[:, 2 + h % 2, 0:P]).then_inc(sem("oda_ctx"), 1)



def stage_na(nc, cx, L):
    w = cx.w
    sem = cx.sem
    ps = cx.ps
    KW = TOK + PAST
    ALLK = NKEY + PAST
    units = [(b, h) for b in range(1 + NBLK) for h in range(NA_H)]
    with ExitStack() as st:
        def sb(name, shape):
            return st.enter_context(nc.sbuf_tensor(name, shape, F32))
        qT = sb("na_qT", [P, 4, TOK])
        kT = sb("na_kT", [P, 4, KW])
        v0 = sb("na_v0", [P, 2, 512])
        vl = sb("na_vl", [P, 2, 512])
        vg = sb("na_vg", [P, NBLK, 2, 512])
        raw = sb("na_raw", [P, 4, NKEY])
        mask = sb("na_mask", [P, NBLK, NKEY])
        bias = sb("na_bias", [P, 2, ALLK])
        pr = sb("na_pr", [P, 2, ALLK])
        pT = sb("na_pT", [P, 2, 3, P])
        o = sb("na_o", [P, 2, 512])
        stage = sb("na_stage", [P, NA_H, NA_HD])
        mx = sb("na_mx", [P, 4])
        nmx = sb("na_nmx", [P, 4])
        sm = sb("na_sm", [P, 2, NA_H])
        rc = sb("na_rc", [P, 2, NA_H])
        block = st.enter_context(nc.Block())

        def grid(ap):
            return ap.rearrange("p (r c) -> p r c", c=GRID_W)

        @block.sync
        def _(sp):
            sp.dma_start(stage[:, :, :], w["cache_na_k"].rearrange("o l h n d -> (o l) h n d")[
                bass.ds(L, 1)].rearrange("o h n d -> n (o h) d")).then_inc(sem("na_cache_k"), 16)
            sp.dma_start(v0[:, 1, :].rearrange("p (h d) -> p h d", h=NA_H),
                         w["cache_na_v"].rearrange("o l h n d -> (o l) h n d")[bass.ds(L, 1)].rearrange(
                             "o h n d -> n (o h) d")).then_inc(sem("na_cache_v"), 16)
            sp.dma_start(mask[:, :, :].rearrange("p a b -> p (a b)"), w["k_mask"]).then_inc(sem("na_mask"), 16)
            load_behind(cx, sp, L, ("in", "nq"), ("in", "nv"))
            for t in range(1, TILES):
                sp.wait_ge(sem("na_v_out"), t + 1)
                sp.dma_start(cx.v_scratch[tok(t - 1), :], vl[:, t % 2, :]).then_inc(sem(f"na_v_dumped{t % 2}"), 16)
            sp.wait_ge(sem("na_v_dumped0"), 32)
            sp.wait_ge(sem("na_v_dumped1"), 32)
            for j in range(NBLK):
                for half in range(2):
                    rows = cx.v_scratch.rearrange("(r c) d -> r c d", c=GRID_W)
                    sp.dma_start(vg[:, j, half, :], rows[4 * half:4 * half + 4, col0(j):col0(j) + WCOLS, :]).then_inc(
                        sem("na_gathered"), 16)
            sp.wait_ge(sem("na_k_staged"), 1)
            sp.dma_start(cx.new_na_k.rearrange("o l h n d -> (o l) h n d")[bass.ds(L, 1)].rearrange(
                "o h n d -> n (o h) d"), stage[:, :, :]).then_inc(sem("na_stored"), 16)
            sp.dma_start(cx.new_na_v.rearrange("o l h n d -> (o l) h n d")[bass.ds(L, 1)].rearrange(
                "o h n d -> n (o h) d"), v0[:, 0, :].rearrange("p (h d) -> p h d", h=NA_H)).then_inc(
                sem("na_stored"), 16)
            for n, (b, h) in enumerate(units[NA_H:]):
                if n >= 4:
                    sp.wait_ge(sem("na_bias_ready"), n - 3)
                at = h * RPB_ROW + RPB_FRONT + col0(b - 1) - QB_C * (b - 1)
                src = bass.AP(tensor=cx.rpb_scratch.tensor, offset=L * (NA_H * RPB_ROW) + at,
                              ap=[[WCOLS, ROWS], [1, QB_C], [1, NKEY]])
                sp.dma_start(raw[:, n % 4, :], src).then_inc(sem(f"na_raw{n % 4}"), 16)
            sp.wait_ge(sem("na_stored"), 32)

        @block.tensor
        def _(pe):
            for n in range(8):
                q, m = n < 4, n % 4
                wide = section_ready(cx, pe, ("in", "nq" if q else "nk")).rearrange("p (k n) -> p k n", k=KT)
                if n >= 2:
                    pe.wait_ge(sem("na_lat_out"), n - 1)
                    pe.wait_ge(sem("na_ctx_out"), n - 1)
                c = slice(m * P, (m + 1) * P)
                project_fm(cx, pe, wide, c, ps[:, n % 2, :], ps[:, 2 + n % 2, 0:P]).then_inc(sem("na_mm"), 1)
                if m == 3:
                    pe.wait_ge(sem("na_mm"), n + 1)
                    pe.sem_inc(cx.ring_free, 1)
            wide = section_ready(cx, pe, ("in", "nv")).rearrange("p (k n) -> p k n", k=KT)
            for t in range(TILES):
                if t >= 2:
                    pe.wait_ge(sem("na_v_out"), t - 1)
                project_tm(cx, pe, wide, t, ps[:, 6 + t % 2, :]).then_inc(sem("na_v_mm"), 1)
            pe.wait_ge(sem("na_v_mm"), TILES)
            pe.sem_inc(cx.ring_free, 1)
            pe.wait_ge(sem("na_cache_k"), 16)
            pe.wait_ge(sem("na_lat_out"), 8)
            pe.wait_ge(sem("na_ctx_out"), 8)
            for c in range(4):
                ins = pe.transpose(ps[:, 0, c * P:(c + 1) * P],
                                   stage[:, 2 * c:2 * c + 2, :].rearrange("p h d -> p (h d)"), cx.ident)
            ins.then_inc(sem("na_kc_turned"), 1)
            for c in range(4):
                ins = pe.transpose(ps[:, 1, c * P:(c + 1) * P], kT[:, c, 0:CTX], cx.ident)
            ins.then_inc(sem("na_kc_turned"), 1)
            pe.wait_ge(sem("na_kc_out"), 1)
            pe.wait_ge(sem("na_k_staged"), 1)
            pe.wait_ge(sem("na_v_out"), TILES)
            pe.wait_ge(sem("na_cache_v"), 16)

            def scores(u):
                b, h = units[u]
                if u >= 3:
                    if units[u - 3][0] == 0:
                        pe.wait_ge(sem("na_exp"), u - 2)
                    else:
                        pe.wait_ge(sem("na_s_read"), u - 2 - NA_H)
                rows, c = slice(64 * (h % 2), 64 * (h % 2) + 64), h // 2
                if b == 0:
                    ins = pe.matmul(ps[:, u % 3, 0:CTX], qT[rows, c, 0:CTX], kT[rows, c, 0:CTX], start=True, stop=True)
                else:
                    j = b - 1
                    q = qT[rows, c, tok(b)]
                    k = grid(kT[rows, c, CTX + PAST:KW])[:, :, col0(j):col0(j) + WCOLS]
                    pe.matmul(ps[:, u % 3, 0:NKEY], q, k, start=True, stop=True)
                    ins = pe.matmul(ps[:, u % 3, NKEY:ALLK], q, kT[rows, c, CTX:CTX + PAST], start=True, stop=True)
                ins.then_inc(sem("na_scores"), 1)

            def turn(u):
                pe.wait_ge(sem("na_exp"), u + 1)
                if u >= 2:
                    pe.wait_ge(sem("na_pT_out"), u - 1)
                for c in range(1 if units[u][0] == 0 else 3):
                    ins = pe.transpose(ps[:, 3 + u % 2, c * P:(c + 1) * P], pr[:, u % 2, c * P:(c + 1) * P], cx.ident)
                ins.then_inc(sem("na_turned"), 1)

            def values(u):
                b, h = units[u]
                pe.wait_ge(sem("na_pT_out"), u + 1)
                if h == 0 and b >= 2:
                    pe.wait_ge(sem("na_o_out"), b - 1)
                out = ps[:, 5 + b % 2, h * 64:(h + 1) * 64]
                c = slice(h * 64, (h + 1) * 64)
                if b == 0:
                    ins = pe.matmul(out, pT[:, u % 2, 0, :], v0[:, 0, c], start=True, stop=True)
                else:
                    if b == 1 and h == 0:
                        pe.wait_ge(sem("na_gathered"), 16 * 2 * NBLK)
                    for x in range(2):
                        pe.matmul(out, pT[:, u % 2, x, :], vg[:, b - 1, x, c], start=(x == 0), stop=False)
                    ins = pe.matmul(out, pT[:, u % 2, 2, :], v0[:, 1, c], start=False, stop=True)
                ins.then_inc(sem("na_o_mm"), 1)

            def output(b):
                pe.wait_ge(sem("na_o_out"), b + 1)
                if b:
                    pe.wait_ge(sem("ona_out"), b)
                for c in range(4):
                    ins = pe.transpose(ps[:, 7, c * P:(c + 1) * P], o[:, b % 2, c * P:(c + 1) * P], cx.ident)
                ins.then_inc(sem("ona_turned"), 1)

            scores(0)
            scores(1)
            for u in range(len(units)):
                if u + 2 < len(units):
                    scores(u + 2)
                turn(u)
                if u:
                    values(u - 1)
                if u % NA_H == 2 and u > NA_H:
                    output(u // NA_H - 1)
            values(len(units) - 1)
            output(NBLK)

        @block.scalar
        def _(act):
            for n in range(8):
                act.wait_ge(sem("na_mm"), n + 1)
                if n < 4:
                    act.activation(reverse(qT[:, n, CTX:TOK].rearrange("p (j r c) -> p r j c", j=NBLK, r=ROWS), 1, 3),
                                   ps[:, n % 2, :].rearrange("p (r j c) -> p r j c", j=NBLK, r=ROWS), ACT.Copy,
                                   scale=NA_HD ** -0.5).then_inc(sem("na_lat_out"), 1)
                else:
                    act.activation(kT[:, n - 4, -LAT:], ps[:, n % 2, :], ACT.Copy).then_inc(sem("na_lat_out"), 1)
            for t in range(TILES):
                act.wait_ge(sem("na_v_mm"), t + 1)
                if t >= 3:
                    act.wait_ge(sem(f"na_v_dumped{t % 2}"), 16)
                dst = v0[:, 0, :] if t == 0 else vl[:, t % 2, :]
                act.activation(dst, ps[:, 6 + t % 2, :], ACT.Copy).then_inc(sem("na_v_out"), 1)
            act.wait_ge(sem("na_kc_turned"), 2)
            act.activation(kT[:, :, CTX:CTX + PAST], ps[:, 0, :].rearrange("p (h n) -> p h n", h=4),
                           ACT.Copy).then_inc(sem("na_kc_out"), 1)

            def evacuate(u):
                act.wait_ge(sem("na_turned"), u + 1)
                if u >= 2:
                    act.wait_ge(sem("na_o_mm"), u - 1)
                c = 1 if units[u][0] == 0 else 3
                act.activation(pT[:, u % 2, 0:c, :].rearrange("p c q -> p (c q)"), ps[:, 3 + u % 2, 0:c * P],
                               ACT.Copy).then_inc(sem("na_pT_out"), 1)

            for u, (b, h) in enumerate(units):
                act.wait_ge(sem("na_max"), u + 1)
                if u >= 2:
                    act.wait_ge(sem("na_turned"), u - 1)
                if b == 0:
                    act.activation(pr[:, u % 2, 0:CTX], ps[:, u % 3, 0:CTX], ACT.Exp, bias=nmx[:, u % 4:u % 4 + 1],
                                   accum_out=sm[:, b % 2, h:h + 1]).then_inc(sem("na_exp"), 1)
                else:
                    if h == 0 and b >= 2:
                        act.wait_ge(sem("na_o_out"), b - 1)
                    act.activation(pr[:, u % 2, :], pr[:, u % 2, :], ACT.Exp, bias=nmx[:, u % 4:u % 4 + 1],
                                   accum_out=sm[:, b % 2, h:h + 1]).then_inc(sem("na_exp"), 1)
                if u:
                    evacuate(u - 1)
            evacuate(len(units) - 1)

        @block.vector
        def _(dve):
            step = cx.vlink
            for x in range(2):
                ins = dve.memset(bias[:, x, NKEY:ALLK], 0.0)
            step(dve, ins)
            for n in range(8):
                dve.wait_ge(sem("na_mm"), n + 1)
                dve.tensor_scalar((qT if n < 4 else kT)[:, n % 4, 0:CTX], ps[:, 2 + n % 2, 0:P],
                                  NA_HD ** -0.5 if n < 4 else 1.0, None, ALU.mult).then_inc(sem("na_ctx_out"), 1)
            dve.wait_ge(sem("na_kc_turned"), 2)
            dve.tensor_copy(stage[:, :, :].rearrange("p h d -> p (h d)"), ps[:, 1, :]).then_inc(
                sem("na_k_staged"), 1)
            dve.wait_ge(sem("na_mask"), 16)

            def maxima(u):
                b, h = units[u]
                dve.wait_ge(sem("na_scores"), u + 1)
                if u >= 4:
                    dve.wait_ge(sem("na_exp"), u - 3)
                if b == 0:
                    dve.tensor_reduce(nmx[:, u % 4:u % 4 + 1], ps[:, u % 3, 0:CTX], AX.X, ALU.max,
                                      negate=True).then_inc(sem("na_max"), 1)
                    return
                n = u - NA_H
                dve.wait_ge(sem(f"na_raw{n % 4}"), 16 * (n // 4 + 1))
                dve.tensor_tensor(bias[:, u % 2, 0:NKEY], raw[:, n % 4, :], mask[:, b - 1, :], ALU.add).then_inc(
                    sem("na_bias_ready"), 1)
                dve.wait_ge(sem("na_bias_ready"), n + 1)
                if u >= 2:
                    dve.wait_ge(sem("na_turned"), u - 1)
                dve.tensor_tensor_reduce(out=pr[:, u % 2, :], in0=ps[:, u % 3, 0:ALLK], in1=bias[:, u % 2, :],
                                         scale=1.0, scalar=-3.0e38, op0=ALU.add, op1=ALU.max,
                                         accum_out=mx[:, u % 4:u % 4 + 1]).then_inc(sem("na_s_read"), 1)
                dve.wait_ge(sem("na_s_read"), n + 1)
                dve.tensor_scalar(nmx[:, u % 4:u % 4 + 1], mx[:, u % 4:u % 4 + 1], -1.0, None, ALU.mult).then_inc(
                    sem("na_max"), 1)

            def take(b):
                step(dve, dve.reciprocal(rc[:, b % 2, :], sm[:, b % 2, :]))
                if b >= 2:
                    dve.wait_ge(sem("ona_turned"), b - 1)
                dve.tensor_tensor(o[:, b % 2, :].rearrange("p (h d) -> p h d", h=NA_H),
                                  ps[:, 5 + b % 2, :].rearrange("p (h d) -> p h d", h=NA_H),
                                  spread(rc[:, b % 2, :], 2, NA_HD), ALU.mult).then_inc(sem("na_o_out"), 1)

            def spill(b):
                dve.wait_ge(sem("ona_turned"), b + 1)
                src = ps[:, 7, :].rearrange("p (c q) -> p c q", c=4)
                for c in range(4):
                    if b == 0:
                        dst, s = cx.oT[:, c, 0:CTX], src[:, c, :]
                    else:
                        dst = grid(cx.oT[:, c, CTX:TOK])[:, :, QB_C * (b - 1):QB_C * b]
                        s = reverse(src[:, c, :].rearrange("p (r q) -> p r q", r=ROWS), 1, 2)
                    ins = dve.tensor_copy(dst, s)
                ins.then_inc(sem("ona_out"), 1)

            for u, (b, h) in enumerate(units):
                maxima(u)
                if u >= NA_H and h == 2:
                    dve.wait_ge(sem("na_o_mm"), b * NA_H)
                    dve.wait_ge(sem("na_exp"), b * NA_H)
                    take(b - 1)
                if u >= NA_H and h == 5:
                    spill(b - 1)
            dve.wait_ge(sem("na_o_mm"), len(units))
            dve.wait_ge(sem("na_exp"), len(units))
            take(NBLK)
            spill(NBLK)



def stage_out(nc, cx, L, x):
    w = cx.w
    sem = cx.sem
    ps = cx.ps
    with ExitStack() as st:
        xn = st.enter_context(nc.sbuf_tensor("out_xn", [P, TILES, D], F32))
        ms = st.enter_context(nc.sbuf_tensor("out_ms", [P, 3, TILES], F32))
        block = st.enter_context(nc.Block())

        @block.sync
        def _(sp):
            sp.dma_start(x[:, 0, :], cx.y_prompt.rearrange("o n d -> (o n) d")).then_inc(sem("x_again"), 16)
            sp.dma_start(x[:, 1:TILES, :], cx.y_sample.rearrange("o (t p) d -> p (o t) d", p=P)).then_inc(
                sem("x_again"), 16)
            load_behind(cx, sp, L, ("out", 0), ("out", 1))

        @block.tensor
        def _(pe):
            wide = [section_ready(cx, pe, ("out", n)).rearrange("p (k n) -> p k n", k=KT) for n in range(2)]
            for t in range(TILES):
                if t >= 4:
                    pe.wait_ge(sem("mixed_out"), t - 3)
                for n in range(2):
                    for k in range(KT):
                        ins = pe.matmul(ps[:, 2 * (t % 4) + n, :], cx.mixT[:, k, tok(t)], wide[n][:, k, :],
                                        start=(k == 0), stop=(k == KT - 1))
                ins.then_inc(sem("mixed_mm"), 1)
            pe.wait_ge(sem("mixed_mm"), TILES)
            pe.sem_inc(cx.ring_free, 1)
            pe.sem_inc(cx.ring_free, 1)
            pe.wait_ge(sem("mixed_out"), TILES)
            norm_tensor(cx, pe, 1, xn)

        @block.scalar
        def _(act):
            for t in range(TILES):
                act.wait_ge(sem("mixed_mm"), t + 1)
                b = 2 * (t % 4)
                act.activation(xn[:, t, :].rearrange("p (b n) -> p b n", b=2), ps[:, b:b + 2, :], ACT.Square,
                               accum_out=ms[:, 0, t:t + 1]).then_inc(sem("mixed_sq"), 1)
                act.wait_ge(sem("mixed_sq"), t + 1)
                act.activation(ms[:, 1, t:t + 1], ms[:, 0, t:t + 1], ACT.Sqrt, scale=1.0 / D,
                               bias=cx.eps[:, :]).then_inc(sem("mixed_rms"), 1)
            act.wait_ge(sem("x1_ready"), TILES)
            norm_scalar(cx, act, 1, x, xn)
            modulate_scalar(cx, act, 1)

        @block.vector
        def _(dve):
            step = cx.vlink
            dve.wait_ge(sem("x_again"), 32)
            for t in range(TILES):
                dve.wait_ge(sem("mixed_rms"), t + 1)
                b = 2 * (t % 4)
                step(dve, dve.reciprocal(ms[:, 2, t:t + 1], ms[:, 1, t:t + 1]))
                dve.scalar_tensor_tensor(out=xn[:, t, :].rearrange("p (b n) -> p b n", b=2), in0=ps[:, b:b + 2, :],
                                         scalar=ms[:, 2, t:t + 1],
                                         in1=cx.gate_post[:, 0, min(t, 1), :].rearrange("p (b n) -> p b n", b=2),
                                         op0=ALU.mult, op1=ALU.mult).then_inc(sem("mixed_out"), 1)
                dve.wait_ge(sem("mixed_out"), t + 1)
                dve.tensor_tensor(x[:, t, :], x[:, t, :], xn[:, t, :], ALU.add).then_inc(sem("x1_ready"), 1)
            norm_vector(cx, dve, 1, x, xn)
            modulate_vector(cx, dve, 1)



def stage_moe(nc, cx, L, x):
    w = cx.w
    sem = cx.sem
    ps = cx.ps
    S0 = FIRST_EXPERT % SLOTS
    assert S0 == 2 and SLOTS == 4
    with ExitStack() as st:
        def sb(name, shape):
            return st.enter_context(nc.sbuf_tensor(name, shape, F32))
        acc = sb("moe_acc", [P, TILES, D])
        act_g = sb("moe_silu", [P, TOK])
        hid = sb("moe_hid", [P, 2, TOK])
        hsh = sb("moe_hsh", [P, 2, TOK])
        gates = sb("moe_gates", [P, TILES, NE])
        wr = sb("moe_wr", [P, KT, NE])
        br = sb("moe_br", [P, NE])
        s = sb("moe_s", [P, TILES, NE])
        sbias = sb("moe_sb", [P, TILES, NE])
        gt = sb("moe_gt", [P, NE])
        eq = sb("moe_eq", [P, NE])
        pf = sb("moe_pf", [P, NE])
        top = sb("moe_top", [P, 8])
        rs = sb("moe_rs", [P, 4])
        fs = sb("moe_fs", [P, 3, TILES])
        block = st.enter_context(nc.Block())
        LOOPS = NE // SLOTS - 1

        @block.sync
        def _(sp):
            sp.dma_start(wr[:, :, :], w["w_router"][bass.ds(L, 1)].rearrange("l (p k) n -> p (l k) n", k=KT)).then_inc(
                sem("router_in"), 16)
            sp.dma_start(br[:, :], w["b_router"][bass.ds(L, 1)].broadcast_to([P, NE])).then_inc(sem("router_in"), 16)
            for e in range(2, SLOTS):
                load_section(cx, sp, L, FIRST_EXPERT + e)
            with sp.Fori(1, NE // SLOTS) as i:
                for u in range(SLOTS):
                    sp.wait_ge(cx.ring_free, i * SLOTS + (FIRST_EXPERT + u - SLOTS + 1))
                    load_expert(cx, sp, L * NE + i * SLOTS + u, (S0 + u) % SLOTS)
            for t in range(TILES):
                sp.wait_ge(sem("x2_ready"), t + 1)
                dst = cx.y_prompt[0] if t == 0 else cx.y_sample[0, tok(t - 1), :]
                sp.dma_start(dst, x[:, t, :]).then_inc(sem("x_stored"), 16)
            sp.wait_ge(sem("x_stored"), 16 * TILES)

        @block.tensor
        def _(pe):
            pe.wait_ge(sem("router_in"), 32)
            for t in range(TILES):
                for k in range(KT):
                    ins = pe.matmul(ps[:, 7, t * NE:(t + 1) * NE], cx.hT[:, k, tok(t)], wr[:, k, :], start=(k == 0),
                                    stop=(k == KT - 1))
            ins.then_inc(sem("router_mm"), 1)

            def up(n, gate_w, up_w, i=0):
                if n:
                    pe.wait_ge(sem("hid_ready"), i * SLOTS + n)
                for g, ws in enumerate((gate_w, up_w)):
                    ins = project_fm(cx, pe, ws, slice(0, P), ps[:, g, :], ps[:, 2, g * P:(g + 1) * P])
                ins.then_inc(sem("up_mm"), 1)

            def expert_up(slot, n, i=0):
                ring = cx.ring[:, slot, :]
                up(n, ring[:, 0:D].rearrange("p (k f) -> p k f", k=KT),
                   ring[:, D:2 * D].rearrange("p (k f) -> p k f", k=KT), i)

            def down(n, hs, ws, i=0):
                for t in range(TILES):
                    if n * TILES + t >= 2:
                        pe.wait_ge(sem("down_out"), i * (SLOTS * TILES) + (n * TILES + t - 1))
                    bank = 3 + 2 * ((n * TILES + t) % 2)
                    for x in range(2):
                        for c, (h, wd) in enumerate(zip(hs, ws)):
                            ins = pe.matmul(ps[:, bank + x, :], h[:, tok(t)], wd[:, x * SEC:(x + 1) * SEC],
                                            start=(c == 0), stop=(c == len(hs) - 1))
                    ins.then_inc(sem("down_mm"), 1)

            sh = section_ready(cx, pe, ("shared_up", 0)).rearrange("p (k n) -> p k n", k=KT)
            for c in range(2):
                up(c, sh[:, :, c * P:(c + 1) * P], sh[:, :, SFF + c * P:SFF + (c + 1) * P])
            pe.wait_ge(sem("up_mm"), 2)
            pe.sem_inc(cx.ring_free, 1)
            pe.wait_ge(cx.ring_full[S0], full_count(FIRST_EXPERT))
            expert_up(S0, 2)
            sd = section_ready(cx, pe, ("shared_down", 0))
            pe.wait_ge(sem("hid_ready"), 2)
            down(0, [hsh[:, 0, :], hsh[:, 1, :]], [sd[:, 0:D], sd[:, D:2 * D]])
            pe.wait_ge(sem("down_mm"), TILES)
            pe.sem_inc(cx.ring_free, 1)

            def expert(u, i=0, more=True):
                if more:
                    nx = FIRST_EXPERT + u + 1
                    pe.wait_ge(cx.ring_full[nx % SLOTS], i * 48 + full_count(nx))
                    expert_up(nx % SLOTS, u + 3, i)
                pe.wait_ge(sem("hid_ready"), i * SLOTS + (u + 3))
                slot = (S0 + u) % SLOTS
                down(u + 1, [hid[:, u % 2, :]], [cx.ring[:, slot, 2 * D:3 * D]], i)
                pe.wait_ge(sem("down_mm"), i * (SLOTS * TILES) + (u + 2) * TILES)
                pe.sem_inc(cx.ring_free, 1)

            with pe.Fori(0, LOOPS) as i:
                for u in range(SLOTS):
                    expert(u, i)
            for u in range(SLOTS):
                expert(SLOTS * LOOPS + u, 0, more=u < SLOTS - 1)

        def silu_up(act, n, i=0):
            act.wait_ge(sem("up_mm"), i * SLOTS + (n + 1))
            if n:
                act.wait_ge(sem("hid_ready"), i * SLOTS + n)
            act.activation(act_g[:, CTX:TOK], ps[:, 0, :], ACT.Silu)
            act.activation(act_g[:, 0:CTX], ps[:, 2, 0:P], ACT.Silu).then_inc(sem("silu_ready"), 1)

        @block.scalar
        def _(act):
            act.wait_ge(sem("router_mm"), 1)
            act.activation(s[:, :, :].rearrange("p t e -> p (t e)"), ps[:, 7, 0:TILES * NE], ACT.Sigmoid).then_inc(
                sem("router_s"), 1)
            for n in range(3):
                silu_up(act, n)
            with act.Fori(0, LOOPS) as i:
                for u in range(SLOTS):
                    silu_up(act, u + 3, i)
            for u in range(SLOTS - 1):
                silu_up(act, SLOTS * LOOPS + u + 3)
            for t in range(TILES):
                act.wait_ge(sem("down_out"), (NE * TILES) + t + 1)
                act.activation(cx.hT[:, :, :].rearrange("p k n -> p (k n)")[:, t * D:(t + 1) * D], acc[:, t, :], ACT.Square,
                               accum_out=fs[:, 0, t:t + 1]).then_inc(sem("moe_sq"), 1)
            act.wait_ge(sem("moe_sq"), TILES)
            act.activation(fs[:, 1, :], fs[:, 0, :], ACT.Sqrt, scale=1.0 / D, bias=cx.eps[:, :]).then_inc(
                sem("moe_rms"), 1)

        @block.vector
        def _(dve):
            step = cx.vlink

            def hidden(n, out, i=0):
                dve.wait_ge(sem("silu_ready"), i * SLOTS + (n + 1))
                dve.tensor_tensor(out[:, CTX:TOK], ps[:, 1, :], act_g[:, CTX:TOK], ALU.mult)
                dve.tensor_tensor(out[:, 0:CTX], ps[:, 2, P:2 * P], act_g[:, 0:CTX], ALU.mult).then_inc(
                    sem("hid_ready"), 1)

            hidden(0, hsh[:, 0, :])
            hidden(1, hsh[:, 1, :])
            hidden(2, hid[:, 0, :])
            for t in range(TILES):
                dve.wait_ge(sem("down_mm"), t + 1)
                bank = 3 + 2 * (t % 2)
                dve.tensor_copy(acc[:, t, :].rearrange("p (b n) -> p b n", b=2), ps[:, bank:bank + 2, :]).then_inc(
                    sem("down_out"), 1)

            dve.wait_ge(sem("router_s"), 1)
            dve.wait_ge(sem("router_in"), 32)
            step(dve, dve.tensor_tensor(sbias[:, :, :], s[:, :, :], spread(br[:, :], 1, TILES), ALU.add))
            for t in range(TILES):
                v = sbias[:, t, :]
                step(dve, dve.max(top[:, :], v))
                thr = top[:, TOP_K - 1:TOP_K]
                step(dve, dve.tensor_scalar(eq[:, :], v, thr, None, ALU.is_equal))
                step(dve, dve.tensor_scalar(gt[:, :], v, thr, None, ALU.is_gt))
                step(dve, dve.tensor_reduce(rs[:, 0:1], gt[:, :], AX.X, ALU.add))
                step(dve, dve.tensor_scalar(rs[:, 1:2], rs[:, 0:1], -1.0, float(TOP_K), ALU.mult, ALU.add))
                step(dve, dve.tensor_tensor_scan(pf[:, :], cx.ones[:, 0:NE], eq[:, :], 0.0, ALU.mult, ALU.add))
                step(dve, dve.tensor_scalar(pf[:, :], pf[:, :], rs[:, 1:2], None, ALU.is_le))
                step(dve, dve.tensor_tensor(eq[:, :], eq[:, :], pf[:, :], ALU.mult))
                step(dve, dve.tensor_tensor(gt[:, :], gt[:, :], eq[:, :], ALU.add))
                step(dve, dve.tensor_tensor(gt[:, :], gt[:, :], s[:, t, :], ALU.mult))
                step(dve, dve.tensor_reduce(rs[:, 2:3], gt[:, :], AX.X, ALU.add))
                step(dve, dve.reciprocal(rs[:, 3:4], rs[:, 2:3]))
                step(dve, dve.tensor_scalar(gates[:, t, :], gt[:, :], rs[:, 3:4], ROUTE_SCALE, ALU.mult, ALU.mult))
            def expert(u, i=0, more=True, looped=True):
                if more:
                    if u >= 1 or looped:
                        dve.wait_ge(sem("down_mm"), i * (SLOTS * TILES) + (u + 1) * TILES)
                    hidden(u + 3, hid[:, (u + 1) % 2, :], i)
                for t in range(TILES):
                    n = (u + 1) * TILES + t
                    dve.wait_ge(sem("down_mm"), i * (SLOTS * TILES) + n + 1)
                    dve.wait_ge(sem("down_out"), i * (SLOTS * TILES) + (n - TILES + 1))
                    bank = 3 + 2 * (n % 2)
                    a = acc[:, t, :].rearrange("p (b n) -> p b n", b=2)
                    col = gates[:, t, u:u + 1] if not looped else gates[:, t, bass.ds(i * SLOTS + u, 1)]
                    dve.scalar_tensor_tensor(out=a, in0=ps[:, bank:bank + 2, :], scalar=col, in1=a, op0=ALU.mult,
                                             op1=ALU.add).then_inc(sem("down_out"), 1)

            with dve.Fori(0, LOOPS) as i:
                for u in range(SLOTS):
                    expert(u, i)
            for u in range(SLOTS):
                expert(SLOTS * LOOPS + u, 0, more=u < SLOTS - 1, looped=False)
            dve.wait_ge(sem("moe_rms"), 1)
            step(dve, dve.reciprocal(fs[:, 2, :], fs[:, 1, :]))
            for t in range(TILES):
                step(dve, dve.scalar_tensor_tensor(out=acc[:, t, :], in0=acc[:, t, :], scalar=fs[:, 2, t:t + 1],
                                                   in1=cx.gate_post[:, 1, min(t, 1), :], op0=ALU.mult, op1=ALU.mult))
                dve.tensor_tensor(x[:, t, :], x[:, t, :], acc[:, t, :], ALU.add).then_inc(sem("x2_ready"), 1)



def trunk(nc, w, outs):
    cx = Cx()
    cx.w = w
    (cx.y_prompt, cx.y_sample, cx.new_da_k, cx.new_da_v, cx.new_na_k, cx.new_na_v, cx.new_ssm_f,
     cx.new_ssm_b) = outs
    cx.v_scratch = nc.dram_tensor("v_scratch", [LAT, 512], F32, kind="Internal").ap()
    cx.rpb_scratch = nc.dram_tensor("rpb_scratch", [DEPTH * NA_H, RPB_ROW], F32, kind="Internal").ap()
    with ExitStack() as st:
        def sb(name, shape):
            return st.enter_context(nc.sbuf_tensor(name, shape, F32))
        base = sb("base", [P, 7 * P])
        sel = sb("sel", [2, 2, P])
        cx.eps = sb("eps", [P, 1])
        cx.ring = sb("ring", [P, SLOTS, 4096])
        cx.hT = sb("hT", [P, KT, TOK])
        cx.gate_post = sb("gate_post", [P, 2, 2, D])
        cx.mod_scale = sb("mod_scale", [P, 2, KT, 2])
        cx.mod_shift = sb("mod_shift", [P, 2, KT, 2])
        cx.ssq = sb("ssq", [P, 2, TILES])
        cx.rms = sb("rms", [P, 2, TILES])
        cx.rstd = sb("rstd", [P, 2, TILES])
        cx.ps = st.enter_context(nc.psum_tensor("ps", [P, 8, 512], F32))
        cx.ident, cx.rot, cx.le, cx.gt, cx.ge, cx.lt, cx.ones = (base[:, n * P:(n + 1) * P] for n in range(7))
        cx.sel = sel
        sems = {}

        def sem(name):
            if name not in sems:
                sems[name] = st.enter_context(nc.semaphore(name))
            return sems[name]

        cx.sem = sem
        cx.ring_full = [sem(f"ring_full{s}") for s in range(SLOTS)]
        cx.ring_free, cx.squares_ready, cx.rms_ready = sem("ring_free"), sem("squares_ready"), sem("rms_ready")
        cx.xn_ready, cx.xnT_ready, cx.mods_ready = sem("xn_ready"), sem("xnT_ready"), sem("mods_ready")
        cx.h_lat_ready, cx.h_ctx_ready = sem("h_lat_ready"), sem("h_ctx_ready")
        setup = st.enter_context(nc.semaphore("setup"))
        setup_x = st.enter_context(nc.semaphore("setup_x"))
        setup_mem = st.enter_context(nc.semaphore("setup_mem"))
        with ExitStack() as once:
            pad = once.enter_context(nc.sbuf_tensor("rpb_pad", [DEPTH * NA_H, RPB_ROW], F32))
            block = once.enter_context(nc.Block())

            @block.sync
            def _(sp):
                sp.dma_start(base[:, :], w["k_base"]).then_inc(setup, 16)
                sp.dma_start(sel[:, :, :], w["k_sel"]).then_inc(setup, 16)
                sp.dma_start(cx.y_prompt[0], w["x_prompt"][0]).then_inc(setup, 16)
                sp.dma_start(cx.y_sample[0], w["x_sample"][0]).then_inc(setup, 16)
                sp.wait_ge(setup_mem, 2)
                sp.dma_start(pad[:, RPB_FRONT:RPB_FRONT + RPB_R * WCOLS].rearrange("p (r c) -> p r c", c=WCOLS)[
                    :, :, 0:RPB_C], w["na_rpb"].rearrange("l h r c -> (l h) r c")).then_inc(setup_x, 16)
                sp.wait_ge(setup_x, 16)
                sp.dma_start(cx.rpb_scratch, pad[:, :]).then_inc(setup_x, 16)
                sp.wait_ge(setup_x, 32)
                sp.wait_ge(setup, 64)

            @block.vector
            def _(dve):
                dve.memset(pad[:, :], 0.0).then_inc(setup_mem, 1)
                dve.memset(cx.eps[:, :], EPS).then_inc(setup_mem, 1)

        with nc.Fori(0, DEPTH) as L:
            cx.vlink = Link(sem("vector_step"))
            stage_ada(nc, cx, L)
            with ExitStack() as mid:
                cx.oT = mid.enter_context(nc.sbuf_tensor("oT", [P, 4, TOK], F32))
                stage_ssm(nc, cx, L)
                cx.mixT = mid.enter_context(nc.sbuf_tensor("mixT", [P, KT, TOK], F32))
                stage_mix(nc, cx, L, 0, "s", 2)
                stage_da(nc, cx, L)
                stage_mix(nc, cx, L, 1, "a", 0)
                stage_na(nc, cx, L)
                stage_mix(nc, cx, L, 2, "n", 4)
                x = mid.enter_context(nc.sbuf_tensor("x", [P, TILES, D], F32))
                stage_out(nc, cx, L, x)
                stage_moe(nc, cx, L, x)
            for s in sems.values():
                nc.sync.sem_clear(s)
            nc.all_engine_barrier()


_INS = ["x_prompt", "x_sample", "c", "cache_da_k", "cache_da_v", "cache_na_k", "cache_na_v", "state_ssm_f",
        "state_ssm_b", "c_ctx", "w_ada", "b_ada", "g_pre1", "g_post1", "g_pre2", "g_post2", "w_in", "w_gate",
        "da_lambda", "da_subln", "ssm_conv_w", "ssm_conv_b", "ssm_dt_bias", "ssm_a_log", "ssm_d", "ssm_norm",
        "na_rpb", "w_br_da", "w_br_ssm", "w_br_na", "w_out", "w_router", "b_router", "w_e_gate", "w_e_up",
        "w_e_down", "w_s_gate", "w_s_up", "w_s_down"]
_OUTS = [(1, 128, 1024), (1, 512, 1024), (1, 2, 4, 128, 2, 64), (1, 2, 4, 128, 128), (1, 2, 8, 128, 64),
         (1, 2, 8, 128, 64), (1, 2, 8, 64, 128), (1, 2, 8, 64, 128)]


def kernel(**inputs):
    import concourse.bacc as _bacc
    from concourse.bass_utils import run_bass_kernel_spmd as _run

    nc = _bacc.Bacc("TRN2", target_bir_lowering=False, num_devices=1)
    arrays, w = {}, {}
    given = {name: np.ascontiguousarray(inputs[name]) for name in _INS}
    given.update({name: np.ascontiguousarray(a) for name, a in shape_constants().items()})
    for name, a in given.items():
        arrays[f"in_{name}"] = a
        w[name] = nc.dram_tensor(f"in_{name}", a.shape, mybir.dt.from_np(a.dtype), kind="ExternalInput").ap()
    outs = [nc.dram_tensor(f"out_{i}", shape, F32, kind="ExternalOutput").ap() for i, shape in enumerate(_OUTS)]
    trunk(nc, w, outs)
    r = _run(nc, [arrays], core_ids=[0])
    return tuple(r.results[0][f"out_{i}"] for i in range(len(_OUTS)))
```

```python
import math
from contextlib import ExitStack

import concourse.bass as bass
import numpy as np
from concourse import mybir

F32 = mybir.dt.float32
ALU = mybir.AluOpType
ACT = mybir.ActivationFunctionType
AX = mybir.AxisListType

P = 128
D = 1024
KT = D // P
DEPTH = 2
CTX = 128
LAT = 512
TOK = CTX + LAT
TILES = TOK // P
PAST = 128
GRID_W = 64
ROWS = LAT // GRID_W
EPS = 1e-6
DA_H, DA_HD = 4, 64
NA_H, NA_HD = 8, 64
SSM_H, SSM_P, SSM_N, SSM_G = 8, 64, 128, 2
CONV_W = 5
CONV_CH = 1024
WIN_R, WIN_C, QB_C = 8, 16, 16
NBLK = GRID_W // QB_C
WCOLS = 32
NKEY = ROWS * WCOLS
RPB_R, RPB_C = 2 * WIN_R - 1, 2 * WIN_C - 1
RPB_FRONT = 32
RPB_ROW = RPB_FRONT + RPB_R * WCOLS + 32
NE, TOP_K, FF, SFF = 32, 4, 128, 256
ROUTE_SCALE = 2.5
SEC = 512
SLOTS = 4
XPW = TOK + 6
MASKED = -1.0e30

UNROLL = SLOTS
N_CHOICE = TOP_K * TILES
MIN_TURNS = N_CHOICE // UNROLL
MAX_TURNS = -(-((TOK * TOP_K + NE * (P - 1)) // P) // UNROLL)
TABLE = UNROLL * MAX_TURNS + 4

OFF = {}
_at = 0
for _n, _w in (("dq", 512), ("dk", 512), ("dv", 512), ("z", 512), ("xb0", 512), ("xb1", 512), ("dt", 16),
               ("nq", 512), ("nk", 512), ("nv", 512)):
    OFF[_n] = _at
    _at += _w

SECTIONS = [("ada", i) for i in range(12)]
SECTIONS += [("in", n) for n in ("xb0", "xb1", "z")] + [("gate", 2), ("br", "s"), ("gate", 3)]
SECTIONS += [("in", n) for n in ("dq", "dk", "dv")] + [("gate", 0), ("br", "a"), ("gate", 1)]
SECTIONS += [("in", n) for n in ("nq", "nk", "nv")] + [("gate", 4), ("br", "n"), ("gate", 5)]
SECTIONS += [("out", 0), ("out", 1), ("shared_up", 0)]
AT = {s: i for i, s in enumerate(SECTIONS)}


def parts_of(i):
    return 2 if SECTIONS[i][0] == "shared_up" else 1


def full_count(i):
    return 16 * sum(parts_of(j) for j in range(i % SLOTS, i + 1, SLOTS))


def tok(t):
    return slice(t * P, (t + 1) * P)


def col0(j):
    return min(max(QB_C * j - WIN_C // 2, 0), GRID_W - WCOLS)


def shape_constants():
    t = np.arange(P)
    a, b = t[:, None], t[None, :]
    rot = np.zeros((P, P), np.float32)
    for o in range(P):
        if o % 32 < 16:
            rot[o + 16, o] = -1.0
        else:
            rot[o - 16, o] = 1.0
    base = np.concatenate([m.astype(np.float32) for m in
                           (a == b, rot, a <= b, a > b, a >= b, a < b, np.ones((P, P)))], axis=1)
    n_freq = DA_HD // 4
    inv = (np.float32(10000.0) ** (-np.arange(n_freq, dtype=np.float32) / np.float32(n_freq))).astype(np.float32)
    pos = np.arange(LAT)
    ang = np.zeros((P, LAT), np.float32)
    for p in range(P):
        d = p % DA_HD
        at = (pos // GRID_W if d < 32 else pos % GRID_W).astype(np.float32)
        ang[p] = at * inv[d % 16]
    rope = np.concatenate([np.cos(ang), np.sin(ang)], axis=1).astype(np.float32)
    mask = np.zeros((P, NBLK, NKEY), np.float32)
    for q in range(P):
        for j in range(NBLK):
            qc = QB_C * j + QB_C - 1 - q % QB_C
            s = min(max(qc - WIN_C // 2, 0), GRID_W - WIN_C)
            kc = col0(j) + np.arange(NKEY) % WCOLS
            mask[q, j] = np.where((kc >= s) & (kc < s + WIN_C), 0.0, MASKED)
    lam = np.zeros((DEPTH, P, 2), np.float32)
    for layer in range(DEPTH):
        li = 0.8 - 0.6 * math.exp(-0.3 * layer)
        lam[layer, :, 0], lam[layer, :, 1] = li, 1.0 - li
    sel = np.zeros((2, 2, P), np.float32)
    sel[0, 0], sel[1, 1] = 1.0, 1.0
    iota = np.concatenate([np.broadcast_to(b, (P, P)), a + P * np.arange(TILES), a], axis=1).astype(np.float32)
    return {"k_iota": iota, "k_base": base, "k_rope": rope, "k_mask": mask.reshape(P, -1), "k_lam": lam, "k_sel": sel}


class Link:

    def __init__(self, sem):
        self.sem, self.n = sem, 0

    def __call__(self, eng, ins):
        ins.then_inc(self.sem, 1)
        self.n += 1
        eng.wait_ge(self.sem, self.n)


class Cx:
    pass


def spread(ap, axis, n):
    ap = ap.unsqueeze(axis)
    shape = list(ap.shape)
    shape[axis] = n
    return ap.broadcast_to(shape)


def reverse(ap, *axes):
    dims = [list(d) for d in ap.ap]
    offset = ap.offset
    for x in axes:
        offset = offset + dims[x][0] * (dims[x][1] - 1)
        dims[x][0] = -dims[x][0]
    return bass.AP(tensor=ap.tensor, offset=offset, ap=dims)



def load_section(cx, sp, L, i, first=False):
    kind, which = SECTIONS[i]
    s = i % SLOTS
    if i >= SLOTS and not first:
        sp.wait_ge(cx.ring_free, i - SLOTS + 1)
    w = cx.w
    slot = cx.ring[:, s, :]

    def fm(src, a, b, dst):
        sp.dma_start(dst, src[bass.ds(L, 1), :, a:b].rearrange("l (p k) n -> p (l k) n", k=KT)).then_inc(
            cx.ring_full[s], 16)

    wide = slot.rearrange("p (k n) -> p k n", k=KT)
    if kind == "ada":
        fm(w["w_ada"], which * SEC, (which + 1) * SEC, wide)
    elif kind == "in":
        fm(w["w_in"], OFF[which], OFF[which] + SEC, wide)
    elif kind == "gate":
        fm(w["w_gate"], which * SEC, (which + 1) * SEC, wide)
    elif kind == "br":
        src = w[{"a": "w_br_da", "s": "w_br_ssm", "n": "w_br_na"}[which]]
        sp.dma_start(slot.rearrange("p (k n) -> p k n", k=4),
                     src[bass.ds(L, 1)].rearrange("l (k p) n -> p (l k) n", p=P)).then_inc(cx.ring_full[s], 16)
    elif kind == "out":
        sp.dma_start(wide, w["w_out"][bass.ds(L, 1), :, which * SEC:(which + 1) * SEC].rearrange(
            "l (k p) n -> p (l k) n", p=P)).then_inc(cx.ring_full[s], 16)
    elif kind == "shared_up":
        fm(w["w_s_gate"], 0, SFF, wide[:, :, 0:SFF])
        fm(w["w_s_up"], 0, SFF, wide[:, :, SFF:2 * SFF])


def load_behind(cx, sp, L, a, b):
    for i in range(AT[a] + SLOTS, min(AT[b] + SLOTS + 1, len(SECTIONS))):
        load_section(cx, sp, L, i)


def section_ready(cx, pe, key):
    i = AT[key]
    pe.wait_ge(cx.ring_full[i % SLOTS], full_count(i))
    return cx.ring[:, i % SLOTS, :]


def project_fm(cx, pe, wide, c, lat, ctx, hT=None, kt_n=KT):
    hT = cx.hT if hT is None else hT
    for k in range(kt_n):
        pe.matmul(lat, wide[:, k, c], hT[:, k, CTX:TOK], start=(k == 0), stop=(k == kt_n - 1))
    for k in range(kt_n):
        last = pe.matmul(ctx, wide[:, k, c], hT[:, k, 0:CTX], start=(k == 0), stop=(k == kt_n - 1))
    return last


def project_tm(cx, pe, wide, t, out):
    for k in range(KT):
        last = pe.matmul(out, cx.hT[:, k, tok(t)], wide[:, k, :], start=(k == 0), stop=(k == KT - 1))
    return last



def norm_scalar(cx, act, sub, x, xn):
    for t in range(TILES):
        act.activation(xn[:, t, :], x[:, t, :], ACT.Square, accum_out=cx.ssq[:, sub, t:t + 1]).then_inc(
            cx.squares_ready, 1)
    act.wait_ge(cx.squares_ready, (sub + 1) * TILES)
    act.activation(cx.rms[:, sub, :], cx.ssq[:, sub, :], ACT.Sqrt, scale=1.0 / D, bias=cx.eps[:, :]).then_inc(
        cx.rms_ready, 1)


def norm_vector(cx, dve, sub, x, xn):
    dve.wait_ge(cx.rms_ready, sub + 1)
    cx.vlink(dve, dve.reciprocal(cx.rstd[:, sub, :], cx.rms[:, sub, :]))
    for t in range(TILES):
        dve.tensor_scalar(xn[:, t, :], x[:, t, :], cx.rstd[:, sub, t:t + 1], None, ALU.mult).then_inc(
            cx.xn_ready, 1)


def norm_tensor(cx, pe, sub, xn):
    pe.wait_ge(cx.xn_ready, (sub + 1) * TILES)
    for k in range(KT):
        n = sub * KT + k
        if k >= 4:
            pe.wait_ge(cx.h_lat_ready, n - 3)
            pe.wait_ge(cx.h_ctx_ready, n - 3)
        for t in range(TILES):
            out = cx.ps[:, 4 + k % 4, 0:P] if t == 0 else cx.ps[:, k % 4, tok(t - 1)]
            ins = pe.transpose(out, xn[:, t, k:D:KT], cx.ident)
        ins.then_inc(cx.xnT_ready, 1)


def modulate_scalar(cx, act, sub):
    act.wait_ge(cx.mods_ready, 1)
    for k in range(KT):
        act.wait_ge(cx.xnT_ready, sub * KT + k + 1)
        act.activation(cx.hT[:, k, CTX:TOK], cx.ps[:, k % 4, :], ACT.Identity, scale=cx.mod_scale[:, sub, k, 1:2],
                       bias=cx.mod_shift[:, sub, k, 1:2]).then_inc(cx.h_lat_ready, 1)


def modulate_vector(cx, dve, sub):
    for k in range(KT):
        dve.wait_ge(cx.xnT_ready, sub * KT + k + 1)
        dve.tensor_scalar(cx.hT[:, k, 0:CTX], cx.ps[:, 4 + k % 4, 0:P], cx.mod_scale[:, sub, k, 0:1],
                          cx.mod_shift[:, sub, k, 0:1], ALU.mult, ALU.add).then_inc(cx.h_ctx_ready, 1)



def stage_ada(nc, cx, L):
    w = cx.w
    with ExitStack() as st:
        def sb(name, shape):
            return st.enter_context(nc.sbuf_tensor(name, shape, F32))
        x = sb("ada_x", [P, TILES, D])
        xn = sb("ada_xn", [P, TILES, D])
        csT = sb("ada_csT", [P, 2, KT])
        mods = sb("ada_mods", [2, 6 * D])
        gpre = sb("ada_gpre", [P, 2, KT])
        gpost = sb("ada_gpost", [P, 2, D])
        sem = cx.sem
        block = st.enter_context(nc.Block())

        @block.sync
        def _(sp):
            sp.dma_start(csT[:, 0, :], w["c_ctx"].rearrange("(p k) -> p k", k=KT)).then_inc(sem("ada_small"), 16)
            sp.dma_start(csT[:, 1, :], w["c"].rearrange("o (p k) -> (o p) k", k=KT)).then_inc(sem("ada_small"), 16)
            for i in range(SLOTS):
                load_section(cx, sp, L, i, first=True)
            b = w["b_ada"][bass.ds(L, 1), :]
            for g in range(2):
                sp.dma_start(mods[g:g + 1, :], b).then_inc(sem("ada_bias"), 16)
            sp.dma_start(x[:, 0, :], cx.y_prompt.rearrange("o n d -> (o n) d")).then_inc(sem("x_loaded"), 16)
            sp.dma_start(x[:, 1:TILES, :], cx.y_sample.rearrange("o (t p) d -> p (o t) d", p=P)).then_inc(
                sem("x_loaded"), 16)
            for n, (pre, post) in enumerate((("g_pre1", "g_post1"), ("g_pre2", "g_post2"))):
                sp.dma_start(gpre[:, n, :], w[pre][bass.ds(L, 1)].rearrange("o (p k) -> (o p) k", k=KT)).then_inc(
                    sem("ada_gains"), 16)
                sp.dma_start(gpost[:, n, :], w[post][bass.ds(L, 1)].broadcast_to([P, D])).then_inc(
                    sem("ada_gains"), 16)
            with sp.Fori(1, 3) as i:
                for s in range(SLOTS):
                    sp.wait_ge(cx.ring_free, i * SLOTS + (s + 1 - SLOTS))
                    sp.dma_start(cx.ring[:, s, :].rearrange("p (k n) -> p k n", k=KT),
                                 w["w_ada"].rearrange("l (p k) (c n) -> l p k c n", k=KT, n=SEC)[
                                     bass.ds(L, 1), :, :, bass.ds(i * SLOTS + s, 1), :].rearrange(
                                     "l p k c n -> p (l k) (c n)")).then_inc(cx.ring_full[s], 16)
            for i in range(12, 16):
                load_section(cx, sp, L, i)

        @block.scalar
        def _(act):
            act.wait_ge(sem("ada_small"), 32)
            act.activation(csT[:, :, :], csT[:, :, :], ACT.Silu).then_inc(sem("c_silu"), 1)
            act.wait_ge(sem("x_loaded"), 32)
            norm_scalar(cx, act, 0, x, xn)
            modulate_scalar(cx, act, 0)

        @block.vector
        def _(dve):
            dve.wait_ge(sem("ada_bias"), 32)
            with dve.Fori(0, 3) as i:
                for s in range(SLOTS):
                    dve.wait_ge(sem("ada_mm"), i * SLOTS + (s + 1))
                    m = mods[:, bass.ds((i * SLOTS + s) * SEC, SEC)]
                    dve.tensor_tensor(m, cx.ps[0:2, s, :], m, ALU.add).then_inc(sem("ada_out"), 1)
            norm_vector(cx, dve, 0, x, xn)
            dve.wait_ge(sem("ada_turned"), 1)
            dve.wait_ge(sem("ada_gains"), 64)
            tp = cx.ps[:, 4, 0:64].rearrange("p (s k g) -> p s k g", s=4, k=KT)
            for sub in range(2):
                dve.tensor_copy(cx.mod_shift[:, sub, :, :], tp[:, 2 * sub, :, :])
                ins = dve.scalar_tensor_tensor(out=cx.mod_scale[:, sub, :, :], in0=tp[:, 2 * sub + 1, :, :], scalar=1.0,
                                               in1=spread(gpre[:, sub, :], 2, 2), op0=ALU.add, op1=ALU.mult)
            ins.then_inc(cx.mods_ready, 1)
            for sub in range(2):
                for g in range(2):
                    for h in range(2):
                        dve.wait_ge(sem("gate_rows"), sub * 4 + g * 2 + h + 1)
                        dve.tensor_tensor(cx.gate_post[:, sub, g, h * SEC:(h + 1) * SEC], cx.ps[:, g * 2 + h, :],
                                          gpost[:, sub, h * SEC:(h + 1) * SEC], ALU.mult).then_inc(sem("gate_out"), 1)
            dve.wait_ge(cx.mods_ready, 1)
            modulate_vector(cx, dve, 0)

        @block.tensor
        def _(pe):
            pe.wait_ge(sem("c_silu"), 1)

            def four_sections(i):
                for s in range(SLOTS):
                    pe.wait_ge(cx.ring_full[s], i * 16 + 16)
                    for k in range(KT):
                        ins = pe.matmul(cx.ps[0:2, s, :], csT[:, :, k], cx.ring[:, s, k * SEC:(k + 1) * SEC],
                                        start=(k == 0), stop=(k == KT - 1))
                    ins.then_inc(sem("ada_mm"), 1)
                    pe.wait_ge(sem("ada_mm"), i * SLOTS + (s + 1))
                    pe.sem_inc(cx.ring_free, 1)

            four_sections(0)
            with pe.Fori(1, 3) as i:
                pe.wait_ge(sem("ada_out"), i * SLOTS)
                four_sections(i)
            pe.wait_ge(sem("ada_out"), 12)
            for s, section in enumerate((0, 1, 3, 4)):
                for k in range(KT):
                    c = (s * KT + k) * 2
                    ins = pe.transpose(cx.ps[:, 4, c:c + 2], mods[:, section * D + k:(section + 1) * D:KT],
                                       cx.ident[0:2, 0:2])
            ins.then_inc(sem("ada_turned"), 1)
            for sub, section in enumerate((2, 5)):
                for g in range(2):
                    for h in range(2):
                        if sub:
                            pe.wait_ge(sem("gate_out"), g * 2 + h + 1)
                        a = section * D + h * SEC
                        pe.matmul(cx.ps[:, g * 2 + h, :], cx.sel[:, g, :], mods[:, a:a + SEC], start=True,
                                  stop=True).then_inc(sem("gate_rows"), 1)
            pe.wait_ge(sem("gate_out"), 8)
            pe.wait_ge(cx.mods_ready, 1)
            norm_tensor(cx, pe, 0, xn)



def conv_tile(t):
    a = 2 if t == 0 else 4 + t * P
    return slice(a, a + P)


def stage_ssm(nc, cx, L):
    w = cx.w
    sem = cx.sem
    LE, GT, GE, LT, ONES = cx.le, cx.gt, cx.ge, cx.lt, cx.ones
    with ExitStack() as st:
        def sb(name, shape):
            return st.enter_context(nc.sbuf_tensor(name, shape, F32))
        xp = sb("ssm_xp", [P, 4, XPW])
        cv = sb("ssm_cv", [P, 8, XPW])
        sz = sb("ssm_sz", [P, TILES, 512])
        xs = sb("ssm_xs", [P, TILES, 512])
        bt = sb("ssm_bt", [P, TILES, 256])
        xdt = sb("ssm_xdt", [P, 2, 2, 512])
        xdd = sb("ssm_xdd", [P, 2, 512])
        xco = sb("ssm_xco", [P, 2, TILES, 8])
        am = sb("ssm_am", [P, 8, P])
        mt = sb("ssm_mt", [P, 3, 8, P])
        cbm = sb("ssm_cbm", [P, 2, 2, P])
        tmp = sb("ssm_tmp", [P, 512])
        rows = sb("ssm_rows", [52, P])
        cols = sb("ssm_cols", [P, 52])
        nrm = cols[:, 48:52]
        wdt = sb("ssm_wdt", [P, KT, 16])
        dv = sb("ssm_dv", [P, 8, TILES, 16])
        hb = sb("ssm_hb", [P, 3, 16])
        dec = sb("ssm_dec", [P, 6, TILES, 8])
        st2 = sb("ssm_ss", [P, 3, 2 * TILES])
        dt, a = dv[:, 7], dv[:, 6]
        state = [cv[:, 0:4, :].rearrange("p a b -> p (a b)")[:, 0:2048].rearrange("p (k f) -> p k f", k=4),
                 xp[:, :, :].rearrange("p a b -> p (a b)")[:, 0:2048].rearrange("p (k f) -> p k f", k=4)]
        hin = am[:, 0:4, :]
        ps = cx.ps
        block = st.enter_context(nc.Block())
        steps = [(0, 1, 1), (1, 4, 2), (0, 2, 2), (1, 3, 1), (0, 3, 3), (1, 2, 0)]

        @block.sync
        def _(sp):
            sp.dma_start(rows[0:40, :], w["ssm_conv_w"].rearrange("l j (m p) -> l (j m) p", p=P)[
                bass.ds(L, 1)].rearrange("o r p -> (o r) p")).then_inc(sem("ssm_conv_in"), 16)
            sp.dma_start(rows[40:48, :], w["ssm_conv_b"].rearrange("l (m p) -> l m p", p=P)[
                bass.ds(L, 1)].rearrange("o r p -> (o r) p")).then_inc(sem("ssm_conv_in"), 16)
            sp.dma_start(rows[48:52, :], w["ssm_norm"].rearrange("l (m p) -> l m p", p=P)[
                bass.ds(L, 1)].rearrange("o r p -> (o r) p")).then_inc(sem("ssm_conv_in"), 16)
            sp.dma_start(wdt[:, :, :], w["w_in"][bass.ds(L, 1), :, OFF["dt"]:OFF["dt"] + 16].rearrange(
                "l (p k) n -> p (l k) n", k=KT)).then_inc(sem("ssm_small"), 16)
            sp.dma_start(hb[:, 0, :], w["ssm_dt_bias"].rearrange("l a b -> l (a b)")[bass.ds(L, 1)].broadcast_to(
                [P, 16])).then_inc(sem("ssm_small"), 16)
            sp.dma_start(hb[:, 1, :], w["ssm_a_log"].rearrange("l a b -> l (a b)")[bass.ds(L, 1)].broadcast_to(
                [P, 16])).then_inc(sem("ssm_small"), 16)
            sp.dma_start(hb[:, 2, 0:8], w["ssm_d"][bass.ds(L, 1)].broadcast_to([P, 8])).then_inc(
                sem("ssm_small"), 16)
            load_behind(cx, sp, L, ("in", "xb0"), ("in", "z"))
            for d, name in enumerate(("state_ssm_f", "state_ssm_b")):
                if d:
                    sp.wait_ge(sem("h0_turned"), 1)
                sp.dma_start(hin, w[name].rearrange("o l h p n -> (o l) (h p) n")[bass.ds(L, 1)].rearrange(
                    "o (m q) n -> q (o m) n", q=P)).then_inc(sem("h0_loaded"), 16)
                if d == 0:
                    sp.wait_ge(sem("h0_loaded"), 16)
            for d, out in enumerate((cx.new_ssm_f, cx.new_ssm_b)):
                sp.wait_ge(sem("hf_copied"), d + 1)
                sp.dma_start(out.rearrange("o l h p n -> (o l) (h p) n")[bass.ds(L, 1)].rearrange(
                    "o (m q) n -> q (o m) n", q=P), mt[:, d, 0:4, :]).then_inc(sem("hf_stored"), 16)
            sp.wait_ge(sem("hf_stored"), 32)

        @block.tensor
        def _(pe):
            pe.wait_ge(sem("ssm_conv_in"), 48)
            pe.transpose(ps[:, 7, 0:52], rows[:, :], cx.ident[0:52, 0:52]).then_inc(sem("cols_turned"), 1)
            for m in range(8):
                wide = section_ready(cx, pe, ("in", f"xb{m // 4}")).rearrange("p (k n) -> p k n", k=KT)
                if m >= 2:
                    pe.wait_ge(sem("xb_lat_out"), m - 1)
                    pe.wait_ge(sem("xb_ctx_out"), m - 1)
                c = slice((m % 4) * P, (m % 4 + 1) * P)
                project_fm(cx, pe, wide, c, ps[:, m % 2, :], ps[:, 2 + m % 2, 0:P]).then_inc(sem("xb_mm"), 1)
                if m % 4 == 3:
                    pe.wait_ge(sem("xb_mm"), m + 1)
                    pe.sem_inc(cx.ring_free, 1)
            pe.wait_ge(sem("ssm_small"), 64)
            for t in range(TILES):
                for k in range(KT):
                    ins = pe.matmul(ps[:, 6, t * 16:(t + 1) * 16], cx.hT[:, k, tok(t)], wdt[:, k, :],
                                    start=(k == 0), stop=(k == KT - 1))
            ins.then_inc(sem("dt_mm"), 1)
            wide = section_ready(cx, pe, ("in", "z")).rearrange("p (k n) -> p k n", k=KT)
            for t in range(TILES):
                if t >= 2:
                    pe.wait_ge(sem("z_out"), t - 1)
                project_tm(cx, pe, wide, t, ps[:, 4 + t % 2, :]).then_inc(sem("z_mm"), 1)
            pe.wait_ge(sem("z_mm"), TILES)
            pe.sem_inc(cx.ring_free, 1)
            pe.wait_ge(sem("a_ready"), 1)
            pe.wait_ge(sem("dt_read"), 1)
            for n, (m, d) in enumerate(((LE, 0), (GE, 1), (GT, 0), (LT, 1), (ONES, 0), (ONES, 1))):
                ins = pe.matmul(ps[:, 6, n * 40:(n + 1) * 40].rearrange("p (t h) -> p t h", h=8), m, a[:, :, d * 8:(d + 1) * 8], start=True, stop=True)
            ins.then_inc(sem("dec_mm"), 1)
            pe.wait_ge(sem("xb_silu"), 6)
            pe.wait_ge(sem("xb_lat_out"), 8)
            pe.wait_ge(sem("xb_ctx_out"), 8)
            for t in range(TILES):
                if t >= 2:
                    pe.wait_ge(sem("xs_out"), t - 1)
                    pe.wait_ge(sem("b_out"), t - 1)
                for m in range(4):
                    pe.transpose(ps[:, t % 2, m * P:(m + 1) * P], cv[:, m, conv_tile(t)], cx.ident)
                for m in range(2):
                    ins = pe.transpose(ps[:, 2 + t % 2, m * P:(m + 1) * P], cv[:, 4 + m, conv_tile(t)], cx.ident)
                ins.then_inc(sem("xs_turned"), 1)
            pe.wait_ge(sem("xs_out"), TILES)
            pe.wait_ge(sem("b_out"), TILES)
            for d in range(2):
                pe.wait_ge(sem("h0_loaded"), 16 * (d + 1))
                for m in range(4):
                    ins = pe.transpose(ps[:, d, m * P:(m + 1) * P], hin[:, m, :], cx.ident)
                ins.then_inc(sem("h0_turned"), 1)
            pe.wait_ge(sem("z_out"), TILES)
            for n, (d, t, _) in enumerate([(0, 0, 0), (1, 0, 0)] + steps):
                pe.wait_ge(sem("xdd_ready"), n + 1)
                if n >= 2:
                    pe.wait_ge(sem("ds_used"), n - 1)
                for g in range(SSM_G):
                    ins = pe.matmul(ps[:, 4 + n % 2, g * 256:(g + 1) * 256], bt[:, t, g * P:(g + 1) * P],
                                    xdd[:, n % 2, g * 256:(g + 1) * 256], start=True, stop=True)
                ins.then_inc(sem("ds_mm"), 1)
                if 1 <= n < 3:
                    pe.wait_ge(sem("ds_used"), n)
                    for m in range(4):
                        ins = pe.transpose(ps[:, 1 + n, m * P:(m + 1) * P], tmp[:, m * P:(m + 1) * P], cx.ident)
                    ins.then_inc(sem("hf_turned"), 1)
            pe.wait_ge(sem("h0_ready"), 2)
            pe.wait_ge(sem("hf_copied"), 2)
            pe.wait_ge(sem("ds_used"), 8)
            pe.wait_ge(sem("xb_silu"), 8)

            def segments(n):
                pe.wait_ge(sem("am_ready"), n + 1)
                if n:
                    pe.wait_ge(sem("seg_exp"), n)
                for h in range(2):
                    ins = pe.matmul(ps[:, 1 + h, :], (GT, LT)[n % 2],
                                    am[:, 4 * h:4 * h + 4, :].rearrange("p h s -> p (h s)"), start=True, stop=True)
                ins.then_inc(sem("seg_mm"), 1)

            def within(t):
                pe.wait_ge(sem("mt_ready"), 2 * t + 2)
                pe.wait_ge(sem("xdt_ready"), t + 1)
                if t:
                    pe.wait_ge(sem("y_read"), t)
                for h in range(SSM_H):
                    for d in range(2):
                        ins = pe.matmul(ps[:, 3, h * 64:(h + 1) * 64], mt[:, (2 * t + d) % 3, h, :],
                                        xdt[:, t % 2, d, h * 64:(h + 1) * 64], start=(d == 0), stop=(d == 1))
                ins.then_inc(sem("y_mm"), 1)

            for t in range(TILES):
                if t:
                    pe.wait_ge(sem("cb_out"), t)
                for g in range(SSM_G):
                    ins = pe.matmul(ps[:, 0, g * P:(g + 1) * P], cv[:, 4 + g, conv_tile(t)], cv[:, 6 + g, conv_tile(t)],
                                    start=True, stop=True)
                ins.then_inc(sem("cb_mm"), 1)
                segments(2 * t)
                if t:
                    within(t - 1)
                segments(2 * t + 1)
                if t:
                    pe.wait_ge(sem("y_done"), t)
                    for d in range(2):
                        for g in range(SSM_G):
                            ins = pe.matmul(ps[:, 4 + d, g * 256:(g + 1) * 256], cv[:, 6 + g, conv_tile(t)],
                                            state[d][:, t - 1, g * 256:(g + 1) * 256], start=True, stop=True)
                    ins.then_inc(sem("yoff_mm"), 1)
            within(TILES - 1)
            pe.wait_ge(sem("y_normed"), 1)
            for m in range(4):
                if m >= 2:
                    pe.wait_ge(sem("ossm_lat"), m - 1)
                    pe.wait_ge(sem("ossm_ctx"), m - 1)
                for t in range(TILES):
                    out = ps[:, 6 + m % 2, 0:P] if t == 0 else ps[:, m % 2, tok(t - 1)]
                    ins = pe.transpose(out, xs[:, t, m * P:(m + 1) * P], cx.ident)
                ins.then_inc(sem("ossm_turned"), 1)

        @block.scalar
        def _(act):
            for m in range(8):
                act.wait_ge(sem("xb_mm"), m + 1)
                if m >= 4:
                    act.wait_ge(sem("conv_done"), m - 3)
                act.activation(xp[:, m % 4, 4 + CTX:4 + TOK], ps[:, m % 2, :], ACT.Copy).then_inc(
                    sem("xb_lat_out"), 1)
                if m >= 2:
                    act.wait_ge(sem("conv_done"), m - 1)
                    act.activation(cv[:, m - 2, 2:XPW - 2], cv[:, m - 2, 2:XPW - 2], ACT.Silu).then_inc(
                        sem("xb_silu"), 1)
            for m in range(6, 8):
                act.wait_ge(sem("conv_done"), m + 1)
                act.activation(cv[:, m, 2:XPW - 2], cv[:, m, 2:XPW - 2], ACT.Silu).then_inc(sem("xb_silu"), 1)
            for t in range(TILES):
                act.wait_ge(sem("z_mm"), t + 1)
                act.activation(sz[:, t, :], ps[:, 4 + t % 2, :], ACT.Silu).then_inc(sem("z_out"), 1)
            act.wait_ge(sem("dt_abs"), 1)
            act.wait_ge(sem("ssm_small"), 64)
            act.activation(dv[:, 2], dv[:, 1], ACT.Exp, scale=-1.0)
            act.activation(hb[:, 1, :], hb[:, 1, :], ACT.Exp).then_inc(sem("dt_exp"), 1)
            act.wait_ge(sem("dt_one"), 1)
            act.activation(dv[:, 4], dv[:, 3], ACT.Ln).then_inc(sem("dt_ln"), 1)
            act.wait_ge(sem("dec_mm"), 1)
            act.activation(dec[:, :, :, :].rearrange("p n t h -> p (n t h)"), ps[:, 6, 0:240], ACT.Exp).then_inc(
                sem("dec_ready"), 1)
            for t in range(TILES):
                act.wait_ge(sem("xs_turned"), t + 1)
                act.activation(xs[:, t, :], ps[:, t % 2, :], ACT.Copy).then_inc(sem("xs_out"), 1)
            for d in range(2):
                act.wait_ge(sem("h0_turned"), d + 1)
                act.activation(state[d][:, 0 if d == 0 else 3, :], ps[:, d, :], ACT.Copy).then_inc(sem("h0_ready"), 1)
            for d in range(2):
                act.wait_ge(sem("hf_turned"), d + 1)
                act.activation(mt[:, d, 0:4, :].rearrange("p m n -> p (m n)"), ps[:, 2 + d, :], ACT.Copy).then_inc(
                    sem("hf_copied"), 1)
            act.wait_ge(sem("hf_stored"), 32)

            def squares(t):
                act.wait_ge(sem("y_done"), t + 1)
                if t >= 2:
                    act.wait_ge(sem("y_squares"), 2 * (t - 1))
                for g in range(SSM_G):
                    act.activation(ps[:, 6 + t % 2, g * 256:(g + 1) * 256], xs[:, t, g * 256:(g + 1) * 256],
                                   ACT.Square, accum_out=st2[:, 0, 2 * t + g:2 * t + g + 1]).then_inc(
                        sem("y_squares"), 1)

            for t in range(TILES):
                for d in range(2):
                    n = 2 * t + d
                    act.wait_ge(sem("seg_mm"), n + 1)
                    if n >= 3:
                        act.wait_ge(sem("y_mm"), (n - 3) // 2 + 1)
                    act.activation(mt[:, n % 3, :, :].rearrange("p h s -> p (h s)"),
                                   ps[:, 1:3, :].rearrange("p b s -> p (b s)"), ACT.Exp).then_inc(sem("seg_exp"), 1)
                if t:
                    squares(t - 1)
            squares(TILES - 1)
            act.wait_ge(sem("y_squares"), 2 * TILES)
            act.activation(st2[:, 1, :], st2[:, 0, :], ACT.Sqrt, scale=1.0 / 256, bias=cx.eps[:, :]).then_inc(
                sem("y_rms"), 1)
            for m in range(4):
                act.wait_ge(sem("ossm_turned"), m + 1)
                act.activation(cx.oT[:, m, CTX:TOK], ps[:, m % 2, :], ACT.Copy, scale=nrm[:, m:m + 1]).then_inc(
                    sem("ossm_lat"), 1)

        @block.gpsimd
        def _(pool):
            def by_head(ap):
                return ap.rearrange("p (h q) -> p h q", h=SSM_H)

            pool.wait_ge(sem("a_ready"), 1)
            pool.wait_ge(sem("dec_ready"), 1)
            for d in range(2):
                pool.tensor_tensor(xco[:, d, :, :], dt[:, :, d * 8:(d + 1) * 8], dec[:, 2 + d, :, :],
                                   ALU.mult).then_inc(sem("xco_ready"), 1)
            pool.wait_ge(sem("xco_ready"), 2)
            pool.wait_ge(sem("xs_out"), TILES)
            for n, (d, t, _) in enumerate([(0, 0, 0), (1, 0, 0)] + steps):
                if n >= 2:
                    pool.wait_ge(sem("ds_mm"), n - 1)
                pool.tensor_tensor(by_head(xdd[:, n % 2, :]), by_head(xs[:, t, :]), spread(xco[:, d, t, :], 2, SSM_P),
                                   ALU.mult).then_inc(sem("xdd_ready"), 1)
            pool.wait_ge(sem("h0_turned"), 2)

            def triangle(n):
                t, d = n // 2, n % 2
                if n:
                    pool.wait_ge(sem("seg_mm"), n)
                pool.tensor_tensor(am[:, :, :], spread(a[:, t, d * 8:(d + 1) * 8], 2, P), spread((LE, GE)[d], 1, 8),
                                   ALU.mult).then_inc(sem("am_ready"), 1)

            for t in range(TILES):
                triangle(2 * t)
                if t >= 2:
                    pool.wait_ge(sem("y_mm"), t - 1)
                for d in range(2):
                    ins = pool.tensor_tensor(by_head(xdt[:, t % 2, d, :]), by_head(xs[:, t, :]),
                                             spread(dt[:, t, d * 8:(d + 1) * 8], 2, SSM_P), ALU.mult)
                ins.then_inc(sem("xdt_ready"), 1)
                y = xs[:, t, :]
                pool.tensor_tensor(by_head(y), by_head(y), spread(hb[:, 2, 0:8], 2, SSM_P), ALU.mult).then_inc(
                    sem("dx_ready"), 1)
                triangle(2 * t + 1)

        @block.vector
        def _(dve):
            step = cx.vlink
            dve.memset(xp[:, :, 0:2], 0.0)
            dve.memset(xp[:, :, 2 + CTX:4 + CTX], 0.0)
            step(dve, dve.memset(xp[:, :, XPW - 2:XPW], 0.0))
            dve.wait_ge(sem("cols_turned"), 1)
            dve.tensor_copy(cols[:, :], ps[:, 7, 0:52]).then_inc(sem("cols_ready"), 1)
            dve.wait_ge(sem("cols_ready"), 1)

            def ctx_out(m):
                dve.wait_ge(sem("xb_mm"), m + 1)
                dve.tensor_copy(xp[:, m % 4, 2:2 + CTX], ps[:, 2 + m % 2, 0:P]).then_inc(sem("xb_ctx_out"), 1)

            for m in range(8):
                ctx_out(m)
                dve.wait_ge(sem("xb_ctx_out"), m + 1)
                dve.wait_ge(sem("xb_lat_out"), m + 1)
                o = cv[:, m, 2:XPW - 2]
                n = XPW - 4
                step(dve, dve.tensor_scalar(o, xp[:, m % 4, 0:n], cols[:, m:m + 1], cols[:, 40 + m:41 + m],
                                            ALU.mult, ALU.add))
                for j in range(1, CONV_W):
                    ins = dve.scalar_tensor_tensor(out=o, in0=xp[:, m % 4, j:j + n], scalar=cols[:, 8 * j + m:8 * j + m + 1], in1=o,
                                                   op0=ALU.mult, op1=ALU.add)
                    if j < CONV_W - 1:
                        step(dve, ins)
                ins.then_inc(sem("conv_done"), 1)
            dve.wait_ge(sem("ssm_small"), 64)
            dve.wait_ge(sem("dt_mm"), 1)
            dve.tensor_tensor(dv[:, 0], ps[:, 6, 0:80].rearrange("p (t h) -> p t h", h=16),
                              spread(hb[:, 0, :], 1, TILES), ALU.add).then_inc(sem("dt_read"), 1)
            dve.wait_ge(sem("dt_read"), 1)
            step(dve, dve.tensor_scalar(dv[:, 1], dv[:, 0], -1.0, None, ALU.mult))
            dve.tensor_tensor(dv[:, 1], dv[:, 1], dv[:, 0], ALU.max).then_inc(sem("dt_abs"), 1)
            dve.wait_ge(sem("dt_exp"), 1)
            dve.tensor_scalar(dv[:, 3], dv[:, 2], 1.0, None, ALU.add).then_inc(sem("dt_one"), 1)
            dve.wait_ge(sem("dt_one"), 1)
            step(dve, dve.tensor_scalar(dv[:, 5], dv[:, 3], -1.0, 1.0e-30, ALU.add, ALU.max))
            step(dve, dve.reciprocal(dv[:, 6], dv[:, 5]))
            step(dve, dve.tensor_tensor(dv[:, 5], dv[:, 6], dv[:, 2], ALU.mult))
            dve.wait_ge(sem("dt_ln"), 1)
            step(dve, dve.tensor_tensor(dv[:, 5], dv[:, 5], dv[:, 4], ALU.mult))
            step(dve, dve.tensor_scalar(dv[:, 6], dv[:, 2], -0.5, 1.0, ALU.mult, ALU.add))
            step(dve, dve.tensor_tensor(dv[:, 6], dv[:, 6], dv[:, 2], ALU.mult))
            step(dve, dve.tensor_tensor(dv[:, 5], dv[:, 5], dv[:, 6], ALU.max))
            step(dve, dve.tensor_scalar(dv[:, 1], dv[:, 0], 0.0, None, ALU.max))
            step(dve, dve.tensor_tensor(dt, dv[:, 5], dv[:, 1], ALU.add))
            step(dve, dve.tensor_scalar(dv[:, 3], dt, -1.0, None, ALU.mult))
            dve.tensor_tensor(a, dv[:, 3], spread(hb[:, 1, :], 1, TILES), ALU.mult).then_inc(sem("a_ready"), 1)
            for t in range(TILES):
                dve.wait_ge(sem("xs_turned"), t + 1)
                dve.tensor_copy(bt[:, t, :], ps[:, 2 + t % 2, 0:256]).then_inc(sem("b_out"), 1)

            def by_head(ap):
                return ap.rearrange("p (h q) -> p h q", h=SSM_H)

            dve.wait_ge(sem("dec_ready"), 1)
            dve.wait_ge(sem("h0_ready"), 2)
            for n, (d, t, slot) in enumerate([(0, 0, 0), (1, 0, 0)] + steps):
                if n < 2:
                    dve.wait_ge(sem("ds_mm"), n + 1)
                    if n:
                        dve.wait_ge(sem("hf_turned"), 1)
                    dve.tensor_copy(tmp[:, :], ps[:, 4 + n % 2, :]).then_inc(sem("ds_used"), 1)
                else:
                    old = state[d][:, t - 1, :]
                    new = state[d][:, slot, :]
                    if n == 2:
                        dve.wait_ge(sem("hf_turned"), 2)
                    else:
                        dve.wait_ge(sem("ds_used"), n)
                    step(dve, dve.tensor_tensor(by_head(tmp[:, :]), by_head(old), spread(dec[:, 4 + d, t, :], 2, SSM_P),
                                                ALU.mult))
                    dve.wait_ge(sem("ds_mm"), n + 1)
                    dve.tensor_tensor(new, ps[:, 4 + n % 2, :], tmp[:, :], ALU.add).then_inc(sem("ds_used"), 1)
            for t in range(TILES):
                dve.wait_ge(sem("cb_mm"), t + 1)
                for d in range(2):
                    ins = dve.tensor_tensor(cbm[:, d, :, :], ps[:, 0, 0:256].rearrange("p (g l) -> p g l", g=2),
                                            spread((LE, GE)[d], 1, 2), ALU.mult)
                    if d == 0:
                        step(dve, ins)
                ins.then_inc(sem("cb_out"), 1)
                dve.wait_ge(sem("cb_out"), t + 1)
                for d in range(2):
                    n = 2 * t + d
                    dve.wait_ge(sem("seg_exp"), n + 1)
                    m4 = mt[:, n % 3, :, :].rearrange("p (g h) s -> p g h s", g=2)
                    dve.tensor_tensor(m4, m4, spread(cbm[:, d, :, :], 2, 4), ALU.mult).then_inc(sem("mt_ready"), 1)
                y = xs[:, t, :]
                dve.wait_ge(sem("dx_ready"), t + 1)
                if t:
                    dve.wait_ge(sem("yoff_mm"), t)
                    for d in range(2):
                        step(dve, dve.tensor_tensor(by_head(tmp[:, :]), by_head(ps[:, 4 + d, :]),
                                                    spread(dec[:, d, t, :], 2, SSM_P), ALU.mult))
                        step(dve, dve.tensor_tensor(y, y, tmp[:, :], ALU.add))
                dve.wait_ge(sem("y_mm"), t + 1)
                dve.tensor_tensor(y, ps[:, 3, :], y, ALU.add).then_inc(sem("y_read"), 1)
                dve.wait_ge(sem("y_read"), t + 1)
                dve.tensor_tensor(y, y, sz[:, t, :], ALU.mult).then_inc(sem("y_done"), 1)
            dve.wait_ge(sem("y_rms"), 1)
            step(dve, dve.reciprocal(st2[:, 2, :], st2[:, 1, :]))
            for t in range(TILES):
                for g in range(SSM_G):
                    y = xs[:, t, g * 256:(g + 1) * 256]
                    ins = dve.tensor_scalar(y, y, st2[:, 2, 2 * t + g:2 * t + g + 1], None, ALU.mult)
            ins.then_inc(sem("y_normed"), 1)
            for m in range(4):
                dve.wait_ge(sem("ossm_turned"), m + 1)
                dve.tensor_scalar(cx.oT[:, m, 0:CTX], ps[:, 6 + m % 2, 0:P], nrm[:, m:m + 1], None, ALU.mult).then_inc(
                    sem("ossm_ctx"), 1)



def stage_mix(nc, cx, L, n, branch, g0):
    sem = cx.sem
    ps = cx.ps
    with ExitStack() as st:
        gate = st.enter_context(nc.sbuf_tensor(f"mix_gate{n}", [P, 2, TOK], F32))
        prod = st.enter_context(nc.sbuf_tensor(f"mix_prod{n}", [P, 2, TOK], F32))
        block = st.enter_context(nc.Block())

        @block.sync
        def _(sp):
            load_behind(cx, sp, L, ("gate", g0), ("gate", g0 + 1))

        @block.tensor
        def _(pe):
            for m in range(KT):
                u = n * KT + m
                b = 4 * (m % 2)
                if m >= 2:
                    pe.wait_ge(sem("mix_gated"), u - 1)
                wg = section_ready(cx, pe, ("gate", g0 + m // 4)).rearrange("p (k n) -> p k n", k=KT)
                wb = section_ready(cx, pe, ("br", branch)).rearrange("p (k n) -> p k n", k=4)
                project_fm(cx, pe, wb, slice(m * P, (m + 1) * P), ps[:, b, :], ps[:, b + 1, 0:P], cx.oT, 4)
                c = slice((m % 4) * P, (m % 4 + 1) * P)
                project_fm(cx, pe, wg, c, ps[:, b + 2, :], ps[:, b + 3, 0:P]).then_inc(sem("mix_mm"), 1)
                if m % 4 == 3:
                    pe.wait_ge(sem("mix_mm"), u + 1)
                    for _i in range(1 + m // 4):
                        pe.sem_inc(cx.ring_free, 1)

        @block.scalar
        def _(act):
            for m in range(KT):
                u = n * KT + m
                b = 4 * (m % 2)
                act.wait_ge(sem("mix_mm"), u + 1)
                if m >= 2:
                    act.wait_ge(sem("mix_gated"), u - 1)
                act.activation(gate[:, m % 2, CTX:TOK], ps[:, b + 2, :], ACT.Sigmoid)
                act.activation(gate[:, m % 2, 0:CTX], ps[:, b + 3, 0:P], ACT.Sigmoid).then_inc(sem("mix_sig"), 1)

        @block.vector
        def _(dve):
            for m in range(KT):
                u = n * KT + m
                b = 4 * (m % 2)
                dve.wait_ge(sem("mix_sig"), u + 1)
                to = cx.mixT[:, m, :] if n == 0 else prod[:, m % 2, :]
                dve.tensor_tensor(to[:, CTX:TOK], ps[:, b, :], gate[:, m % 2, CTX:TOK], ALU.mult)
                dve.tensor_tensor(to[:, 0:CTX], ps[:, b + 1, 0:P], gate[:, m % 2, 0:CTX], ALU.mult).then_inc(
                    sem("mix_gated"), 1)
                if n:
                    dve.wait_ge(sem("mix_gated"), u + 1)
                    dve.tensor_tensor(cx.mixT[:, m, :], cx.mixT[:, m, :], to, ALU.add)



def stage_da(nc, cx, L):
    w = cx.w
    sem = cx.sem
    ps = cx.ps
    KW = TOK + PAST
    units = [(t, h) for t in range(TILES) for h in range(DA_H)]
    with ExitStack() as st:
        def sb(name, shape):
            return st.enter_context(nc.sbuf_tensor(name, shape, F32))
        qT = sb("da_qT", [P, DA_H, TOK])
        kT = sb("da_kT", [P, DA_H, KW])
        v = sb("da_v", [P, TILES + 1, 512])
        stage = sb("da_stage", [P, DA_H, P])
        rope = sb("da_rope", [P, 2, LAT])
        rt = sb("da_rt", [P, 2, LAT])
        e = sb("da_e", [P, 2, 2, PAST + LAT])
        aT = sb("da_aT", [P, 5, P])
        o = sb("da_o", [P, TILES, 512])
        sub = sb("da_sub", [P, P])
        lam = sb("da_lam", [P, 4, DA_HD])
        lk = sb("da_lk", [P, 2])
        ls = sb("da_ls", [P, 8])
        nmx = sb("da_nmx", [P, 2, 2])
        sm = sb("da_sm", [P, 2, 2])
        rc = sb("da_rc", [P, 2, 2])
        co = sb("da_co", [P, 2])
        ss = sb("da_ss", [P, 3, 20])
        block = st.enter_context(nc.Block())

        @block.sync
        def _(sp):
            sp.dma_start(stage[:, :, :], w["cache_da_k"].rearrange("o l h n t d -> (o l) h n (t d)")[
                bass.ds(L, 1)].rearrange("o h n d -> n (o h) d")).then_inc(sem("da_cache_k"), 16)
            sp.dma_start(v[:, 1, :].rearrange("p (h d) -> p h d", h=DA_H),
                         w["cache_da_v"].rearrange("o l h n d -> (o l) h n d")[bass.ds(L, 1)].rearrange(
                             "o h n d -> n (o h) d")).then_inc(sem("da_cache_v"), 16)
            sp.dma_start(rope[:, :, :].rearrange("p a b -> p (a b)"), w["k_rope"]).then_inc(sem("da_small"), 16)
            sp.dma_start(sub[:, :], w["da_subln"][bass.ds(L, 1)].broadcast_to([P, P])).then_inc(sem("da_small"), 16)
            sp.dma_start(lam[:, :, :].rearrange("p a b -> p (a b)"),
                         w["da_lambda"].rearrange("l a b -> l (a b)")[bass.ds(L, 1)].broadcast_to(
                             [P, 4 * DA_HD])).then_inc(sem("da_small"), 16)
            sp.dma_start(lk[:, :], w["k_lam"][bass.ds(L, 1)].rearrange("o p n -> (o p) n")).then_inc(
                sem("da_small"), 16)
            spare = UNROLL * (MAX_TURNS - MIN_TURNS)
            for a in range(0, spare, TILES):
                n = min(TILES, spare - a)
                sp.dma_start(cx.y_rows[UNROLL * MIN_TURNS + a:UNROLL * MIN_TURNS + a + n].rearrange("t p d -> p t d"),
                             cx.hT[:, :, :].rearrange("p k n -> p (k n)")[:, 0:n * D].rearrange(
                                 "p (t d) -> p t d", d=D)).then_inc(sem("rows_filled"), 16)
            load_behind(cx, sp, L, ("in", "dq"), ("in", "dv"))
            sp.wait_ge(sem("da_k_staged"), 1)
            sp.dma_start(cx.new_da_k.rearrange("o l h n t d -> (o l) h n (t d)")[bass.ds(L, 1)].rearrange(
                "o h n d -> n (o h) d"), stage[:, :, :]).then_inc(sem("da_stored"), 16)
            sp.wait_ge(sem("da_v_out"), 1)
            sp.dma_start(cx.new_da_v.rearrange("o l h n d -> (o l) h n d")[bass.ds(L, 1)].rearrange(
                "o h n d -> n (o h) d"), v[:, 0, :].rearrange("p (h d) -> p h d", h=DA_H)).then_inc(
                sem("da_stored"), 16)
            sp.wait_ge(sem("da_stored"), 32)

        def s_banks(n):
            return 2 * (n % 3)

        @block.tensor
        def _(pe):
            for n in range(8):
                q, m = n < 4, n % 4
                wide = section_ready(cx, pe, ("in", "dq" if q else "dk")).rearrange("p (k n) -> p k n", k=KT)
                if n >= 2:
                    pe.wait_ge(sem("da_lat_out"), n - 1)
                    pe.wait_ge(sem("da_ctx_out"), n - 1)
                c = slice(m * P, (m + 1) * P)
                project_fm(cx, pe, wide, c, ps[:, n % 2, :], ps[:, 2 + n % 2, 0:P]).then_inc(sem("da_mm"), 1)
                if m == 3:
                    pe.wait_ge(sem("da_mm"), n + 1)
                    pe.sem_inc(cx.ring_free, 1)
                if n >= 2:
                    src = (qT if n - 2 < 4 else kT)[:, (n - 2) % 4, -LAT:]
                    if n >= 4:
                        pe.wait_ge(sem("da_sin"), n - 3)
                    pe.matmul(ps[:, 4 + n % 2, :], cx.rot, src, start=True, stop=True).then_inc(sem("da_rot"), 1)
            wide = section_ready(cx, pe, ("in", "dv")).rearrange("p (k n) -> p k n", k=KT)
            for t in range(TILES):
                if t >= 2:
                    pe.wait_ge(sem("da_v_out"), t - 1)
                project_tm(cx, pe, wide, t, ps[:, 6 + t % 2, :]).then_inc(sem("da_v_mm"), 1)
                if t < 2:
                    n = 8 + t
                    pe.wait_ge(sem("da_lat_out"), n - 1)
                    pe.wait_ge(sem("da_sin"), n - 3)
                    pe.matmul(ps[:, 4 + n % 2, :], cx.rot, kT[:, n - 6, -LAT:], start=True, stop=True).then_inc(
                        sem("da_rot"), 1)
            pe.wait_ge(sem("da_v_mm"), TILES)
            pe.sem_inc(cx.ring_free, 1)
            pe.wait_ge(sem("da_cache_k"), 16)
            pe.wait_ge(sem("da_ctx_out"), 8)
            pe.wait_ge(sem("da_lat_out"), 8)
            for h in range(DA_H):
                ins = pe.transpose(ps[:, 0, h * P:(h + 1) * P], stage[:, h, :], cx.ident)
            ins.then_inc(sem("da_kc_turned"), 1)
            for h in range(DA_H):
                ins = pe.transpose(ps[:, 1, h * P:(h + 1) * P], kT[:, h, 0:CTX], cx.ident)
            ins.then_inc(sem("da_kc_turned"), 1)
            pe.wait_ge(sem("da_kc_out"), 1)
            pe.wait_ge(sem("da_k_staged"), 1)
            pe.wait_ge(sem("da_roped"), 8)
            pe.wait_ge(sem("da_v_out"), TILES)

            def scores(u, m):
                t, h = units[u]
                n = 2 * u + m
                if n >= 3:
                    pe.wait_ge(sem("da_exp"), n - 2)
                b = s_banks(n)
                rows = slice(64 * m, 64 * m + 64)
                lhs = qT[rows, h, tok(t)]
                if t == 0:
                    ins = pe.matmul(ps[:, b, 0:CTX], lhs, kT[rows, h, 0:CTX], start=True, stop=True)
                else:
                    for x in range(2):
                        ins = pe.matmul(ps[:, b + x, 0:320], lhs, kT[rows, h, CTX + 320 * x:CTX + 320 * (x + 1)],
                                        start=True, stop=True)
                ins.then_inc(sem("da_scores"), 1)

            def turn(u):
                pe.wait_ge(sem("da_a_ready"), u + 1)
                if u:
                    pe.wait_ge(sem("da_o_out"), u)
                keys = 1 if units[u][0] == 0 else 5
                for c in range(keys):
                    out = ps[:, 7, 0:P] if c == 0 else ps[:, 6, (c - 1) * P:c * P]
                    ins = pe.transpose(out, e[:, u % 2, 0, c * P:(c + 1) * P], cx.ident)
                ins.then_inc(sem("da_turned"), 1)

            def values(u):
                t, h = units[u]
                pe.wait_ge(sem("da_aT_out"), u + 1)
                keys = 1 if t == 0 else 5
                for c in range(keys):
                    ins = pe.matmul(ps[:, 7, 256:384], aT[:, c, :], v[:, c + (t > 0), h * P:(h + 1) * P],
                                    start=(c == 0), stop=(c == keys - 1))
                ins.then_inc(sem("da_o_mm"), 1)

            pe.wait_ge(sem("da_cache_v"), 16)
            scores(0, 0)
            scores(0, 1)
            scores(1, 0)
            for u in range(len(units)):
                if u + 1 < len(units):
                    scores(u + 1, 1)
                turn(u)
                if u + 2 < len(units):
                    scores(u + 2, 0)
                values(u)
            pe.wait_ge(sem("da_normed"), 1)
            for h in range(DA_H):
                if h >= 2:
                    pe.wait_ge(sem("oda_lat"), h - 1)
                    pe.wait_ge(sem("oda_ctx"), h - 1)
                for t in range(TILES):
                    out = ps[:, 2 + h % 2, 0:P] if t == 0 else ps[:, h % 2, tok(t - 1)]
                    ins = pe.transpose(out, o[:, t, h * P:(h + 1) * P], cx.ident)
                ins.then_inc(sem("oda_turned"), 1)

        @block.scalar
        def _(act):
            for n in range(8):
                act.wait_ge(sem("da_mm"), n + 1)
                dst = qT if n < 4 else kT
                act.activation(dst[:, n % 4, -LAT:], ps[:, n % 2, :], ACT.Copy,
                               scale=DA_HD ** -0.5 if n < 4 else 1.0).then_inc(sem("da_lat_out"), 1)
            act.wait_ge(sem("da_small"), 64)
            act.wait_ge(sem("da_lam_sums"), 1)
            act.activation(ls[:, 2:4], ls[:, 0:2], ACT.Exp).then_inc(sem("da_lam_exp"), 1)
            for t in range(TILES):
                act.wait_ge(sem("da_v_mm"), t + 1)
                act.activation(v[:, t if t == 0 else t + 1, :], ps[:, 6 + t % 2, :], ACT.Copy).then_inc(
                    sem("da_v_out"), 1)
            act.wait_ge(sem("da_kc_turned"), 2)
            act.activation(kT[:, :, CTX:CTX + PAST], ps[:, 0, :].rearrange("p (h n) -> p h n", h=DA_H),
                           ACT.Copy).then_inc(sem("da_kc_out"), 1)

            def evacuate(u):
                act.wait_ge(sem("da_turned"), u + 1)
                if u:
                    act.wait_ge(sem("da_o_mm"), u)
                if units[u][0]:
                    act.activation(aT[:, 1:5, :].rearrange("p c q -> p (c q)"), ps[:, 6, :], ACT.Copy)
                act.activation(aT[:, 0, :], ps[:, 7, 0:P], ACT.Copy).then_inc(sem("da_aT_out"), 1)

            def exps(u, m):
                t = units[u][0]
                n = 2 * u + m
                if u >= 2:
                    act.wait_ge(sem("da_turned"), u - 1)
                act.wait_ge(sem("da_max"), n + 1)
                b = s_banks(n)
                if t == 0:
                    src, dst = ps[:, b, 0:CTX], e[:, u % 2, m, 0:CTX]
                else:
                    src = ps[:, b:b + 2, 0:320]
                    dst = e[:, u % 2, m, :].rearrange("p (x k) -> p x k", x=2)
                act.activation(dst, src, ACT.Exp, bias=nmx[:, u % 2, m:m + 1],
                               accum_out=sm[:, u % 2, m:m + 1]).then_inc(sem("da_exp"), 1)

            def squares(t):
                act.wait_ge(sem("da_o_out"), (t + 1) * DA_H)
                if t == 0:
                    act.wait_ge(sem("da_roped"), 8)
                else:
                    act.wait_ge(sem("da_squares"), t * DA_H)
                for h in range(DA_H):
                    act.activation(rt[:, 0, h * P:(h + 1) * P], o[:, t, h * P:(h + 1) * P], ACT.Square,
                                   accum_out=ss[:, 0, t * DA_H + h:t * DA_H + h + 1]).then_inc(sem("da_squares"), 1)

            exps(0, 0)
            exps(0, 1)
            for u in range(len(units)):
                if u + 1 < len(units):
                    exps(u + 1, 0)
                evacuate(u)
                if u + 1 < len(units):
                    exps(u + 1, 1)
                if u % DA_H == 1 and u > DA_H:
                    squares(u // DA_H - 1)
            squares(TILES - 1)
            act.wait_ge(sem("da_squares"), 20)
            act.activation(ss[:, 1, :], ss[:, 0, :], ACT.Sqrt, scale=1.0 / (2 * DA_HD), bias=cx.eps[:, :]).then_inc(
                sem("da_rms"), 1)
            for h in range(DA_H):
                act.wait_ge(sem("oda_turned"), h + 1)
                act.activation(cx.oT[:, h, CTX:TOK], ps[:, h % 2, :], ACT.Copy).then_inc(sem("oda_lat"), 1)

        @block.vector
        def _(dve):
            step = cx.vlink

            def rope_chunk(n):
                x = (qT if n < 4 else kT)[:, n % 4, -LAT:]
                dve.wait_ge(sem("da_rot"), n + 1)
                r = rt[:, n % 2, :]
                dve.tensor_tensor(r, ps[:, 4 + n % 2, :], rope[:, 1, :], ALU.mult).then_inc(sem("da_sin"), 1)
                step(dve, dve.tensor_tensor(x, x, rope[:, 0, :], ALU.mult))
                dve.tensor_tensor(x, x, r, ALU.add).then_inc(sem("da_roped"), 1)

            dve.wait_ge(sem("da_small"), 64)
            step(dve, dve.tensor_tensor(lam[:, 0:4:2, :], lam[:, 0:4:2, :], lam[:, 1:4:2, :], ALU.mult))
            dve.tensor_reduce(ls[:, 0:2], lam[:, 0:4:2, :], AX.X, ALU.add).then_inc(sem("da_lam_sums"), 1)
            for n in range(8):
                dve.wait_ge(sem("da_mm"), n + 1)
                dve.tensor_scalar((qT if n < 4 else kT)[:, n % 4, 0:CTX], ps[:, 2 + n % 2, 0:P],
                                  DA_HD ** -0.5 if n < 4 else 1.0, None, ALU.mult).then_inc(sem("da_ctx_out"), 1)
                if n >= 2:
                    rope_chunk(n - 2)
            rope_chunk(6)
            rope_chunk(7)
            dve.wait_ge(sem("da_lam_exp"), 1)
            step(dve, dve.tensor_tensor(ls[:, 4:5], ls[:, 3:4], ls[:, 2:3], ALU.subtract))
            step(dve, dve.tensor_tensor(ls[:, 5:6], ls[:, 4:5], lk[:, 0:1], ALU.subtract))
            step(dve, dve.tensor_scalar(sub[:, :], sub[:, :], lk[:, 1:2], None, ALU.mult))
            dve.wait_ge(sem("da_kc_turned"), 2)
            dve.tensor_copy(stage[:, :, :].rearrange("p h d -> p (h d)"), ps[:, 1, :]).then_inc(
                sem("da_k_staged"), 1)

            def maxima(u, m):
                n = 2 * u + m
                dve.wait_ge(sem("da_scores"), n + 1)
                b = s_banks(n)
                if n >= 4:
                    dve.wait_ge(sem("da_exp"), n - 3)
                src = ps[:, b, 0:CTX] if units[u][0] == 0 else ps[:, b:b + 2, 0:320]
                dve.tensor_reduce(nmx[:, u % 2, m:m + 1], src, AX.X if units[u][0] == 0 else AX.XY, ALU.max,
                                  negate=True).then_inc(sem("da_max"), 1)

            def combine(u):
                keys = CTX if units[u][0] == 0 else PAST + LAT
                dve.wait_ge(sem("da_exp"), 2 * u + 2)
                step(dve, dve.reciprocal(rc[:, u % 2, :], sm[:, u % 2, :]))
                e0, e1 = e[:, u % 2, 0, 0:keys], e[:, u % 2, 1, 0:keys]
                step(dve, dve.tensor_scalar(co[:, u % 2:u % 2 + 1], sm[:, u % 2, 0:1], rc[:, u % 2, 1:2], ls[:, 5:6],
                                            ALU.mult, ALU.mult))
                dve.scalar_tensor_tensor(out=e0, in0=e1, scalar=co[:, u % 2:u % 2 + 1], in1=e0, op0=ALU.mult,
                                         op1=ALU.add).then_inc(sem("da_a_ready"), 1)

            def take(u):
                t, h = units[u]
                dve.wait_ge(sem("da_o_mm"), u + 1)
                dve.tensor_scalar(o[:, t, h * P:(h + 1) * P], ps[:, 7, 256:384], rc[:, u % 2, 0:1], None,
                                  ALU.mult).then_inc(sem("da_o_out"), 1)

            maxima(0, 0)
            maxima(0, 1)
            maxima(1, 0)
            for u in range(len(units)):
                combine(u)
                if u:
                    take(u - 1)
                if u + 1 < len(units):
                    maxima(u + 1, 1)
                if u + 2 < len(units):
                    maxima(u + 2, 0)
            take(len(units) - 1)
            dve.wait_ge(sem("da_rms"), 1)
            step(dve, dve.reciprocal(ss[:, 2, :], ss[:, 1, :]))
            for t in range(TILES):
                for h in range(DA_H):
                    x = o[:, t, h * P:(h + 1) * P]
                    ins = dve.scalar_tensor_tensor(out=x, in0=x, scalar=ss[:, 2, t * 4 + h:t * 4 + h + 1],
                                                   in1=sub[:, :], op0=ALU.mult, op1=ALU.mult)
            ins.then_inc(sem("da_normed"), 1)
            for h in range(DA_H):
                dve.wait_ge(sem("oda_turned"), h + 1)
                dve.tensor_copy(cx.oT[:, h, 0:CTX], ps[:, 2 + h % 2, 0:P]).then_inc(sem("oda_ctx"), 1)



def stage_na(nc, cx, L):
    w = cx.w
    sem = cx.sem
    ps = cx.ps
    KW = TOK + PAST
    ALLK = NKEY + PAST
    units = [(b, h) for b in range(1 + NBLK) for h in range(NA_H)]
    with ExitStack() as st:
        def sb(name, shape):
            return st.enter_context(nc.sbuf_tensor(name, shape, F32))
        qT = sb("na_qT", [P, 4, TOK])
        kT = sb("na_kT", [P, 4, KW])
        v0 = sb("na_v0", [P, 2, 512])
        vlo = sb("na_vlo", [P, 4, 512])
        vg = sb("na_vg", [P, NBLK, 2, 512])
        raw = sb("na_raw", [P, 4, NKEY])
        mask = sb("na_mask", [P, NBLK, NKEY])
        bias = sb("na_bias", [P, 2, ALLK])
        pr = sb("na_pr", [P, 2, ALLK])
        pT = sb("na_pT", [P, 2, 3, P])
        o = vlo[:, 2:4, :]
        stage = sb("na_stage", [P, NA_H, NA_HD])
        mx = sb("na_mx", [P, 4])
        nmx = sb("na_nmx", [P, 4])
        sm = sb("na_sm", [P, 2, NA_H])
        rc = sb("na_rc", [P, 2, NA_H])
        block = st.enter_context(nc.Block())

        def grid(ap):
            return ap.rearrange("p (r c) -> p r c", c=GRID_W)

        @block.sync
        def _(sp):
            sp.dma_start(stage[:, :, :], w["cache_na_k"].rearrange("o l h n d -> (o l) h n d")[
                bass.ds(L, 1)].rearrange("o h n d -> n (o h) d")).then_inc(sem("na_cache_k"), 16)
            sp.dma_start(v0[:, 1, :].rearrange("p (h d) -> p h d", h=NA_H),
                         w["cache_na_v"].rearrange("o l h n d -> (o l) h n d")[bass.ds(L, 1)].rearrange(
                             "o h n d -> n (o h) d")).then_inc(sem("na_cache_v"), 16)
            sp.dma_start(mask[:, :, :].rearrange("p a b -> p (a b)"), w["k_mask"]).then_inc(sem("na_mask"), 16)
            load_behind(cx, sp, L, ("in", "nq"), ("in", "nv"))
            for t in range(1, TILES):
                sp.wait_ge(sem("na_v_out"), t + 1)
                sp.dma_start(cx.v_scratch[tok(t - 1), :], vlo[:, t - 1, :]).then_inc(sem("na_v_dumped"), 16)
            sp.wait_ge(sem("na_v_dumped"), 64)
            for j in range(NBLK):
                for half in range(2):
                    rows = cx.v_scratch.rearrange("(r c) d -> r c d", c=GRID_W)
                    sp.dma_start(vg[:, j, half, :], rows[4 * half:4 * half + 4, col0(j):col0(j) + WCOLS, :]).then_inc(
                        sem("na_gathered"), 16)
            sp.wait_ge(sem("na_k_staged"), 1)
            sp.dma_start(cx.new_na_k.rearrange("o l h n d -> (o l) h n d")[bass.ds(L, 1)].rearrange(
                "o h n d -> n (o h) d"), stage[:, :, :]).then_inc(sem("na_stored"), 16)
            sp.dma_start(cx.new_na_v.rearrange("o l h n d -> (o l) h n d")[bass.ds(L, 1)].rearrange(
                "o h n d -> n (o h) d"), v0[:, 0, :].rearrange("p (h d) -> p h d", h=NA_H)).then_inc(
                sem("na_stored"), 16)
            for n, (b, h) in enumerate(units[NA_H:]):
                if n >= 4:
                    sp.wait_ge(sem("na_bias_ready"), n - 3)
                at = h * RPB_ROW + RPB_FRONT + col0(b - 1) - QB_C * (b - 1)
                src = bass.AP(tensor=cx.rpb_scratch.tensor, offset=L * (NA_H * RPB_ROW) + at,
                              ap=[[WCOLS, ROWS], [1, QB_C], [1, NKEY]])
                sp.dma_start(raw[:, n % 4, :], src).then_inc(sem(f"na_raw{n % 4}"), 16)
            sp.wait_ge(sem("na_stored"), 32)
            sp.wait_ge(sem("rows_filled"), 16 * -(-UNROLL * (MAX_TURNS - MIN_TURNS) // TILES))

        @block.tensor
        def _(pe):
            for n in range(8):
                q, m = n < 4, n % 4
                wide = section_ready(cx, pe, ("in", "nq" if q else "nk")).rearrange("p (k n) -> p k n", k=KT)
                if n >= 2:
                    pe.wait_ge(sem("na_lat_out"), n - 1)
                    pe.wait_ge(sem("na_ctx_out"), n - 1)
                c = slice(m * P, (m + 1) * P)
                project_fm(cx, pe, wide, c, ps[:, n % 2, :], ps[:, 2 + n % 2, 0:P]).then_inc(sem("na_mm"), 1)
                if m == 3:
                    pe.wait_ge(sem("na_mm"), n + 1)
                    pe.sem_inc(cx.ring_free, 1)
            wide = section_ready(cx, pe, ("in", "nv")).rearrange("p (k n) -> p k n", k=KT)
            for t in range(TILES):
                if t >= 2:
                    pe.wait_ge(sem("na_v_out"), t - 1)
                project_tm(cx, pe, wide, t, ps[:, 6 + t % 2, :]).then_inc(sem("na_v_mm"), 1)
            pe.wait_ge(sem("na_v_mm"), TILES)
            pe.sem_inc(cx.ring_free, 1)
            pe.wait_ge(sem("na_cache_k"), 16)
            pe.wait_ge(sem("na_lat_out"), 8)
            pe.wait_ge(sem("na_ctx_out"), 8)
            for c in range(4):
                ins = pe.transpose(ps[:, 0, c * P:(c + 1) * P],
                                   stage[:, 2 * c:2 * c + 2, :].rearrange("p h d -> p (h d)"), cx.ident)
            ins.then_inc(sem("na_kc_turned"), 1)
            for c in range(4):
                ins = pe.transpose(ps[:, 1, c * P:(c + 1) * P], kT[:, c, 0:CTX], cx.ident)
            ins.then_inc(sem("na_kc_turned"), 1)
            pe.wait_ge(sem("na_kc_out"), 1)
            pe.wait_ge(sem("na_k_staged"), 1)
            pe.wait_ge(sem("na_v_out"), TILES)
            pe.wait_ge(sem("na_cache_v"), 16)

            def scores(u):
                b, h = units[u]
                if u >= 3:
                    if units[u - 3][0] == 0:
                        pe.wait_ge(sem("na_exp"), u - 2)
                    else:
                        pe.wait_ge(sem("na_s_read"), u - 2 - NA_H)
                rows, c = slice(64 * (h % 2), 64 * (h % 2) + 64), h // 2
                if b == 0:
                    ins = pe.matmul(ps[:, u % 3, 0:CTX], qT[rows, c, 0:CTX], kT[rows, c, 0:CTX], start=True, stop=True)
                else:
                    j = b - 1
                    q = qT[rows, c, tok(b)]
                    k = grid(kT[rows, c, CTX + PAST:KW])[:, :, col0(j):col0(j) + WCOLS]
                    pe.matmul(ps[:, u % 3, 0:NKEY], q, k, start=True, stop=True)
                    ins = pe.matmul(ps[:, u % 3, NKEY:ALLK], q, kT[rows, c, CTX:CTX + PAST], start=True, stop=True)
                ins.then_inc(sem("na_scores"), 1)

            def turn(u):
                pe.wait_ge(sem("na_exp"), u + 1)
                if u >= 2:
                    pe.wait_ge(sem("na_pT_out"), u - 1)
                for c in range(1 if units[u][0] == 0 else 3):
                    ins = pe.transpose(ps[:, 3 + u % 2, c * P:(c + 1) * P], pr[:, u % 2, c * P:(c + 1) * P], cx.ident)
                ins.then_inc(sem("na_turned"), 1)

            def values(u):
                b, h = units[u]
                pe.wait_ge(sem("na_pT_out"), u + 1)
                if h == 0 and b >= 2:
                    pe.wait_ge(sem("na_o_out"), b - 1)
                out = ps[:, 5 + b % 2, h * 64:(h + 1) * 64]
                c = slice(h * 64, (h + 1) * 64)
                if b == 0:
                    ins = pe.matmul(out, pT[:, u % 2, 0, :], v0[:, 0, c], start=True, stop=True)
                else:
                    if b == 1 and h == 0:
                        pe.wait_ge(sem("na_gathered"), 16 * 2 * NBLK)
                    for x in range(2):
                        pe.matmul(out, pT[:, u % 2, x, :], vg[:, b - 1, x, c], start=(x == 0), stop=False)
                    ins = pe.matmul(out, pT[:, u % 2, 2, :], v0[:, 1, c], start=False, stop=True)
                ins.then_inc(sem("na_o_mm"), 1)

            def output(b):
                pe.wait_ge(sem("na_o_out"), b + 1)
                if b:
                    pe.wait_ge(sem("ona_out"), b)
                for c in range(4):
                    ins = pe.transpose(ps[:, 7, c * P:(c + 1) * P], o[:, b % 2, c * P:(c + 1) * P], cx.ident)
                ins.then_inc(sem("ona_turned"), 1)

            scores(0)
            scores(1)
            for u in range(len(units)):
                if u + 2 < len(units):
                    scores(u + 2)
                turn(u)
                if u:
                    values(u - 1)
                if u % NA_H == 2 and u > NA_H:
                    output(u // NA_H - 1)
            values(len(units) - 1)
            output(NBLK)

        @block.scalar
        def _(act):
            for n in range(8):
                act.wait_ge(sem("na_mm"), n + 1)
                if n < 4:
                    act.activation(reverse(qT[:, n, CTX:TOK].rearrange("p (j r c) -> p r j c", j=NBLK, r=ROWS), 1, 3),
                                   ps[:, n % 2, :].rearrange("p (r j c) -> p r j c", j=NBLK, r=ROWS), ACT.Copy,
                                   scale=NA_HD ** -0.5).then_inc(sem("na_lat_out"), 1)
                else:
                    act.activation(kT[:, n - 4, -LAT:], ps[:, n % 2, :], ACT.Copy).then_inc(sem("na_lat_out"), 1)
            for t in range(TILES):
                act.wait_ge(sem("na_v_mm"), t + 1)
                dst = v0[:, 0, :] if t == 0 else vlo[:, t - 1, :]
                act.activation(dst, ps[:, 6 + t % 2, :], ACT.Copy).then_inc(sem("na_v_out"), 1)
            act.wait_ge(sem("na_kc_turned"), 2)
            act.activation(kT[:, :, CTX:CTX + PAST], ps[:, 0, :].rearrange("p (h n) -> p h n", h=4),
                           ACT.Copy).then_inc(sem("na_kc_out"), 1)

            def evacuate(u):
                act.wait_ge(sem("na_turned"), u + 1)
                if u >= 2:
                    act.wait_ge(sem("na_o_mm"), u - 1)
                c = 1 if units[u][0] == 0 else 3
                act.activation(pT[:, u % 2, 0:c, :].rearrange("p c q -> p (c q)"), ps[:, 3 + u % 2, 0:c * P],
                               ACT.Copy).then_inc(sem("na_pT_out"), 1)

            for u, (b, h) in enumerate(units):
                act.wait_ge(sem("na_max"), u + 1)
                if u >= 2:
                    act.wait_ge(sem("na_turned"), u - 1)
                if b == 0:
                    act.activation(pr[:, u % 2, 0:CTX], ps[:, u % 3, 0:CTX], ACT.Exp, bias=nmx[:, u % 4:u % 4 + 1],
                                   accum_out=sm[:, b % 2, h:h + 1]).then_inc(sem("na_exp"), 1)
                else:
                    if h == 0 and b >= 2:
                        act.wait_ge(sem("na_o_out"), b - 1)
                    act.activation(pr[:, u % 2, :], pr[:, u % 2, :], ACT.Exp, bias=nmx[:, u % 4:u % 4 + 1],
                                   accum_out=sm[:, b % 2, h:h + 1]).then_inc(sem("na_exp"), 1)
                if u:
                    evacuate(u - 1)
            evacuate(len(units) - 1)

        @block.vector
        def _(dve):
            step = cx.vlink
            for x in range(2):
                ins = dve.memset(bias[:, x, NKEY:ALLK], 0.0)
            step(dve, ins)
            for n in range(8):
                dve.wait_ge(sem("na_mm"), n + 1)
                dve.tensor_scalar((qT if n < 4 else kT)[:, n % 4, 0:CTX], ps[:, 2 + n % 2, 0:P],
                                  NA_HD ** -0.5 if n < 4 else 1.0, None, ALU.mult).then_inc(sem("na_ctx_out"), 1)
            dve.wait_ge(sem("na_kc_turned"), 2)
            dve.tensor_copy(stage[:, :, :].rearrange("p h d -> p (h d)"), ps[:, 1, :]).then_inc(
                sem("na_k_staged"), 1)
            dve.wait_ge(sem("na_mask"), 16)

            def maxima(u):
                b, h = units[u]
                dve.wait_ge(sem("na_scores"), u + 1)
                if u >= 4:
                    dve.wait_ge(sem("na_exp"), u - 3)
                if b == 0:
                    dve.tensor_reduce(nmx[:, u % 4:u % 4 + 1], ps[:, u % 3, 0:CTX], AX.X, ALU.max,
                                      negate=True).then_inc(sem("na_max"), 1)
                    return
                n = u - NA_H
                dve.wait_ge(sem(f"na_raw{n % 4}"), 16 * (n // 4 + 1))
                dve.tensor_tensor(bias[:, u % 2, 0:NKEY], raw[:, n % 4, :], mask[:, b - 1, :], ALU.add).then_inc(
                    sem("na_bias_ready"), 1)
                dve.wait_ge(sem("na_bias_ready"), n + 1)
                if u >= 2:
                    dve.wait_ge(sem("na_turned"), u - 1)
                dve.tensor_tensor_reduce(out=pr[:, u % 2, :], in0=ps[:, u % 3, 0:ALLK], in1=bias[:, u % 2, :],
                                         scale=1.0, scalar=-3.0e38, op0=ALU.add, op1=ALU.max,
                                         accum_out=mx[:, u % 4:u % 4 + 1]).then_inc(sem("na_s_read"), 1)
                dve.wait_ge(sem("na_s_read"), n + 1)
                dve.tensor_scalar(nmx[:, u % 4:u % 4 + 1], mx[:, u % 4:u % 4 + 1], -1.0, None, ALU.mult).then_inc(
                    sem("na_max"), 1)

            def take(b):
                step(dve, dve.reciprocal(rc[:, b % 2, :], sm[:, b % 2, :]))
                if b >= 2:
                    dve.wait_ge(sem("ona_turned"), b - 1)
                else:
                    dve.wait_ge(sem("na_v_dumped"), 64)
                dve.tensor_tensor(o[:, b % 2, :].rearrange("p (h d) -> p h d", h=NA_H),
                                  ps[:, 5 + b % 2, :].rearrange("p (h d) -> p h d", h=NA_H),
                                  spread(rc[:, b % 2, :], 2, NA_HD), ALU.mult).then_inc(sem("na_o_out"), 1)

            def spill(b):
                dve.wait_ge(sem("ona_turned"), b + 1)
                src = ps[:, 7, :].rearrange("p (c q) -> p c q", c=4)
                for c in range(4):
                    if b == 0:
                        dst, s = cx.oT[:, c, 0:CTX], src[:, c, :]
                    else:
                        dst = grid(cx.oT[:, c, CTX:TOK])[:, :, QB_C * (b - 1):QB_C * b]
                        s = reverse(src[:, c, :].rearrange("p (r q) -> p r q", r=ROWS), 1, 2)
                    ins = dve.tensor_copy(dst, s)
                ins.then_inc(sem("ona_out"), 1)

            for u, (b, h) in enumerate(units):
                maxima(u)
                if u >= NA_H and h == 2:
                    dve.wait_ge(sem("na_o_mm"), b * NA_H)
                    dve.wait_ge(sem("na_exp"), b * NA_H)
                    take(b - 1)
                if u >= NA_H and h == 5:
                    spill(b - 1)
            dve.wait_ge(sem("na_o_mm"), len(units))
            dve.wait_ge(sem("na_exp"), len(units))
            take(NBLK)
            spill(NBLK)



def stage_out(nc, cx, L, x):
    w = cx.w
    sem = cx.sem
    ps = cx.ps
    with ExitStack() as st:
        xn = st.enter_context(nc.sbuf_tensor("out_xn", [P, TILES, D], F32))
        ms = st.enter_context(nc.sbuf_tensor("out_ms", [P, 3, TILES], F32))
        block = st.enter_context(nc.Block())

        @block.sync
        def _(sp):
            sp.dma_start(x[:, 0, :], cx.y_prompt.rearrange("o n d -> (o n) d")).then_inc(sem("x_again"), 16)
            sp.dma_start(x[:, 1:TILES, :], cx.y_sample.rearrange("o (t p) d -> p (o t) d", p=P)).then_inc(
                sem("x_again"), 16)

        @block.tensor
        def _(pe):
            wide = [section_ready(cx, pe, ("out", n)).rearrange("p (k n) -> p k n", k=KT) for n in range(2)]
            for t in range(TILES):
                if t >= 4:
                    pe.wait_ge(sem("mixed_out"), t - 3)
                for n in range(2):
                    for k in range(KT):
                        ins = pe.matmul(ps[:, 2 * (t % 4) + n, :], cx.mixT[:, k, tok(t)], wide[n][:, k, :],
                                        start=(k == 0), stop=(k == KT - 1))
                ins.then_inc(sem("mixed_mm"), 1)
            pe.wait_ge(sem("mixed_mm"), TILES)
            pe.sem_inc(cx.ring_free, 1)
            pe.sem_inc(cx.ring_free, 1)
            pe.wait_ge(sem("mixed_out"), TILES)
            norm_tensor(cx, pe, 1, xn)

        @block.scalar
        def _(act):
            for t in range(TILES):
                act.wait_ge(sem("mixed_mm"), t + 1)
                b = 2 * (t % 4)
                act.activation(xn[:, t, :].rearrange("p (b n) -> p b n", b=2), ps[:, b:b + 2, :], ACT.Square,
                               accum_out=ms[:, 0, t:t + 1]).then_inc(sem("mixed_sq"), 1)
                act.wait_ge(sem("mixed_sq"), t + 1)
                act.activation(ms[:, 1, t:t + 1], ms[:, 0, t:t + 1], ACT.Sqrt, scale=1.0 / D,
                               bias=cx.eps[:, :]).then_inc(sem("mixed_rms"), 1)
            act.wait_ge(sem("x1_ready"), TILES)
            norm_scalar(cx, act, 1, x, xn)
            modulate_scalar(cx, act, 1)

        @block.vector
        def _(dve):
            step = cx.vlink
            dve.wait_ge(sem("x_again"), 32)
            for t in range(TILES):
                dve.wait_ge(sem("mixed_rms"), t + 1)
                b = 2 * (t % 4)
                step(dve, dve.reciprocal(ms[:, 2, t:t + 1], ms[:, 1, t:t + 1]))
                dve.scalar_tensor_tensor(out=xn[:, t, :].rearrange("p (b n) -> p b n", b=2), in0=ps[:, b:b + 2, :],
                                         scalar=ms[:, 2, t:t + 1],
                                         in1=cx.gate_post[:, 0, min(t, 1), :].rearrange("p (b n) -> p b n", b=2),
                                         op0=ALU.mult, op1=ALU.mult).then_inc(sem("mixed_out"), 1)
                dve.wait_ge(sem("mixed_out"), t + 1)
                dve.tensor_tensor(x[:, t, :], x[:, t, :], xn[:, t, :], ALU.add).then_inc(sem("x1_ready"), 1)
            norm_vector(cx, dve, 1, x, xn)
            modulate_vector(cx, dve, 1)





def tile_slot(n):
    return (n + 1) % SLOTS


def stage_route(nc, cx, L, m):
    w = cx.w
    sem = cx.sem
    ps = cx.ps
    with ExitStack() as st:
        def sb(name, shape, dt=F32):
            return st.enter_context(nc.sbuf_tensor(name, shape, dt))
        silu = sb("route_silu", [P, TOK])
        wr = sb("route_wr", [P, KT, NE])
        br = sb("route_br", [P, NE])
        iota = sb("route_iota", [P, P + TILES + 1])
        s = sb("route_s", [P, TILES, NE])
        sbias = sb("route_sb", [P, TILES, NE])
        gt = sb("route_gt", [P, TILES, NE])
        eq = sb("route_eq", [P, TILES, NE])
        mask = sb("route_mask", [P, TILES, NE])
        order = sb("route_order", [P, TILES, NE])
        pos = sb("route_pos", [P, TILES, NE])
        over = sb("route_over", [P, TILES, NE])
        vals = sb("route_vals", [P, 3, TILES, NE])
        pick = sb("route_pick", [P, 3, TILES, NE])
        chosen = sb("route_chosen", [P, TOP_K, 3, TILES])
        top = sb("route_top", [P, TILES, 8])
        small = sb("route_small", [P, 4, TILES])
        cnt = sb("route_cnt", [P, 4, NE])
        ids = sb("route_ids", [P, 2])
        where = sb("route_where", [P, N_CHOICE, TABLE])
        place = cx.oT[:, :, :].rearrange("p a b -> p (a b)").rearrange("p (n s) -> p n s", s=P)
        rows = cx.mixT[:, :, :].rearrange("p a b -> p (a b)").rearrange("p (t d) -> p t d", d=D)
        row = iota[:, 0:P]
        token = iota[:, P:P + TILES]
        col = iota[:, P + TILES:P + TILES + 1]
        block = st.enter_context(nc.Block())

        @block.sync
        def _(sp):
            sp.dma_start(wr[:, :, :], w["w_router"][bass.ds(L, 1)].rearrange("l (p k) n -> p (l k) n", k=KT)).then_inc(
                sem("router_in"), 16)
            sp.dma_start(br[:, :], w["b_router"][bass.ds(L, 1)].broadcast_to([P, NE])).then_inc(sem("router_in"), 16)
            sp.dma_start(iota[:, :], w["k_iota"]).then_inc(sem("router_in"), 16)
            sp.dma_start(m.wsd[:, :, :], w["w_s_down"][bass.ds(L, 1)].rearrange("l (k p) n -> p (l k) n", p=P)).then_inc(
                sem("shared_down_in"), 16)
            for t in range(TILES):
                sp.wait_ge(sem("rows_out"), t + 1)
                sp.dma_start(cx.h_rows[tok(t), :], rows[:, t, :]).then_inc(sem("rows_stored"), 16)
            sp.wait_ge(sem("rows_stored"), 16 * TILES)
            sp.wait_ge(sem("shared_down_in"), 16)

        @block.tensor
        def _(pe):
            pe.wait_ge(sem("router_in"), 48)
            for t in range(TILES):
                for k in range(KT):
                    ins = pe.matmul(ps[:, 7, t * NE:(t + 1) * NE], cx.hT[:, k, tok(t)], wr[:, k, :], start=(k == 0),
                                    stop=(k == KT - 1))
            ins.then_inc(sem("router_mm"), 1)
            for t in range(TILES):
                if t >= 2:
                    pe.wait_ge(sem("rows_out"), t - 1)
                for k in range(KT):
                    ins = pe.transpose(ps[:, 3 + 2 * (t % 2) + k // 4, (k % 4) * P:(k % 4 + 1) * P],
                                       cx.hT[:, k, tok(t)], cx.ident)
                ins.then_inc(sem("rows_turned"), 1)

            def shared(c):
                sh = section_ready(cx, pe, ("shared_up", 0)).rearrange("p (k n) -> p k n", k=KT)
                if c:
                    pe.wait_ge(sem("shared_hid"), c)
                project_fm(cx, pe, sh, slice(c * P, (c + 1) * P), ps[:, 0, :], ps[:, 2, 0:P])
                project_fm(cx, pe, sh, slice(SFF + c * P, SFF + (c + 1) * P), ps[:, 1, :], ps[:, 2, P:2 * P]).then_inc(
                    sem("shared_mm"), 1)

            shared(0)
            pe.wait_ge(sem("mask_ready"), 1)
            for t in range(TILES):
                out = ps[:, 7, t * NE:(t + 1) * NE]
                for b in range(t):
                    pe.matmul(out, cx.ones, mask[:, b, :], start=(b == 0), stop=False)
                pe.matmul(out, cx.lt, mask[:, t, :], start=(t == 0), stop=True)
            for b in range(TILES):
                ins = pe.matmul(ps[:, 7, TILES * NE:(TILES + 1) * NE], cx.ones, mask[:, b, :], start=(b == 0),
                                stop=(b == TILES - 1))
            ins.then_inc(sem("rank_mm"), 1)
            shared(1)
            pe.wait_ge(sem("rows_out"), TILES)
            pe.wait_ge(sem("ids_ready"), 1)
            pe.transpose(ps[0:1, 4, 0:P], ids[:, 1:2], cx.ident).then_inc(sem("ids_turned"), 1)
            pe.wait_ge(sem("place_ready"), 1)
            for n in range(N_CHOICE):
                ins = pe.matmul(ps[:, 3, 0:TABLE], place[:, n, :], where[:, n, :], start=(n == 0),
                                stop=(n == N_CHOICE - 1))
            ins.then_inc(sem("table_mm"), 1)

        @block.scalar
        def _(act):
            act.wait_ge(sem("router_mm"), 1)
            act.activation(s[:, :, :].rearrange("p t e -> p (t e)"), ps[:, 7, 0:TILES * NE], ACT.Sigmoid).then_inc(
                sem("router_s"), 1)
            for t in range(TILES):
                act.wait_ge(sem("rows_turned"), t + 1)
                b = 3 + 2 * (t % 2)
                act.activation(rows[:, t, :].rearrange("p (b n) -> p b n", b=2), ps[:, b:b + 2, :], ACT.Copy).then_inc(
                    sem("rows_out"), 1)
            for c in range(2):
                act.wait_ge(sem("shared_mm"), c + 1)
                if c:
                    act.wait_ge(sem("shared_hid"), c)
                act.activation(silu[:, CTX:TOK], ps[:, 0, :], ACT.Silu)
                act.activation(silu[:, 0:CTX], ps[:, 2, 0:P], ACT.Silu).then_inc(sem("shared_silu"), 1)

        @block.vector
        def _(dve):
            step = cx.vlink

            def shared(c):
                dve.wait_ge(sem("shared_silu"), c + 1)
                dve.tensor_tensor(m.hsh[:, c, CTX:TOK], ps[:, 1, :], silu[:, CTX:TOK], ALU.mult)
                dve.tensor_tensor(m.hsh[:, c, 0:CTX], ps[:, 2, P:2 * P], silu[:, 0:CTX], ALU.mult).then_inc(
                    sem("shared_hid"), 1)

            dve.wait_ge(sem("router_in"), 48)
            dve.wait_ge(sem("router_s"), 1)
            step(dve, dve.tensor_tensor(sbias[:, :, :], s[:, :, :], spread(br[:, :], 1, TILES), ALU.add))
            for t in range(TILES):
                ins = dve.max(top[:, t, :], sbias[:, t, :])
            step(dve, ins)
            least = spread(top[:, :, TOP_K - 1], 2, NE)
            step(dve, dve.tensor_tensor(gt[:, :, :], sbias[:, :, :], least, ALU.is_gt))
            step(dve, dve.tensor_tensor(eq[:, :, :], sbias[:, :, :], least, ALU.is_equal))
            step(dve, dve.tensor_reduce(small[:, 0, :], gt[:, :, :], AX.X, ALU.add))
            for t in range(TILES):
                ins = dve.tensor_tensor_scan(order[:, t, :], cx.ones[:, 0:NE], eq[:, t, :], 0.0, ALU.mult, ALU.add)
            step(dve, ins)
            step(dve, dve.tensor_scalar(small[:, 1, :], small[:, 0, :], -1.0, float(TOP_K), ALU.mult, ALU.add))
            step(dve, dve.tensor_tensor(order[:, :, :], order[:, :, :], spread(small[:, 1, :], 2, NE), ALU.is_le))
            step(dve, dve.tensor_tensor(eq[:, :, :], eq[:, :, :], order[:, :, :], ALU.mult))
            dve.tensor_tensor(mask[:, :, :], gt[:, :, :], eq[:, :, :], ALU.add).then_inc(sem("mask_ready"), 1)
            dve.wait_ge(sem("mask_ready"), 1)
            step(dve, dve.tensor_tensor(gt[:, :, :], mask[:, :, :], s[:, :, :], ALU.mult))
            step(dve, dve.tensor_reduce(small[:, 2, :], gt[:, :, :], AX.X, ALU.add))
            step(dve, dve.reciprocal(small[:, 3, :], small[:, 2, :]))
            dve.scalar_tensor_tensor(out=vals[:, 2, :, :], in0=gt[:, :, :], scalar=ROUTE_SCALE,
                                     in1=spread(small[:, 3, :], 2, NE), op0=ALU.mult, op1=ALU.mult)
            for t in range(TILES):
                ins = dve.tensor_tensor_scan(order[:, t, :], cx.ones[:, 0:NE], mask[:, t, :], 0.0, ALU.mult, ALU.add)
            step(dve, ins)
            shared(0)
            dve.wait_ge(sem("rank_mm"), 1)
            dve.tensor_copy(pos[:, :, :].rearrange("p t e -> p (t e)"), ps[:, 7, 0:TILES * NE])
            step(dve, dve.tensor_copy(cnt[:, 0, :], ps[:, 7, TILES * NE:(TILES + 1) * NE]))
            step(dve, dve.tensor_scalar(cnt[:, 1, :], cnt[:, 0, :], 0.0, None, ALU.is_gt))
            for x in range(1, TILES):
                step(dve, dve.scalar_tensor_tensor(out=cnt[:, 1, :], in0=cnt[:, 0, :], scalar=float(x * P),
                                                   in1=cnt[:, 1, :], op0=ALU.is_gt, op1=ALU.add))
            step(dve, dve.tensor_tensor_scan(cnt[:, 2, :], cx.ones[:, 0:NE], cnt[:, 1, :], 0.0, ALU.mult, ALU.add))
            step(dve, dve.tensor_tensor(cnt[:, 3, :], cnt[:, 2, :], cnt[:, 1, :], ALU.subtract))
            step(dve, dve.tensor_scalar(pick[:, 0, 0, 0:MAX_TURNS], iota[:, 0:UNROLL * MAX_TURNS:UNROLL],
                                        cnt[:, 2, NE - 1:NE], None, ALU.is_lt))
            step(dve, dve.tensor_reduce(ids[:, 0:1], pick[:, 0, 0, 0:MAX_TURNS], AX.X, ALU.add))
            dve.tensor_copy(m.turns[:, :], ids[0:1, 0:1])
            step(dve, dve.tensor_scalar(pick[:, 1, 0, :], cnt[:, 2, :], col, None, ALU.is_le))
            step(dve, dve.tensor_reduce(ids[:, 0:1], pick[:, 1, 0, :], AX.X, ALU.add))
            dve.tensor_scalar(ids[:, 1:2], ids[:, 0:1], float(NE - 1), None, ALU.min).then_inc(sem("ids_ready"), 1)
            step(dve, dve.tensor_scalar(over[:, :, :], pos[:, :, :], float(P), None, ALU.is_ge))
            for x in range(2, TILES):
                step(dve, dve.scalar_tensor_tensor(out=over[:, :, :], in0=pos[:, :, :], scalar=float(x * P),
                                                   in1=over[:, :, :], op0=ALU.is_ge, op1=ALU.add))
            dve.scalar_tensor_tensor(out=vals[:, 0, :, :], in0=over[:, :, :], scalar=-float(P), in1=pos[:, :, :],
                                     op0=ALU.mult, op1=ALU.add)
            step(dve, dve.tensor_tensor(vals[:, 1, :, :], over[:, :, :], spread(cnt[:, 3, :], 1, TILES), ALU.add))
            for k in range(TOP_K):
                step(dve, dve.scalar_tensor_tensor(out=eq[:, :, :], in0=order[:, :, :], scalar=float(k + 1),
                                                   in1=mask[:, :, :], op0=ALU.is_equal, op1=ALU.mult))
                step(dve, dve.tensor_tensor(pick[:, :, :, :].rearrange("p v t e -> p v (t e)"),
                                            vals[:, :, :, :].rearrange("p v t e -> p v (t e)"),
                                            spread(eq[:, :, :].rearrange("p t e -> p (t e)"), 1, 3), ALU.mult))
                step(dve, dve.tensor_reduce(chosen[:, k, :, :], pick[:, :, :, :], AX.X, ALU.add))
            for k in range(TOP_K):
                dve.scalar_tensor_tensor(out=m.slot_of[:, k, :], in0=chosen[:, k, 1, :], scalar=float(P),
                                         in1=chosen[:, k, 0, :], op0=ALU.mult, op1=ALU.add)
                dve.tensor_copy(m.gates[:, k, :], chosen[:, k, 2, :])
                for t in range(TILES):
                    n = k * TILES + t
                    dve.tensor_scalar(place[:, n, :], row, chosen[:, k, 0, t:t + 1], None, ALU.is_equal)
                    ins = dve.tensor_scalar(where[:, n, :], iota[:, 0:TABLE], chosen[:, k, 1, t:t + 1],
                                            token[:, t:t + 1], ALU.is_equal, ALU.mult)
            ins.then_inc(sem("place_ready"), 1)
            dve.wait_ge(sem("ids_turned"), 1)
            dve.tensor_copy(m.expert_of[:, :], ps[0:1, 4, 0:P])
            shared(1)
            dve.wait_ge(sem("table_mm"), 1)
            dve.tensor_copy(m.table[:, :], ps[:, 3, 0:TABLE])


def stage_experts(nc, cx, L, m):
    w = cx.w
    sem = cx.sem
    ps = cx.ps
    with ExitStack() as st:
        def sb(name, shape, dt=F32):
            return st.enter_context(nc.sbuf_tensor(name, shape, dt))
        xg = sb("ex_xg", [P, 2, D])
        xT = sb("ex_xT", [P, 2, KT, P])
        silu = sb("ex_silu", [P, 2, P])
        hid = sb("ex_hid", [P, 2, P])
        y = sb("ex_y", [P, 2, D])
        index = sb("ex_index", [P, 2], mybir.dt.uint32)
        block = st.enter_context(nc.Block())

        def turns(eng):
            return eng.value_load(m.turns[0:1, 0:1], min_val=MIN_TURNS, max_val=MAX_TURNS)

        def at(n, i):
            return i * UNROLL + n

        def load(sp, n, i):
            s = tile_slot(n)
            e = sp.value_load(m.expert_of[0:1, bass.ds(at(n, i), 1)] if n else m.expert_of[0:1, 0:1], min_val=0,
                              max_val=NE - 1)
            le = sp.snap(L * NE + e)
            for x, name in enumerate(("w_e_gate", "w_e_up")):
                sp.dma_start(cx.ring[:, s, x * D:(x + 1) * D],
                             w[name].rearrange("l e (p k) f -> (l e) p (k f)", k=KT)[bass.ds(le, 1)].rearrange(
                                 "o p n -> (o p) n")).then_inc(sem(f"tile_full{s}"), 16)
            sp.dma_start(cx.ring[:, s, 2 * D:3 * D],
                         w["w_e_down"].rearrange("l e f d -> (l e) f d")[bass.ds(le, 1)].rearrange(
                             "o p n -> (o p) n")).then_inc(sem(f"tile_full{s}"), 16)

        @block.sync
        def _(sp):
            load(sp, 0, 0)
            count = turns(sp)
            with sp.Fori(0, count) as i:
                for n in range(1, UNROLL + 1):
                    sp.wait_ge(sem("tile_free"), at(n + 1, i))
                    load(sp, n, i)

        @block.gpsimd
        def _(pool):
            def gather(n, i=0):
                b = n % 2
                if n >= 2:
                    pool.wait_ge(sem("x_turned"), at(n - 1, i))
                pool.tensor_copy(index[:, b:b + 1], m.table[:, bass.ds(at(n, i), 1)] if n >= 2 else m.table[:, n:n + 1]).then_inc(
                    sem("index_ready"), 1)
                pool.wait_ge(sem("index_ready"), at(n + 1, i))
                pool.sem_inc(sem("pool_go"), 1)
                pool.indirect_dma_start(xg[:, b, :], None, cx.h_rows,
                                        bass.IndirectOffsetOnAxis(ap=index[:, b:b + 1], axis=0)).then_inc(
                    sem(f"xg_ready{b}"), 16)

            gather(0)
            gather(1)
            count = turns(pool)
            with pool.Fori(0, count) as i:
                for n in range(2, UNROLL + 2):
                    gather(n, i)
            pool.wait_ge(sem("xg_ready1"), count * (16 * UNROLL // 2) + 16)
            pool.wait_ge(sem("xg_ready0"), count * (16 * UNROLL // 2) + 16)
            pool.sem_inc(sem("pool_go"), 1)

        @block.tensor
        def _(pe):
            def turn(n, i=0):
                b = n % 2
                pe.wait_ge(sem(f"xg_ready{b}"), i * (16 * UNROLL // 2) + 16 * (n // 2 + 1))
                if n:
                    pe.wait_ge(sem("xT_low"), at(n, i))
                    pe.wait_ge(sem("xT_high"), at(n, i))
                for k in range(KT):
                    ins = pe.transpose(ps[:, k // 4, (k % 4) * P:(k % 4 + 1) * P], xg[:, b, k * P:(k + 1) * P],
                                       cx.ident)
                ins.then_inc(sem("x_turned"), 1)

            def up(n, i=0):
                s = tile_slot(n)
                b = n % 2
                pe.wait_ge(sem(f"tile_full{s}"), i * 48 + 48 * (n // SLOTS + 1))
                pe.wait_ge(sem("xT_low"), at(n + 1, i))
                pe.wait_ge(sem("xT_high"), at(n + 1, i))
                for g in range(2):
                    wide = cx.ring[:, s, g * D:(g + 1) * D].rearrange("p (k f) -> p k f", k=KT)
                    for k in range(KT):
                        ins = pe.matmul(ps[:, 2 + b, g * P:(g + 1) * P], wide[:, k, :], xT[:, b, k, :],
                                        start=(k == 0), stop=(k == KT - 1))
                ins.then_inc(sem("tile_up"), 1)

            def down(n, i=0):
                s = tile_slot(n)
                b = n % 2
                pe.wait_ge(sem("tile_hid"), at(n + 1, i))
                if n >= 2:
                    pe.wait_ge(sem("y_low"), at(n - 1, i))
                    pe.wait_ge(sem("y_high"), at(n - 1, i))
                else:
                    pe.wait_ge(sem("y_low"), at(n - 1 + 2, i))
                    pe.wait_ge(sem("y_high"), at(n - 1 + 2, i))
                for x in range(2):
                    ins = pe.matmul(ps[:, 4 + 2 * b + x, :], hid[:, b, :],
                                    cx.ring[:, s, 2 * D + x * SEC:2 * D + (x + 1) * SEC], start=True, stop=True)
                ins.then_inc(sem("tile_down"), 1)
                pe.wait_ge(sem("tile_down"), at(n + 1, i))
                pe.sem_inc(sem("tile_free"), 1)

            pe.sem_inc(sem("tile_free"), SLOTS)
            turn(0)
            up(0)
            count = turns(pe)
            with pe.Fori(0, count) as i:
                for n in range(1, UNROLL + 1):
                    turn(n, i)
                    down(n - 1, i)
                    up(n, i)

        @block.scalar
        def _(act):
            def turned(n, i=0):
                act.wait_ge(sem("x_turned"), at(n + 1, i))
                if n >= 2:
                    act.wait_ge(sem("tile_up"), at(n - 1, i))
                act.activation(xT[:, n % 2, 0:4, :].rearrange("p k s -> p (k s)"), ps[:, 0, :], ACT.Copy).then_inc(
                    sem("xT_low"), 1)

            def silu_up(n, i=0):
                b = n % 2
                act.wait_ge(sem("tile_up"), at(n + 1, i))
                act.activation(silu[:, b, :], ps[:, 2 + b, 0:P], ACT.Silu).then_inc(sem("tile_silu"), 1)

            turned(0)
            silu_up(0)
            count = turns(act)
            with act.Fori(0, count) as i:
                for n in range(1, UNROLL + 1):
                    turned(n, i)
                    b = (n - 1) % 2
                    act.wait_ge(sem("tile_down"), at(n, i))
                    act.wait_ge(sem(f"y_stored{b}"), i * (16 * UNROLL // 2) + 16 * ((n - 1) // 2 + 1))
                    act.activation(y[:, b, 0:SEC], ps[:, 4 + 2 * b, :], ACT.Copy).then_inc(sem("y_low"), 1)
                    silu_up(n, i)
                    act.wait_ge(sem("y_low"), at(n + 2, i))
                    act.wait_ge(sem("y_high"), at(n + 2, i))
                    act.dma_start(cx.y_rows[bass.ds(at(n - 1, i), 1)].rearrange("o p d -> (o p) d"),
                                  y[:, b, :]).then_inc(sem(f"y_stored{b}"), 16)
            for b in range(2):
                act.wait_ge(sem(f"y_stored{b}"), count * (16 * UNROLL // 2) + 16)
            act.sem_inc(sem("act_go"), 1)

        @block.vector
        def _(dve):
            def turned(n, i=0):
                dve.wait_ge(sem("x_turned"), at(n + 1, i))
                if n >= 2:
                    dve.wait_ge(sem("tile_up"), at(n - 1, i))
                dve.tensor_copy(xT[:, n % 2, 4:8, :].rearrange("p k s -> p (k s)"), ps[:, 1, :]).then_inc(
                    sem("xT_high"), 1)

            def hidden(n, i=0):
                b = n % 2
                dve.wait_ge(sem("tile_silu"), at(n + 1, i))
                dve.tensor_tensor(hid[:, b, :], ps[:, 2 + b, P:2 * P], silu[:, b, :], ALU.mult).then_inc(
                    sem("tile_hid"), 1)

            dve.sem_inc(sem("y_low"), 2)
            dve.sem_inc(sem("y_high"), 2)
            for b in range(2):
                dve.sem_inc(sem(f"y_stored{b}"), 16)
            turned(0)
            hidden(0)
            count = turns(dve)
            with dve.Fori(0, count) as i:
                for n in range(1, UNROLL + 1):
                    turned(n, i)
                    b = (n - 1) % 2
                    dve.wait_ge(sem("tile_down"), at(n, i))
                    dve.wait_ge(sem(f"y_stored{b}"), i * (16 * UNROLL // 2) + 16 * ((n - 1) // 2 + 1))
                    dve.tensor_copy(y[:, b, SEC:D], ps[:, 5 + 2 * b, :]).then_inc(sem("y_high"), 1)
                    hidden(n, i)


def stage_combine(nc, cx, L, m, x):
    sem = cx.sem
    ps = cx.ps
    BUFS = 8
    with ExitStack() as st:
        def sb(name, shape):
            return st.enter_context(nc.sbuf_tensor(name, shape, F32))
        yg = sb("co_yg", [P, BUFS, D])
        junk = cx.mixT[:, :, :].rearrange("p a b -> p (a b)").rearrange(
            "p (t d) -> p t d", d=D)
        fs = sb("co_fs", [P, 3, TILES])
        acc = cx.hT[:, :, :].rearrange("p a b -> p (a b)").rearrange("p (t d) -> p t d", d=D)
        block = st.enter_context(nc.Block())

        @block.gpsimd
        def _(pool):
            for n in range(N_CHOICE):
                t, k = n // TOP_K, n % TOP_K
                if n >= BUFS:
                    pool.wait_ge(sem("yg_used"), n - BUFS + 1)
                pool.indirect_dma_start(yg[:, n % BUFS, :], None, cx.y_rows.rearrange("n p d -> (n p) d"),
                                        bass.IndirectOffsetOnAxis(ap=m.slot_of[:, k, t:t + 1], axis=0)).then_inc(
                    sem(f"yg_ready{n % BUFS}"), 16)
            for b in range(BUFS):
                pool.wait_ge(sem(f"yg_ready{b}"), 16 * len(range(b, N_CHOICE, BUFS)))

        @block.tensor
        def _(pe):
            for t in range(TILES):
                if t >= 4:
                    pe.wait_ge(sem("co_first"), t - 3)
                for h in range(2):
                    for c in range(2):
                        ins = pe.matmul(ps[:, 2 * (t % 4) + h, :], m.hsh[:, c, tok(t)],
                                        m.wsd[:, c, h * SEC:(h + 1) * SEC], start=(c == 0), stop=(c == 1))
                ins.then_inc(sem("co_mm"), 1)

        @block.scalar
        def _(act):
            for t in range(TILES):
                act.wait_ge(sem("co_done"), t + 1)
                act.activation(junk[:, t, :], acc[:, t, :], ACT.Square, accum_out=fs[:, 0, t:t + 1]).then_inc(
                    sem("co_sq"), 1)
                act.wait_ge(sem("co_sq"), t + 1)
                act.activation(fs[:, 1, t:t + 1], fs[:, 0, t:t + 1], ACT.Sqrt, scale=1.0 / D,
                               bias=cx.eps[:, :]).then_inc(sem("co_rms"), 1)

        @block.sync
        def _(sp):
            for t in range(TILES):
                sp.wait_ge(sem("x2_ready"), t + 1)
                dst = cx.y_prompt[0] if t == 0 else cx.y_sample[0, tok(t - 1), :]
                sp.dma_start(dst, x[:, t, :]).then_inc(sem("x_stored"), 16)
            sp.wait_ge(sem("x_stored"), 16 * TILES)

        @block.vector
        def _(dve):
            step = cx.vlink

            def finish(t):
                dve.wait_ge(sem("co_rms"), t + 1)
                step(dve, dve.reciprocal(fs[:, 2, t:t + 1], fs[:, 1, t:t + 1]))
                step(dve, dve.scalar_tensor_tensor(out=acc[:, t, :], in0=acc[:, t, :], scalar=fs[:, 2, t:t + 1],
                                                   in1=cx.gate_post[:, 1, min(t, 1), :], op0=ALU.mult, op1=ALU.mult))
                dve.tensor_tensor(x[:, t, :], x[:, t, :], acc[:, t, :], ALU.add).then_inc(sem("x2_ready"), 1)

            for t in range(TILES):
                a = acc[:, t, :]
                for k in range(TOP_K):
                    n = t * TOP_K + k
                    dve.wait_ge(sem(f"yg_ready{n % BUFS}"), 16 * (n // BUFS + 1))
                    if k == 0:
                        dve.wait_ge(sem("co_mm"), t + 1)
                        dve.scalar_tensor_tensor(out=a.rearrange("p (h n) -> p h n", h=2),
                                                 in0=yg[:, n % BUFS, :].rearrange("p (h n) -> p h n", h=2),
                                                 scalar=m.gates[:, k, t:t + 1],
                                                 in1=ps[:, 2 * (t % 4):2 * (t % 4) + 2, :],
                                                 op0=ALU.mult, op1=ALU.add).then_inc(sem("co_first"), 1)
                        dve.wait_ge(sem("co_first"), t + 1)
                        dve.sem_inc(sem("yg_used"), 1)
                    else:
                        ins = dve.scalar_tensor_tensor(out=a, in0=yg[:, n % BUFS, :], scalar=m.gates[:, k, t:t + 1],
                                                       in1=a, op0=ALU.mult, op1=ALU.add)
                        ins.then_inc(sem("yg_used"), 1)
                        dve.wait_ge(sem("yg_used"), n + 1)
                dve.sem_inc(sem("co_done"), 1)
                if t:
                    finish(t - 1)
            finish(TILES - 1)



def trunk(nc, w, outs):
    cx = Cx()
    cx.w = w
    (cx.y_prompt, cx.y_sample, cx.new_da_k, cx.new_da_v, cx.new_na_k, cx.new_na_v, cx.new_ssm_f,
     cx.new_ssm_b) = outs
    cx.v_scratch = nc.dram_tensor("v_scratch", [LAT, 512], F32, kind="Internal").ap()
    cx.h_rows = nc.dram_tensor("h_rows", [TOK, D], F32, kind="Internal").ap()
    cx.y_rows = nc.dram_tensor("y_rows", [UNROLL * MAX_TURNS, P, D], F32, kind="Internal").ap()
    cx.rpb_scratch = nc.dram_tensor("rpb_scratch", [DEPTH * NA_H, RPB_ROW], F32, kind="Internal").ap()
    with ExitStack() as st:
        def sb(name, shape):
            return st.enter_context(nc.sbuf_tensor(name, shape, F32))
        base = sb("base", [P, 7 * P])
        sel = sb("sel", [2, 2, P])
        cx.eps = sb("eps", [P, 1])
        cx.ring = sb("ring", [P, SLOTS, 4096])
        cx.hT = sb("hT", [P, KT, TOK])
        cx.gate_post = sb("gate_post", [P, 2, 2, D])
        cx.mod_scale = sb("mod_scale", [P, 2, KT, 2])
        cx.mod_shift = sb("mod_shift", [P, 2, KT, 2])
        cx.ssq = sb("ssq", [P, 2, TILES])
        cx.rms = sb("rms", [P, 2, TILES])
        cx.rstd = sb("rstd", [P, 2, TILES])
        cx.ps = st.enter_context(nc.psum_tensor("ps", [P, 8, 512], F32))
        cx.ident, cx.rot, cx.le, cx.gt, cx.ge, cx.lt, cx.ones = (base[:, n * P:(n + 1) * P] for n in range(7))
        cx.sel = sel
        sems, half_sems = {}, {}

        def sem(name):
            if name not in sems:
                if name not in half_sems:
                    half_sems[name] = cx.half.enter_context(nc.semaphore(name))
                return half_sems[name]
            return sems[name]

        for name in ([f"ring_full{s}" for s in range(SLOTS)] + [
                "ring_free", "squares_ready", "rms_ready", "xn_ready", "xnT_ready", "mods_ready", "h_lat_ready",
                "h_ctx_ready", "vector_step"]):
            sems[name] = st.enter_context(nc.semaphore(name))

        def clear_half():
            for s in half_sems.values():
                nc.sync.sem_clear(s)
            half_sems.clear()
            nc.all_engine_barrier()
            cx.half.close()

        cx.sem = sem
        cx.ring_full = [sem(f"ring_full{s}") for s in range(SLOTS)]
        cx.ring_free, cx.squares_ready, cx.rms_ready = sem("ring_free"), sem("squares_ready"), sem("rms_ready")
        cx.xn_ready, cx.xnT_ready, cx.mods_ready = sem("xn_ready"), sem("xnT_ready"), sem("mods_ready")
        cx.h_lat_ready, cx.h_ctx_ready = sem("h_lat_ready"), sem("h_ctx_ready")
        setup = st.enter_context(nc.semaphore("setup"))
        setup_x = st.enter_context(nc.semaphore("setup_x"))
        setup_mem = st.enter_context(nc.semaphore("setup_mem"))
        with ExitStack() as once:
            pad = once.enter_context(nc.sbuf_tensor("rpb_pad", [DEPTH * NA_H, RPB_ROW], F32))
            block = once.enter_context(nc.Block())

            @block.sync
            def _(sp):
                sp.dma_start(base[:, :], w["k_base"]).then_inc(setup, 16)
                sp.dma_start(sel[:, :, :], w["k_sel"]).then_inc(setup, 16)
                sp.dma_start(cx.y_prompt[0], w["x_prompt"][0]).then_inc(setup, 16)
                sp.dma_start(cx.y_sample[0], w["x_sample"][0]).then_inc(setup, 16)
                sp.wait_ge(setup_mem, 2)
                sp.dma_start(pad[:, RPB_FRONT:RPB_FRONT + RPB_R * WCOLS].rearrange("p (r c) -> p r c", c=WCOLS)[
                    :, :, 0:RPB_C], w["na_rpb"].rearrange("l h r c -> (l h) r c")).then_inc(setup_x, 16)
                sp.wait_ge(setup_x, 16)
                sp.dma_start(cx.rpb_scratch, pad[:, :]).then_inc(setup_x, 16)
                sp.wait_ge(setup_x, 32)
                sp.wait_ge(setup, 64)

            @block.vector
            def _(dve):
                dve.memset(pad[:, :], 0.0).then_inc(setup_mem, 1)
                dve.memset(cx.eps[:, :], EPS).then_inc(setup_mem, 1)

        with nc.Fori(0, DEPTH) as L:
            cx.vlink = Link(sem("vector_step"))
            cx.half = ExitStack()
            stage_ada(nc, cx, L)
            with ExitStack() as mid:
                cx.oT = mid.enter_context(nc.sbuf_tensor("oT", [P, 4, TOK], F32))
                stage_ssm(nc, cx, L)
                cx.mixT = mid.enter_context(nc.sbuf_tensor("mixT", [P, KT, TOK], F32))
                stage_mix(nc, cx, L, 0, "s", 2)
                stage_da(nc, cx, L)
                stage_mix(nc, cx, L, 1, "a", 0)
                stage_na(nc, cx, L)
                stage_mix(nc, cx, L, 2, "n", 4)
                x = mid.enter_context(nc.sbuf_tensor("x", [P, TILES, D], F32))
                stage_out(nc, cx, L, x)
                clear_half()
                cx.half = ExitStack()
                m = Cx()
                m.hsh = mid.enter_context(nc.sbuf_tensor("shared_hidden", [P, 2, TOK], F32))
                m.wsd = mid.enter_context(nc.sbuf_tensor("shared_down", [P, 2, D], F32))
                m.gates = mid.enter_context(nc.sbuf_tensor("choice_gates", [P, TOP_K, TILES], F32))
                m.slot_of = mid.enter_context(nc.sbuf_tensor("choice_slots", [P, TOP_K, TILES], mybir.dt.uint32))
                m.table = mid.enter_context(nc.sbuf_tensor("token_of_slot", [P, TABLE], mybir.dt.uint32))
                m.expert_of = mid.enter_context(nc.sbuf_tensor("expert_of_tile", [1, P], mybir.dt.int32))
                m.turns = mid.enter_context(nc.sbuf_tensor("turns", [1, 1], mybir.dt.int32))
                stage_route(nc, cx, L, m)
                stage_experts(nc, cx, L, m)
                stage_combine(nc, cx, L, m, x)
            nc.gpsimd.dma_reset()
            for s in sems.values():
                nc.sync.sem_clear(s)
            clear_half()


_INS = ["x_prompt", "x_sample", "c", "cache_da_k", "cache_da_v", "cache_na_k", "cache_na_v", "state_ssm_f",
        "state_ssm_b", "c_ctx", "w_ada", "b_ada", "g_pre1", "g_post1", "g_pre2", "g_post2", "w_in", "w_gate",
        "da_lambda", "da_subln", "ssm_conv_w", "ssm_conv_b", "ssm_dt_bias", "ssm_a_log", "ssm_d", "ssm_norm",
        "na_rpb", "w_br_da", "w_br_ssm", "w_br_na", "w_out", "w_router", "b_router", "w_e_gate", "w_e_up",
        "w_e_down", "w_s_gate", "w_s_up", "w_s_down"]
_OUTS = [(1, 128, 1024), (1, 512, 1024), (1, 2, 4, 128, 2, 64), (1, 2, 4, 128, 128), (1, 2, 8, 128, 64),
         (1, 2, 8, 128, 64), (1, 2, 8, 64, 128), (1, 2, 8, 64, 128)]


def kernel(**inputs):
    import concourse.bacc as _bacc
    from concourse.bass_utils import run_bass_kernel_spmd as _run

    nc = _bacc.Bacc("TRN2", target_bir_lowering=False, num_devices=1)
    arrays, w = {}, {}
    given = {name: np.ascontiguousarray(inputs[name]) for name in _INS}
    given.update({name: np.ascontiguousarray(a) for name, a in shape_constants().items()})
    for name, a in given.items():
        arrays[f"in_{name}"] = a
        w[name] = nc.dram_tensor(f"in_{name}", a.shape, mybir.dt.from_np(a.dtype), kind="ExternalInput").ap()
    outs = [nc.dram_tensor(f"out_{i}", shape, F32, kind="ExternalOutput").ap() for i, shape in enumerate(_OUTS)]
    trunk(nc, w, outs)
    r = _run(nc, [arrays], core_ids=[0])
    return tuple(r.results[0][f"out_{i}"] for i in range(len(_OUTS)))
```
